# Optimizing a Trainium2 kernel written in Bass

```python
import math
import jax, jax.numpy as jnp
from jax import lax
import numpy as np

D_MODEL = 1024
BATCH = 1
SEQ = 2048
DEPTH = 1
DEC_BATCH = 8
DEC_SEQ = 16
PAST_LEN = 128

CHUNK = 64
Q_BLOCK = 128
RMS_EPS = 1e-6
ATTN_WIDTH = D_MODEL // 2
A_HEAD_DIM = 64
A_HEADS = ATTN_WIDTH // (2 * A_HEAD_DIM)
QK_A = A_HEADS * 2 * A_HEAD_DIM
REC_WIDTH = D_MODEL - ATTN_WIDTH
R_HEADS = 4
R_DV = REC_WIDTH // R_HEADS
R_DK = 128
FK_R = R_HEADS * R_DK
SPLITS = list(np.cumsum([QK_A, QK_A, ATTN_WIDTH, FK_R, FK_R, REC_WIDTH])[:].tolist())
IN_COLS = 2 * QK_A + ATTN_WIDTH + 2 * FK_R + 2 * REC_WIDTH
MIX_WIDTH = ATTN_WIDTH + REC_WIDTH
N_GROUPS = 4
EXPERTS_PER_GROUP = 8
N_EXPERTS = N_GROUPS * EXPERTS_PER_GROUP
TOP_K = 2
D_EXPERT = 512
ROW_BLOCK = 128

kernel_name = "hymba_diffattn_hgrn2_hmoe_stream"

F32 = jnp.float32

def rmsnorm(x, w):
    xf = x.astype(F32)
    y = xf * lax.rsqrt(jnp.mean(xf * xf, axis=-1, keepdims=True) + RMS_EPS)
    return (y * w.astype(F32)).astype(x.dtype)

def split_proj(h, w_in, lb):
    B, L, _ = h.shape
    z = h @ w_in
    qa, ka, va, qr, fr, ir, gr = jnp.split(z, SPLITS, axis=-1)
    qa = qa.reshape(B, L, A_HEADS, 2, A_HEAD_DIM)
    ka = ka.reshape(B, L, A_HEADS, 2, A_HEAD_DIM)
    va = va.reshape(B, L, A_HEADS, 2 * A_HEAD_DIM)
    qr = jax.nn.silu(qr.astype(F32)).reshape(B, L, R_HEADS, R_DK)
    f = lb + (1.0 - lb) * jax.nn.sigmoid(fr.astype(F32).reshape(B, L, R_HEADS, R_DK))
    logf = jnp.log(f)
    kr = 1.0 - f
    ir = ir.astype(F32).reshape(B, L, R_HEADS, R_DV)
    gr = gr.reshape(B, L, R_HEADS, R_DV)
    return qa, ka, va, qr, kr, logf, ir, gr

def diff_attention(q, k, v, q_pos, k_pos, lam):
    s = jnp.einsum('bqhcd,bkhcd->bhcqk', q.astype(F32), k.astype(F32)) * (A_HEAD_DIM ** -0.5)
    visible = (k_pos[None, :] // CHUNK) <= (q_pos[:, None] // CHUNK)
    s = jnp.where(visible, s, -jnp.inf)
    p = jax.nn.softmax(s, axis=-1)
    w = p[:, :, 0] - lam * p[:, :, 1]
    return jnp.einsum('bhqk,bkhe->bqhe', w, v.astype(F32))

def attn_prompt(qa, ka, va, lam):
    B, S = qa.shape[:2]
    nqb = S // Q_BLOCK
    qb = qa.reshape(B, nqb, Q_BLOCK, A_HEADS, 2, A_HEAD_DIM).swapaxes(0, 1)
    k_pos = jnp.arange(S)

    def one(args):
        q_blk, bi = args
        q_pos = bi * Q_BLOCK + jnp.arange(Q_BLOCK)
        return diff_attention(q_blk, ka, va, q_pos, k_pos, lam)

    o = lax.map(one, (qb, jnp.arange(nqb)))
    return o.swapaxes(0, 1).reshape(B, S, A_HEADS, 2 * A_HEAD_DIM)

def hgrn_block(q, k, v, logf, S0):
    L = q.shape[1]
    b = jnp.cumsum(logf, axis=1)
    causal = jnp.tril(jnp.ones((L, L), dtype=bool))
    diff = b[:, :, None] - b[:, None, :]
    decay = jnp.exp(jnp.where(causal[None, :, :, None, None], diff, -jnp.inf))
    A = jnp.einsum('bthk,btshk,bshk->bhts', q, decay, k)
    o = jnp.einsum('bhts,bshv->bthv', A, v) + jnp.einsum('bthk,bhkv->bthv', q * jnp.exp(b), S0)
    bL = b[:, -1]
    S_new = jnp.exp(bL)[..., None] * S0 + jnp.einsum('bshk,bshv->bhkv', k * jnp.exp(bL[:, None] - b), v)
    return o, S_new

def hgrn_prompt(q, k, v, logf):
    B, L = q.shape[:2]
    nc = L // CHUNK

    def to_chunks(a):
        return a.reshape(B, nc, CHUNK, *a.shape[2:]).swapaxes(0, 1)

    def step(S, inp):
        qc, kc, vc, lc = inp
        o, S = hgrn_block(qc, kc, vc, lc, S)
        return S, o

    S0 = jnp.zeros((B, R_HEADS, R_DK, R_DV), F32)
    S, o = lax.scan(step, S0, (to_chunks(q), to_chunks(k), to_chunks(v), to_chunks(logf)))
    return o.swapaxes(0, 1).reshape(B, L, R_HEADS, R_DV), S

def merge_groups(oa, orec, gr, subln_w, gnorm_w, w_out, lam_init, dtype):
    B, L = oa.shape[:2]
    a = (rmsnorm(oa, subln_w) * (1.0 - lam_init)).reshape(B, L, ATTN_WIDTH).astype(dtype)
    r = (rmsnorm(orec, gnorm_w) * jax.nn.silu(gr.astype(F32))).reshape(B, L, REC_WIDTH).astype(dtype)
    return jnp.concatenate([a, r], axis=-1) @ w_out

def grouped_experts(t, experts, gates, wg, wu, wd):
    N, K = experts.shape
    M = N * K
    flat_e = experts.reshape(-1)
    flat_tok = jnp.repeat(jnp.arange(N, dtype=jnp.int32), K)
    flat_g = gates.reshape(-1)
    order = jnp.argsort(flat_e)
    se = flat_e[order]
    counts = jnp.bincount(flat_e, length=N_EXPERTS)
    starts = jnp.cumsum(counts) - counts
    pcounts = (counts + ROW_BLOCK - 1) // ROW_BLOCK * ROW_BLOCK
    pends = jnp.cumsum(pcounts)
    pstarts = pends - pcounts
    dest = pstarts[se] + jnp.arange(M) - starts[se]
    n_blocks = -(-M // ROW_BLOCK) + N_EXPERTS
    R = n_blocks * ROW_BLOCK
    row_tok = jnp.full((R,), N, jnp.int32).at[dest].set(flat_tok[order])
    row_gate = jnp.zeros((R,), flat_g.dtype).at[dest].set(flat_g[order])
    blk_exp = jnp.minimum(jnp.searchsorted(pends, jnp.arange(n_blocks) * ROW_BLOCK, side='right'), N_EXPERTS - 1)
    t_pad = jnp.concatenate([t, jnp.zeros((1, t.shape[1]), t.dtype)], axis=0)
    xs = t_pad[row_tok].reshape(n_blocks, ROW_BLOCK, t.shape[1])

    def run(args):
        xb, e = args
        return (jax.nn.silu(xb @ wg[e]) * (xb @ wu[e])) @ wd[e]

    ys = lax.map(run, (xs, blk_exp)).reshape(R, t.shape[1])
    ys = ys * row_gate[:, None].astype(ys.dtype)
    return jax.ops.segment_sum(ys, row_tok, num_segments=N + 1)[:N]

def hier_moe(h, w_group, w_router, wg, wu, wd):
    shp = h.shape
    t = h.reshape(-1, shp[-1])
    N = t.shape[0]
    g_logits = (t @ w_group).astype(F32)
    g_prob = jax.nn.softmax(g_logits, axis=-1)
    g_sel = jnp.argmax(g_logits, axis=-1)
    p_group = jnp.take_along_axis(g_prob, g_sel[:, None], axis=-1)
    e_logits = (t @ w_router).astype(F32).reshape(N, N_GROUPS, EXPERTS_PER_GROUP)
    e_logits = jnp.take_along_axis(e_logits, g_sel[:, None, None], axis=1)[:, 0]
    top_v, top_i = lax.top_k(e_logits, TOP_K)
    gates = p_group * jax.nn.softmax(top_v, axis=-1)
    experts = (g_sel[:, None] * EXPERTS_PER_GROUP + top_i).astype(jnp.int32)
    return grouped_experts(t, experts, gates, wg, wu, wd).reshape(shp)

def setup_inputs(seed: int = 0) -> dict:
    key = jax.random.key(seed)
    ks = jax.random.split(key, 24)
    nrm = lambda k, s, sc: jax.random.normal(k, s, F32) * sc
    gain = lambda k, s: 1.0 + 0.02 * jax.random.normal(k, s, F32)
    return {
        "x_prompt": nrm(ks[0], (BATCH, SEQ, D_MODEL), 1.0),
        "x_sample": nrm(ks[1], (DEC_BATCH, DEC_SEQ, D_MODEL), 1.0),
        "cache_k": nrm(ks[2], (DEPTH, DEC_BATCH, PAST_LEN, A_HEADS, 2 * A_HEAD_DIM), 1.0),
        "cache_v": nrm(ks[3], (DEPTH, DEC_BATCH, PAST_LEN, A_HEADS, 2 * A_HEAD_DIM), 1.0),
        "state_rec": nrm(ks[4], (DEPTH, DEC_BATCH, R_HEADS, R_DK, R_DV), 0.5),
        "w_in": nrm(ks[5], (DEPTH, D_MODEL, IN_COLS), D_MODEL ** -0.5),
        "lam_q1": nrm(ks[6], (DEPTH, A_HEAD_DIM), 0.1),
        "lam_k1": nrm(ks[7], (DEPTH, A_HEAD_DIM), 0.1),
        "lam_q2": nrm(ks[8], (DEPTH, A_HEAD_DIM), 0.1),
        "lam_k2": nrm(ks[9], (DEPTH, A_HEAD_DIM), 0.1),
        "subln_w": gain(ks[10], (DEPTH, 2 * A_HEAD_DIM)),
        "lb_param": nrm(ks[11], (DEPTH + 1, FK_R), 0.5),
        "gnorm_w": gain(ks[12], (DEPTH, R_DV)),
        "w_out": nrm(ks[13], (DEPTH, MIX_WIDTH, D_MODEL), MIX_WIDTH ** -0.5),
        "norm1_w": gain(ks[14], (DEPTH, D_MODEL)),
        "norm2_w": gain(ks[15], (DEPTH, D_MODEL)),
        "w_group": nrm(ks[16], (DEPTH, D_MODEL, N_GROUPS), D_MODEL ** -0.5),
        "w_router": nrm(ks[17], (DEPTH, D_MODEL, N_EXPERTS), D_MODEL ** -0.5),
        "w_e_gate": nrm(ks[18], (DEPTH, N_EXPERTS, D_MODEL, D_EXPERT), D_MODEL ** -0.5),
        "w_e_up": nrm(ks[19], (DEPTH, N_EXPERTS, D_MODEL, D_EXPERT), D_MODEL ** -0.5),
        "w_e_down": nrm(ks[20], (DEPTH, N_EXPERTS, D_EXPERT, D_MODEL), D_EXPERT ** -0.5),
        "final_w": gain(ks[21], (D_MODEL,)),
    }

def reference(x_prompt, x_sample, cache_k, cache_v, state_rec, w_in, lam_q1, lam_k1, lam_q2, lam_k2,
              subln_w, lb_param, gnorm_w, w_out, norm1_w, norm2_w, w_group, w_router,
              w_e_gate, w_e_up, w_e_down, final_w):
    lbs = jnp.cumsum(jax.nn.softmax(lb_param.astype(F32), axis=0), axis=0)
    yp, ys = x_prompt, x_sample
    Bp, S = x_prompt.shape[:2]
    Bs, T = x_sample.shape[:2]
    kp_l, vp_l, sp_l, ks_l, vs_l, ss_l = [], [], [], [], [], []
    for l in range(DEPTH):
        lam_init = 0.8 - 0.6 * math.exp(-0.3 * l)
        lam = (jnp.exp(jnp.sum(lam_q1[l].astype(F32) * lam_k1[l].astype(F32)))
               - jnp.exp(jnp.sum(lam_q2[l].astype(F32) * lam_k2[l].astype(F32))) + lam_init)
        lb = lbs[l].reshape(R_HEADS, R_DK)

        h = rmsnorm(yp, norm1_w[l])
        qa, ka, va, qr, kr, logf, ir, gr = split_proj(h, w_in[l], lb)
        oa = attn_prompt(qa, ka, va, lam)
        orec, s_p = hgrn_prompt(qr, kr, ir, logf)
        yp = yp + merge_groups(oa, orec, gr, subln_w[l], gnorm_w[l], w_out[l], lam_init, yp.dtype)
        yp = yp + hier_moe(rmsnorm(yp, norm2_w[l]), w_group[l], w_router[l], w_e_gate[l], w_e_up[l], w_e_down[l])
        kp_l.append(ka.reshape(Bp, S, A_HEADS, 2 * A_HEAD_DIM))
        vp_l.append(va)
        sp_l.append(s_p)

        h = rmsnorm(ys, norm1_w[l])
        qa, ka, va, qr, kr, logf, ir, gr = split_proj(h, w_in[l], lb)
        k_all = jnp.concatenate([cache_k[l].astype(ka.dtype).reshape(Bs, -1, A_HEADS, 2, A_HEAD_DIM), ka], axis=1)
        v_all = jnp.concatenate([cache_v[l].astype(va.dtype), va], axis=1)
        P = cache_k.shape[2]
        oa = diff_attention(qa, k_all, v_all, P + jnp.arange(T), jnp.arange(P + T), lam)
        orec, s_s = hgrn_block(qr, kr, ir, logf, state_rec[l].astype(F32))
        ys = ys + merge_groups(oa, orec, gr, subln_w[l], gnorm_w[l], w_out[l], lam_init, ys.dtype)
        ys = ys + hier_moe(rmsnorm(ys, norm2_w[l]), w_group[l], w_router[l], w_e_gate[l], w_e_up[l], w_e_down[l])
        ks_l.append(ka.reshape(Bs, T, A_HEADS, 2 * A_HEAD_DIM))
        vs_l.append(va)
        ss_l.append(s_s)

    y_prompt = rmsnorm(yp, final_w)
    y_sample = rmsnorm(ys, final_w)
    return (y_prompt, y_sample, jnp.stack(kp_l), jnp.stack(vp_l), jnp.stack(sp_l),
            jnp.stack(ks_l), jnp.stack(vs_l), jnp.stack(ss_l))


_drawn_inputs = setup_inputs


def setup_inputs(seed=0):
    import zlib

    import numpy as np

    out = dict(_drawn_inputs(seed))
    spreads = {}
    factors = {'lam_k2': 6.252,
     'subln_w': 2.707,
     'gnorm_w': 12.038,
     'final_w': 7.493,
     'lam_q1': 3.599,
     'norm2_w': 4.285}
    for name, (base, spread) in spreads.items():
        noise = np.random.default_rng([zlib.crc32(name.encode()), seed]).standard_normal(out[name].shape)
        drawn = base * np.exp(spread * noise) if base else spread * noise
        out[name] = __import__('jax').numpy.asarray(drawn.astype(out[name].dtype))
    for name, factor in factors.items():
        out[name] = (out[name] * factor).astype(out[name].dtype)
    return out
```

```python
from contextlib import ExitStack

import concourse.bass as bass
from concourse import mybir

P = 128
D = 1024
DC = D // P
SEQ = 2048
NT = SEQ // P
TILES = NT + 1
HEADS = 4
HW = 512
EPS = 1e-6
N_GRP = 4
N_EXP = 32
LOGITS = N_GRP + N_EXP
D_EXP = 512
QUEUE = TILES * P
PAD_ROWS = P // 2
N_BLOCKS = 2 * TILES + N_EXP - 1
LAM_INIT = 0.8 - 0.6
HIDDEN = -1e30
DEC_B = 8
DEC = 16
F32 = mybir.dt.float32
I32 = mybir.dt.int32
U32 = mybir.dt.uint32
U8 = mybir.dt.uint8
BF16 = mybir.dt.bfloat16
ALU = mybir.AluOpType
ACT = mybir.ActivationFunctionType
AX = mybir.AxisListType
QA, KA, VA, KT, FR, QR, IR, GR = range(8)
ORDER = range(8)
W_COL = {QA: 0, KA: 1, VA: 2, QR: 3, FR: 4, IR: 5, GR: 6}
CHANNEL_MAJOR = (QA, QR, FR)


class Chain:

    def __init__(self, eng, sem):
        self.eng, self.sem, self.base, self.n = eng, sem, 0, 0

    def loop(self, i, per_iter):
        self.start, self.n = self.base + self.n, 0
        self.base = i * per_iter + self.start
        self.per_iter = per_iter

    def end_loop(self, trips):
        assert self.n == self.per_iter, (self.sem, self.n, self.per_iter)
        self.base, self.n = self.start + trips * self.per_iter, 0

    def after(self, ins):
        ins.then_inc(self.sem, 1)
        self.n += 1
        self.eng.wait_ge(self.sem, self.base + self.n)


def stage_semaphores(nc, ctx):
    held = []

    def give_back():
        nc.clear_and_free_semaphores(held)
        nc.all_engine_barrier()

    def sem(name):
        held.append(nc.alloc_semaphore(name))
        return held[-1]

    ctx.callback(give_back)
    return sem


def row(ap, t):
    return ap[bass.ds(t, 1)].rearrange("o p d -> (o p) d")


def wait(eng, sem, value):
    if not isinstance(value, int) or value > 0:
        eng.wait_ge(sem, value)


def levels(t):
    top = P // 2 if not (isinstance(t, int) and t == NT) else DEC // 2
    halves = []
    while top >= 1:
        halves.append(top)
        top //= 2
    return list(enumerate([0] + halves))


def heads(ap):
    return ap.rearrange("p (h t) -> p h t", h=HEADS)


def project(nc, dr, consts):
    ident = consts["ident"]
    with ExitStack() as ctx:
        sb = lambda n, s, d=F32: ctx.enter_context(nc.sbuf_tensor(n, s, d))
        ps = lambda n, s, d=F32: ctx.enter_context(nc.psum_tensor(n, s, d))
        sem = stage_semaphores(nc, ctx)
        w = sb("w_in_sb", [P, DC, 7 * HW])
        n1 = sb("norm1_row", [P, D])
        x = sb("x_tile", [P, D])
        h = sb("h_tile", [P, D])
        junk = sb("square_out", [P, D], BF16)
        st = sb("rms_stats", [P, 4])
        hT = sb("hT", [P, 2, DC, P])
        z = sb("z_ring", [P, 4, HW])
        F = sb("forget", [P, HW])
        qraw = sb("q_raw", [P, HW])
        eq = sb("exp_q", [P, HW])
        dl = sb("decay_to_end", [P, HW])
        bcum = sb("log_decay", [P, 2, HW])
        q = sb("q_silu", [P, 2, HW])
        k = sb("k_gate", [P, 2, HW])
        qe = sb("q_decayed", [P, 2, HW])
        kd = sb("k_decayed", [P, HW])
        kdT = sb("k_decayed_T", [P, HW])
        ir = sb("ir", [P, 2, HW])
        gr = sb("gr", [P, 2, HW])
        gate = sb("gate", [P, HW])
        gnrow = sb("gnorm_row", [P, P])
        diff = sb("level_decay", [P, 2, HW])
        X = sb("level_operand", [P, 2, HW])
        A = sb("scores_T", [P, HW])
        S = sb("state", [P, HW])
        o_row = sb("rec_out", [P, HW])
        mask = sb("level_mask", [P, 8, P], U8)
        reset = sb("reset", [P, HW])
        lb = sb("lb", [P, HEADS])
        oml = sb("one_minus_lb", [P, HEADS])
        lbp = sb("lb_param_sb", [P, 2, HEADS])
        eL = sb("decay_of_tile", [P, 2, HEADS * DEC_B])
        ssr = sb("rec_stats", [P, 12])
        rowmask = sb("stream_mask", [P, DEC_B])
        S0 = w[:, :, 0:HW]
        qez = w[:, :, HW:2 * HW]
        kdz = w[:, :, 2 * HW:3 * HW]
        Sout = w[:, :, 3 * HW:4 * HW]

        hps = ps("hT_psum", [P, 2, HW])
        zps = [ps(f"z_psum{s}", [P, HW]) for s in range(2)]
        lps = [ps(f"level_psum{s}", [P, HW]) for s in range(2)]
        ops = ps("rec_out_psum", [P, HW])
        mps = ps("state_psum", [P, HW])

        w_in = [sem(f"w_loaded{g}") for g in range(7)]
        row_in = sem("rows_loaded")
        x_in = sem("x_loaded")
        act_step, dve_step, pool_step = sem("p1_act_step"), sem("p1_dve_step"), sem("p1_pool_step")
        rstd_ok, h_ok, hT_ps = sem("rstd_ready"), sem("h_ready"), sem("hT_transposed")
        hT_act, hT_dve = sem("hT_half0_ready"), sem("hT_half1_ready")
        z_ps, z_act, z_dve = sem("z_in_psum"), sem("z_even_copied"), sem("z_odd_copied")
        z_out = [sem(f"z_stored{s}") for s in range(4)]
        f_ok, lf_ok, b_ok, eq_ok, qk_ok = sem("f_ready"), sem("logf_ready"), sem("b_ready"), sem("expq_ready"), sem("qk_ready")
        eb_ok, dl_ok, ed_ok, qek_ok = sem("expb_ready"), sem("enddiff_ready"), sem("enddecay_ready"), sem("decayed_ready")
        diff_ok, E_ok, X_ok = sem("level_diff_ready"), sem("level_exp_ready"), sem("level_operand_ready")
        lv_ps, cp_ok = sem("level_in_psum"), sem("level_merged")
        kdt_ps, kdt_ok, st_ps, s_ok = sem("kdT_in_psum"), sem("kdT_ready"), sem("state_in_psum"), sem("state_ready")
        o_ps, r_ok, eg_ok, orow_ok, orow_out = sem("o_in_psum"), sem("rec_rstd_ready"), sem("expg_ready"), sem("rec_out_ready"), sem("rec_out_stored")
        lb_e, masks_ok, sp_out = sem("lb_exp"), sem("masks_ready"), sem("state_prompt_stored")
        S0_in, qz_ok, kz_ok, so_ps, so_ok, ss_out = (sem("state_rec_loaded"), sem("sample_q_zeroed"), sem("sample_k_ready"),
                                                    sem("sample_state_in_psum"), sem("sample_state_ready"), sem("state_sample_stored"))
        qzf_ok = sem("sample_q_ready")
        merge_turn = sem("merge_turn")
        block = ctx.enter_context(nc.Block())

        xp = dr["x_prompt"].rearrange("b (t p) d -> (b t) p d", p=P)
        xs = dr["x_sample"].rearrange("b t d -> (b t) d")
        kp = dr["k_prompt"].rearrange("l b (t p) h d -> (l b t) p (h d)", p=P)
        vp = dr["v_prompt"].rearrange("l b (t p) h d -> (l b t) p (h d)", p=P)
        ksm = dr["k_sample"].rearrange("l b t h d -> (l b t) (h d)")
        vsm = dr["v_sample"].rearrange("l b t h d -> (l b t) (h d)")
        TRIPS = NT // 2 - 1

        def is_last(t):
            return isinstance(t, int) and t == NT

        @block.sync
        def _(sp):
            wv = dr["w_in"].rearrange("l (c p) n -> p (l c) n", p=P)

            def load_x(t):
                wait(sp, h_ok, t)
                sp.dma_start(x[:, :], xs if is_last(t) else row(xp, t)).then_inc(x_in, 16)

            load_x(0)
            sp.dma_start(n1[:, :], dr["norm1_w"].to_broadcast([P, D])).then_inc(row_in, 16)
            sp.dma_start(gnrow[:, :], dr["gnorm_w"].to_broadcast([P, P])).then_inc(row_in, 16)
            with nc.allow_non_contiguous_dma(reason="1024 floats, once"):
                for i in range(2):
                    sp.dma_start(lbp[:, i, :], dr["lb_param"][i].rearrange("(h p) -> p h", p=P)).then_inc(row_in, 16)
            for j in ORDER:
                if j in W_COL:
                    g = W_COL[j]
                    sp.dma_start(w[:, :, g * HW:(g + 1) * HW], wv[:, :, g * HW:(g + 1) * HW]).then_inc(w_in[g], 16)

            def store(t, j):
                sp.wait_ge(z_dve if j % 2 else z_act, 4 * t + j // 2 + 2)
                if j == KA:
                    dst = ksm if is_last(t) else row(kp, t)
                elif j == VA:
                    dst = vsm if is_last(t) else row(vp, t)
                else:
                    dst = row(dr["z"][j], t)
                sp.dma_start(dst, z[:, j, :]).then_inc(z_out[j], 16)

            def store_rec(t):
                sp.wait_ge(orow_ok, t + 1)
                sp.dma_start(row(dr["rec"], t), o_row[:, :]).then_inc(orow_out, 16)

            def tile(t, rec=True):
                if not is_last(t):
                    load_x(t + 1)
                for j in (QA, KA, VA, KT):
                    store(t, j)
                if rec:
                    store_rec(t - 1)

            tile(0, False)
            tile(1)
            with sp.Fori(1, NT // 2 - 1) as i:
                for u in range(2):
                    tile(i * 2 + u)
            for t in (NT - 2, NT - 1, NT):
                tile(t)
            sp.wait_ge(s_ok, NT + 1)
            sp.dma_start(dr["state_prompt"][0, 0].rearrange("h k v -> k h v"), heads(S[:, :])).then_inc(sp_out, 16)
            sp.wait_ge(z_ps, 8 * TILES)
            for b in range(DEC_B):
                sp.dma_start(heads(S0[:, b, :]), dr["state_rec"][0, b].rearrange("h k v -> k h v")).then_inc(S0_in, 16)
            store_rec(NT)
            sp.wait_ge(so_ok, DEC_B)
            for b in range(DEC_B):
                sp.dma_start(dr["state_sample"][0, b].rearrange("h k v -> k h v"), heads(Sout[:, b, :])).then_inc(ss_out, 16)
            for s in range(4):
                sp.wait_ge(z_out[s], 16 * TILES)
            sp.wait_ge(orow_out, 16 * TILES)
            sp.wait_ge(sp_out, 16)
            sp.wait_ge(ss_out, 16 * DEC_B)

        @block.gpsimd
        def _(pool):
            chain = Chain(pool, pool_step)
            pool.memset(mask[:, :, :], 0.0)
            chain.after(pool.memset(rowmask[:, :], 1.0))
            mf = diff[:, :, :].rearrange("p a n -> p (a n)").rearrange("p (l t) -> p l t", t=P)
            chain.after(pool.memset(mf, 0.0))
            for l, m in levels(0)[1:]:
                v = mf[:, l, :].rearrange("p (g s m) -> p g s m", s=2, m=m)[:, :, 1, :]
                chain.after(pool.memset(v, 1.0))
                chain.after(pool.affine_select(out=v, in_=v, compare_op=ALU.is_ge, fill=0.0, base=0,
                                               pattern=[[-2 * m, P // (2 * m)], [0, m]], channel_multiplier=1))
                chain.after(pool.affine_select(out=v, in_=v, compare_op=ALU.is_ge, fill=0.0, base=m - 1,
                                               pattern=[[2 * m, P // (2 * m)], [0, m]], channel_multiplier=-1))
            chain.after(pool.tensor_copy(mask[:, 1:8, :], mf[:, 1:8, :]))
            chain.after(pool.tensor_copy(mask[:, 0, :], ident[:, :]))
            chain.after(pool.affine_select(out=rowmask[:, :], in_=rowmask[:, :], compare_op=ALU.is_ge, fill=0.0, base=0,
                                           pattern=[[-DEC, DEC_B]], channel_multiplier=1))
            pool.affine_select(out=rowmask[:, :], in_=rowmask[:, :], compare_op=ALU.is_ge, fill=0.0, base=DEC - 1,
                               pattern=[[DEC, DEC_B]], channel_multiplier=-1).then_inc(masks_ok, 1)

            def diffs(t, u):
                pool.wait_ge(b_ok, t + 1)
                n = DEC if is_last(t) else P
                bg = bcum[:, u, :].rearrange("p (g n) -> p g n", n=n)
                end = bg[:, :, n - 1:n].to_broadcast([P, HW // n, n])
                pool.tensor_tensor(dl[:, :].rearrange("p (g n) -> p g n", n=n), end, bg, ALU.subtract).then_inc(dl_ok, 1)
                for pos, m in levels(t)[1:]:
                    s = (u + pos - 1) % 2
                    wait(pool, X_ok, 7 * t + pos - 2)
                    bv = bcum[:, u, :].rearrange("p (g s m) -> p g s m", s=2, m=m)
                    dv = diff[:, s, :].rearrange("p (g s m) -> p g s m", s=2, m=m)
                    split = bv[:, :, 0, m - 1:m].to_broadcast([P, HW // (2 * m), m])
                    pool.tensor_tensor(dv[:, :, 0, :], split, bv[:, :, 0, :], ALU.subtract)
                    pool.tensor_tensor(dv[:, :, 1, :], bv[:, :, 1, :], split, ALU.subtract).then_inc(diff_ok, 1)

            diffs(0, 0)
            diffs(1, 1)
            with pool.Fori(1, NT // 2) as i:
                for u in range(2):
                    diffs(i * 2 + u, u)
            pool.wait_ge(z_ps, 8 * TILES)
            pool.memset(qez, 0.0).then_inc(qz_ok, 1)
            diffs(NT, 0)

        @block.scalar
        def _(act):
            chain = Chain(act, act_step)
            act.sem_inc(z_act, 1)
            act.wait_ge(row_in, 64)
            act.wait_ge(consts["sem"], consts["n"])

            def stats(t):
                act.wait_ge(x_in, 16 * t + 16)
                wait(act, h_ok, t)
                chain.after(nc.scalar.activation(junk[:, :], x[:, :], ACT.Square, accum_out=st[:, 0:1]))
                chain.after(nc.scalar.activation(st[:, 1:2], st[:, 0:1], ACT.Ln, scale=1.0 / D, bias=consts["eps"][:, 0:1]))
                nc.scalar.activation(st[:, 2:3], st[:, 1:2], ACT.Exp, scale=-0.5).then_inc(rstd_ok, 1)

            def hT_copy(t, u):
                act.wait_ge(hT_ps, t + 1)
                nc.scalar.copy(hT[:, u, 0:4, :].rearrange("p c t -> p (c t)"), hps[:, 0, :]).then_inc(hT_act, 1)

            def evac(t, u, j):
                act.wait_ge(z_ps, 8 * t + j + 1)
                if j == FR:
                    wait(act, b_ok, t)
                    nc.scalar.activation(F[:, :], zps[0][:, :], ACT.Exp, scale=-1.0).then_inc(z_act, 1)
                elif j == IR:
                    nc.scalar.copy(ir[:, u, :], zps[0][:, :]).then_inc(z_act, 1)
                else:
                    wait(act, z_out[j], 16 * t)
                    nc.scalar.copy(z[:, j, :], zps[0][:, :]).then_inc(z_act, 1)

            def expo(t, u, pos):
                s = (u + pos - 1) % 2
                act.wait_ge(diff_ok, 7 * t + pos)
                nc.scalar.activation(diff[:, s, :], diff[:, s, :], ACT.Exp).then_inc(E_ok, 1)

            def logf(t):
                act.wait_ge(f_ok, t + 1)
                nc.scalar.activation(F[:, :], F[:, :], ACT.Ln).then_inc(lf_ok, 1)

            def expq(t):
                act.wait_ge(z_dve, 4 * t + 4)
                nc.scalar.activation(eq[:, :], qraw[:, :], ACT.Exp, scale=-1.0).then_inc(eq_ok, 1)

            def expb(t, u):
                act.wait_ge(b_ok, t + 1)
                nc.scalar.activation(eq[:, :], bcum[:, u, :], ACT.Exp).then_inc(eb_ok, 1)
                act.wait_ge(dl_ok, t + 1)
                nc.scalar.activation(dl[:, :], dl[:, :], ACT.Exp).then_inc(ed_ok, 1)

            def expg(t, u):
                act.wait_ge(z_dve, 4 * t + 5)
                wait(act, orow_ok, t)
                nc.scalar.activation(gate[:, :], gr[:, u, :], ACT.Exp, scale=-1.0).then_inc(eg_ok, 1)

            def kdT_copy(t):
                act.wait_ge(kdt_ps, t + 1)
                nc.scalar.copy(kdT[:, :], mps[:, :]).then_inc(kdt_ok, 1)

            def rec_stats(t):
                act.wait_ge(o_ps, t + 1)
                for hd in range(HEADS):
                    ins = nc.scalar.activation(junk[:, 0:P], ops[:, hd * P:(hd + 1) * P], ACT.Square, accum_out=ssr[:, hd:hd + 1])
                    chain.after(ins)
                chain.after(nc.scalar.activation(ssr[:, 4:8], ssr[:, 0:4], ACT.Ln, scale=1.0 / P, bias=consts["eps"][:, 0:1]))
                nc.scalar.activation(ssr[:, 8:12], ssr[:, 4:8], ACT.Exp, scale=-0.5).then_inc(r_ok, 1)

            def tile(t, u, rec=True):
                g, v = t - 1, 1 - u
                evac(t, u, QA)
                if rec:
                    expo(g, v, 1)
                if not is_last(t):
                    stats(t + 1)
                if rec:
                    expo(g, v, 2)
                evac(t, u, VA)
                if rec:
                    expo(g, v, 3)
                    expo(g, v, 4)
                evac(t, u, FR)
                if not is_last(t):
                    hT_copy(t + 1, 1 - u)
                if rec:
                    expo(g, v, 5)
                logf(t)
                expq(t)
                if rec:
                    expo(g, v, 6)
                    kdT_copy(g)
                evac(t, u, IR)
                if rec:
                    expo(g, v, 7)
                expb(t, u)
                if rec:
                    rec_stats(g)
                expg(t, u)

            act.wait_ge(lb_e, 1)
            nc.scalar.activation(oml[:, :], oml[:, :], ACT.Exp).then_inc(lb_e, 1)
            stats(0)
            hT_copy(0, 0)
            tile(0, 0, False)
            tile(1, 1)
            with act.Fori(1, NT // 2) as i:
                chain.loop(i - 1, 14)
                for u in range(2):
                    tile(i * 2 + u, u)
            chain.end_loop(TRIPS)
            tile(NT, 0)
            for pos, m in levels(NT)[1:]:
                expo(NT, 0, pos)
            kdT_copy(NT)
            rec_stats(NT)

        @block.vector
        def _(dve):
            chain = Chain(dve, dve_step)
            dve.sem_inc(z_dve, 1)
            tt, ts, stt = nc.vector.tensor_tensor, nc.vector.tensor_scalar, nc.vector.scalar_tensor_tensor
            dve.wait_ge(row_in, 64)
            dve.wait_ge(consts["sem"], consts["n"])
            chain.after(nc.vector.memset(reset[:, :], 1.0))
            nc.vector.memset(heads(reset[:, :])[:, :, 0:1], 0.0)
            nc.vector.memset(A[:, :], 0.0)
            chain.after(nc.vector.memset(S[:, :], 0.0))
            tt(oml[:, :], lbp[:, 1, :], lbp[:, 0, :], ALU.subtract).then_inc(lb_e, 1)
            dve.wait_ge(lb_e, 2)
            chain.after(ts(oml[:, :], oml[:, :], 1.0, None, ALU.add))
            chain.after(nc.vector.reciprocal(lb[:, :], oml[:, :]))
            chain.after(ts(oml[:, :], lb[:, :], -1.0, 1.0, ALU.mult, ALU.add))
            chain.after(ts(gnrow[:, :], gnrow[:, :], 1.0, None, ALU.mult))
            dve.sem_inc(s_ok, 1)

            def make_h(t):
                dve.wait_ge(rstd_ok, t + 1)
                wait(dve, hT_ps, t)
                stt(out=h[:, :], in0=x[:, :], scalar=st[:, 2:3], in1=n1[:, :], op0=ALU.mult, op1=ALU.mult).then_inc(h_ok, 1)

            def hT_copy(t, u):
                dve.wait_ge(hT_ps, t + 1)
                nc.vector.tensor_copy(hT[:, u, 4:8, :].rearrange("p c t -> p (c t)"), hps[:, 1, :]).then_inc(hT_dve, 1)

            def evac(t, u, j):
                dve.wait_ge(z_ps, 8 * t + j + 1)
                if j in (KA, KT):
                    wait(dve, z_out[j], 16 * t)
                dst = {KA: z[:, KA, :], KT: z[:, KT, :], QR: qraw[:, :], GR: gr[:, u, :]}[j]
                nc.vector.tensor_copy(dst, zps[1][:, :]).then_inc(z_dve, 1)

            def forget(t, u):
                dve.wait_ge(z_act, 4 * t + 4)
                chain.after(ts(F[:, :], F[:, :], 1.0, None, ALU.add))
                chain.after(nc.vector.reciprocal(F[:, :], F[:, :]))
                for hd in range(HEADS):
                    f = F[:, hd * P:(hd + 1) * P]
                    ins = ts(f, f, oml[:, hd:hd + 1], lb[:, hd:hd + 1], ALU.mult, ALU.add)
                chain.after(ins)
                ts(k[:, u, :], F[:, :], -1.0, 1.0, ALU.mult, ALU.add).then_inc(f_ok, 1)

            def silu_q(t, u):
                dve.wait_ge(eq_ok, t + 1)
                chain.after(ts(eq[:, :], eq[:, :], 1.0, None, ALU.add))
                chain.after(nc.vector.reciprocal(eq[:, :], eq[:, :]))
                tt(q[:, u, :], qraw[:, :], eq[:, :], ALU.mult).then_inc(qk_ok, 1)

            def scan(t, u):
                dve.wait_ge(lf_ok, t + 1)
                if is_last(t):
                    chain.after(nc.vector.memset(reset[:, :].rearrange("p (g n) -> p g n", n=DEC)[:, :, 0:1], 0.0))
                nc.vector.tensor_tensor_scan(bcum[:, u, :], reset[:, :], F[:, :], 0.0, ALU.mult, ALU.add).then_inc(b_ok, 1)

            def decayed(t, u):
                n = DEC if is_last(t) else P
                dve.wait_ge(eb_ok, t + 1)
                tt(qe[:, u, :], q[:, u, :], eq[:, :], ALU.mult)
                nc.vector.tensor_copy(eL[:, u, 0:HW // n], eq[:, :].rearrange("p (g n) -> p g n", n=n)[:, :, n - 1])
                dve.wait_ge(ed_ok, t + 1)
                wait(dve, kdt_ps, t)
                tt(kd[:, :], k[:, u, :], dl[:, :], ALU.mult).then_inc(qek_ok, 1)

            def operand(t, u, pos, m):
                s = (u + pos - 1) % 2
                dve.wait_ge(E_ok, 7 * t + pos)
                wait(dve, lv_ps, 8 * t + (pos - 1 if pos >= 3 else 0))
                if pos == 1:
                    dve.wait_ge(qk_ok, t + 1)
                v = lambda a: a.rearrange("p (g s m) -> p g s m", s=2, m=m)
                tt(v(X[:, s, :])[:, :, 0, :], v(k[:, u, :])[:, :, 0, :], v(diff[:, s, :])[:, :, 0, :], ALU.mult)
                tt(v(X[:, s, :])[:, :, 1, :], v(q[:, u, :])[:, :, 1, :], v(diff[:, s, :])[:, :, 1, :], ALU.mult).then_inc(X_ok, 1)

            def merge(t, pos, m):
                dve.wait_ge(lv_ps, 8 * t + pos + 1)
                dve.sem_inc(merge_turn, 1)
                l = 0 if m == 0 else 7 - (m.bit_length() - 1)
                if pos == 0 and is_last(t):
                    chain.after(nc.vector.memset(A[:, :], 0.0))
                if isinstance(t, int) and t == 0 and pos == 0:
                    dve.wait_ge(masks_ok, 1)
                mk = mask[:, l:l + 1, :].to_broadcast([P, HEADS, P])
                ins = nc.vector.copy_predicated(heads(A[:, :]), mk, heads(lps[pos % 2][:, :]))
                ins.then_inc(cp_ok, 1)

            def rec_gate(t, u):
                dve.wait_ge(eg_ok, t + 1)
                chain.after(ts(gate[:, :], gate[:, :], 1.0, None, ALU.add))
                chain.after(nc.vector.reciprocal(gate[:, :], gate[:, :]))
                chain.after(tt(gate[:, :], gate[:, :], gr[:, u, :], ALU.mult))
                chain.after(tt(heads(gate[:, :]), heads(gate[:, :]), gnrow[:, None, :].to_broadcast([P, HEADS, P]), ALU.mult))

            def rec_row(t):
                dve.wait_ge(r_ok, t + 1)
                wait(dve, orow_out, 16 * t)
                for hd in range(HEADS):
                    c = slice(hd * P, (hd + 1) * P)
                    ins = stt(out=o_row[:, c], in0=ops[:, c], scalar=ssr[:, 8 + hd:9 + hd], in1=gate[:, c], op0=ALU.mult, op1=ALU.mult)
                ins.then_inc(orow_ok, 1)

            def state(t, u):
                dve.wait_ge(st_ps, t + 1)
                for hd in range(HEADS):
                    c = slice(hd * P, (hd + 1) * P)
                    ins = stt(out=S[:, c], in0=S[:, c], scalar=eL[:, u, hd:hd + 1], in1=mps[:, c], op0=ALU.mult, op1=ALU.add)
                ins.then_inc(s_ok, 1)

            def tile(t, u, rec=True):
                g, v = t - 1, 1 - u
                lv = levels(0)
                if rec:
                    merge(g, 0, 0)
                    operand(g, v, *lv[1])
                evac(t, u, KA)
                if not is_last(t):
                    make_h(t + 1)
                if rec:
                    merge(g, *lv[1])
                    operand(g, v, *lv[2])
                    rec_gate(g, v)
                    merge(g, *lv[2])
                    operand(g, v, *lv[3])
                evac(t, u, KT)
                if rec:
                    merge(g, *lv[3])
                    operand(g, v, *lv[4])
                forget(t, u)
                if not is_last(t):
                    hT_copy(t + 1, 1 - u)
                if rec:
                    merge(g, *lv[4])
                    operand(g, v, *lv[5])
                evac(t, u, QR)
                if rec:
                    merge(g, *lv[5])
                    operand(g, v, *lv[6])
                silu_q(t, u)
                scan(t, u)
                if rec:
                    merge(g, *lv[6])
                    operand(g, v, *lv[7])
                    merge(g, *lv[7])
                decayed(t, u)
                evac(t, u, GR)
                if rec:
                    rec_row(g)
                    state(g, v)

            make_h(0)
            hT_copy(0, 0)
            tile(0, 0, False)
            tile(1, 1)
            with dve.Fori(1, NT // 2) as i:
                chain.loop(i - 1, 18)
                for u in range(2):
                    tile(i * 2 + u, u)
            chain.end_loop(TRIPS)
            tile(NT, 0)
            dve.wait_ge(qz_ok, 1)
            dve.wait_ge(qek_ok, TILES)
            for b in range(DEC_B):
                c = slice(b * DEC, (b + 1) * DEC)
                ins = nc.vector.tensor_copy(heads(qez[:, b, :])[:, :, c], heads(qe[:, 0, :])[:, :, c])
            ins.then_inc(qzf_ok, 1)
            lv = levels(NT)
            merge(NT, 0, 0)
            for pos, m in lv[1:]:
                operand(NT, 0, pos, m)
                merge(NT, pos, m)
            rec_gate(NT, 0)
            dve.wait_ge(kdt_ok, TILES)
            for b in range(DEC_B):
                ins = ts(kdz[:, b, :], kdT[:, :], rowmask[:, b:b + 1], None, ALU.mult)
            ins.then_inc(kz_ok, 1)
            rec_row(NT)
            dve.wait_ge(S0_in, 16 * DEC_B)
            for b in range(DEC_B):
                dve.wait_ge(so_ps, b + 1)
                for hd in range(HEADS):
                    c = slice(hd * P, (hd + 1) * P)
                    g = hd * DEC_B + b
                    ins = stt(out=Sout[:, b, c], in0=S0[:, b, c], scalar=eL[:, 0, g:g + 1], in1=lps[b % 2][:, c],
                              op0=ALU.mult, op1=ALU.add)
                ins.then_inc(so_ok, 1)

        @block.tensor
        def _(pe):
            def turn(t):
                pe.wait_ge(h_ok, t + 1)
                wait(pe, hT_act, t)
                wait(pe, hT_dve, t)
                for c in range(DC):
                    mm = pe.transpose(hps[:, c // 4, (c % 4) * P:(c % 4 + 1) * P], h[:, c * P:(c + 1) * P], ident[:, :])
                mm.then_inc(hT_ps, 1)

            def group(t, u, j):
                pe.wait_ge(z_dve if j % 2 else z_act, 4 * t + j // 2 + 1)
                out = zps[j % 2]
                if j == KT:
                    pe.wait_ge(z_dve, 4 * t + KA // 2 + 2)
                    for hd in range(HEADS):
                        mm = pe.transpose(out[:, hd * P:(hd + 1) * P], z[:, KA, hd * P:(hd + 1) * P], ident[:, :])
                    mm.then_inc(z_ps, 1)
                    return
                g = W_COL[j]
                if isinstance(t, int) and t == 0:
                    pe.wait_ge(w_in[g], 16)
                if j in CHANNEL_MAJOR:
                    for hd in range(HEADS):
                        for c in range(DC):
                            col = g * HW + hd * P
                            mm = pe.matmul(out[:, hd * P:(hd + 1) * P], w[:, c, col:col + P], hT[:, u, c, :],
                                           start=(c == 0), stop=(c == DC - 1))
                else:
                    for c in range(DC):
                        mm = pe.matmul(out[:, :], hT[:, u, c, :], w[:, c, g * HW:(g + 1) * HW],
                                       start=(c == 0), stop=(c == DC - 1))
                mm.then_inc(z_ps, 1)

            def level(t, u, pos):
                wait(pe, cp_ok, 8 * t + pos - 1)
                if pos == 0:
                    pe.wait_ge(qk_ok, t + 1)
                    left, right = k[:, u, :], q[:, u, :]
                else:
                    pe.wait_ge(X_ok, 7 * t + pos)
                    left = right = X[:, (u + pos - 1) % 2, :]
                for hd in range(HEADS):
                    c = slice(hd * P, (hd + 1) * P)
                    mm = pe.matmul(lps[pos % 2][:, c], left[:, c], right[:, c], start=True, stop=True)
                mm.then_inc(lv_ps, 1)

            def turn_kd(t):
                pe.wait_ge(qek_ok, t + 1)
                pe.wait_ge(s_ok, t + 1)
                for hd in range(HEADS):
                    c = slice(hd * P, (hd + 1) * P)
                    mm = pe.transpose(mps[:, c], kd[:, c], ident[:, :])
                mm.then_inc(kdt_ps, 1)

            def rec_out(t, u):
                pe.wait_ge(cp_ok, 8 * t + 8 if not is_last(t) else 8 * NT + len(levels(NT)))
                wait(pe, orow_ok, t)
                pe.wait_ge(s_ok, t + 1)
                for hd in range(HEADS):
                    c = slice(hd * P, (hd + 1) * P)
                    pe.matmul(ops[:, c], A[:, c], ir[:, u, c], start=True, stop=False)
                    if is_last(t):
                        for b in range(DEC_B):
                            mm = pe.matmul(ops[:, c], qez[:, b, c], S0[:, b, c], start=False, stop=(b == DEC_B - 1))
                    else:
                        mm = pe.matmul(ops[:, c], qe[:, u, c], S[:, c], start=False, stop=True)
                mm.then_inc(o_ps, 1)

            def new_state(t, u):
                pe.wait_ge(kdt_ok, t + 1)
                for hd in range(HEADS):
                    c = slice(hd * P, (hd + 1) * P)
                    mm = pe.matmul(mps[:, c], kdT[:, c], ir[:, u, c], start=True, stop=True)
                mm.then_inc(st_ps, 1)

            def tile(t, u, rec=True):
                pe.wait_ge(hT_act, t + 1)
                pe.wait_ge(hT_dve, t + 1)
                for j in range(8):
                    group(t, u, j)
                    if rec:
                        g, v = t - 1, 1 - u
                        if j < 7:
                            level(g, v, j)
                        if j == 4:
                            turn_kd(g)
                        if j == 6:
                            level(g, v, 7)
                        if j == 7:
                            rec_out(g, v)
                            new_state(g, v)
                    if j == 3 and not is_last(t):
                        turn(t + 1)

            pe.wait_ge(consts["sem"], consts["n"])
            turn(0)
            tile(0, 0, False)
            tile(1, 1)
            with pe.Fori(1, NT // 2) as i:
                for u in range(2):
                    tile(i * 2 + u, u)
            tile(NT, 0)
            for pos, m in levels(NT):
                level(NT, 0, pos)
            turn_kd(NT)
            pe.wait_ge(S0_in, 16 * DEC_B)
            pe.wait_ge(qzf_ok, 1)
            pe.wait_ge(z_act, 4 * TILES + 1)
            rec_out(NT, 0)
            pe.wait_ge(kz_ok, 1)
            for b in range(DEC_B):
                wait(pe, so_ok, b - 1)
                for hd in range(HEADS):
                    c = slice(hd * P, (hd + 1) * P)
                    mm = pe.matmul(lps[b % 2][:, c], kdz[:, b, c], ir[:, 0, c], start=True, stop=True)
                mm.then_inc(so_ps, 1)


def seg_of(i):
    return [(4 * s, min(4, i + 1 - 4 * s)) for s in range(i // 4 + 1)]


def attend(nc, dr, consts):
    ident = consts["ident"]
    scale = 64 ** -0.5
    NSEG = [len(seg_of(i)) for i in range(NT)]
    BASE = [sum(NSEG[:i]) for i in range(NT)]
    PER_HEAD = sum(NSEG)

    def tile_before(h, i, back):
        i -= back
        if i >= 0:
            return h, i, NSEG[i] if i < NT else 0
        return h - 1, i + NT, 0 if isinstance(h, int) and h == 0 else NSEG[i + NT]

    def each_head(eng, step, chain=None, per_head=0):
        for i in range(NT):
            step(0, i)
        with eng.Fori(1, HEADS) as h:
            if chain:
                chain.loop(h - 1, per_head)
            for i in range(NT):
                step(h, i)
        if chain:
            chain.end_loop(HEADS - 1)
        for i in range(NT, NT + 2):
            step(HEADS - 1, i)

    with ExitStack() as ctx:
        sb = lambda n, s, d=F32: ctx.enter_context(nc.sbuf_tensor(n, s, d))
        ps = lambda n, s, d=F32: ctx.enter_context(nc.psum_tensor(n, s, d))
        sem = stage_semaphores(nc, ctx)
        q = sb("att_q", [P, NT, HW])
        k = sb("att_k", [P, NT, HW])
        v = sb("att_v", [P, NT, HW])
        qz = sb("q_by_map", [P, 2, 2, P])
        pr = sb("probs", [P, 4, 2, SEQ])
        wT = sb("weights_T", [P, 2, HW])
        o = sb("att_o", [P, 2, P])
        nmax = sb("neg_max", [P, 2, 2, 4])
        zsum = sb("seg_sum", [P, 2, 2, 4])
        fac = sb("seg_factor", [P, 2, 2, 4])
        tot = sb("row_stats", [P, 2, 6])
        coef = sb("map_coef", [P, 2])
        lamv = sb("lam_rows", [P, 4, 64])
        lamd = sb("lam_dots", [P, 4])
        sps = [ps(f"score_psum{s}", [P, 2, HW]) for s in range(2)]
        tps = [ps(f"weights_T_psum{s}", [P, HW]) for s in range(2)]
        ops = [ps(f"att_out_psum{s}", [P, HW]) for s in range(2)]

        q_in, k_in, v_in = ([sem(f"att_{n}_loaded{g}") for g in range(4)] for n in "qkv")
        lam_in, lam_e = sem("lam_loaded"), sem("lam_exp")
        dve_step = sem("p2_dve_step")
        qz_ok, s_ps, m_ok, e_ok = sem("q_maps_ready"), sem("scores_in_psum"), sem("seg_max_ready"), sem("seg_exp_ready")
        nM_ok, ef_ok, w_ok = sem("row_max_ready"), sem("seg_factor_exp"), sem("weights_ready")
        tg_ps, wt_sb, pv, wt_tile = sem("weights_T_in_psum"), sem("weights_T_copied"), sem("pv_done"), sem("probs_used")
        o_ok, o_free = sem("att_o_ready"), sem("att_o_free")
        att_out = [sem(f"att_stored{s}") for s in range(2)]
        fac_ok, w1_ok, stand = sem("factors_ready"), sem("second_map_weighed"), sem("p2_pool_stand")
        block = ctx.enter_context(nc.Block())
        vp = dr["v_prompt"].rearrange("l b (t p) h d -> (l b t) p (h d)", p=P)

        @block.sync
        def _(sp):
            for n, name in enumerate(("lam_q1", "lam_k1", "lam_q2", "lam_k2")):
                sp.dma_start(lamv[:, n, :], dr[name].to_broadcast([P, 64])).then_inc(lam_in, 16)
            for g in range(4):
                c = slice(4 * g, 4 * g + 4)
                sp.dma_start(q[:, c, :], dr["z"][QA][c].rearrange("t p d -> p t d")).then_inc(q_in[g], 16)
                sp.dma_start(k[:, c, :], dr["z"][KT][c].rearrange("t p d -> p t d")).then_inc(k_in[g], 16)
                sp.dma_start(v[:, c, :], vp[c].rearrange("t p d -> p t d")).then_inc(v_in[g], 16)
            att = dr["att"]
            with sp.Fori(0, HEADS) as h:
                for i in range(NT):
                    sp.wait_ge(o_ok, h * NT + i + 1)
                    sp.dma_start(att[i][:, bass.ds(h * P, P)], o[:, i % 2, :]).then_inc(att_out[i % 2], 16)
                    sp.wait_ge(att_out[i % 2], (h * (NT // 2) + i // 2) * 16 + 16)
                    sp.sem_inc(o_free, 1)

        @block.gpsimd
        def _(pool):
            with pool.Fori(0, HEADS) as h:
                for i in range(NT):
                    pool.wait_ge(fac_ok, h * NT + i + 1)
                    for s in range(NSEG[i]):
                        k0, kw = seg_of(i)[s]
                        p1 = pr[:, i % 4, 1, k0 * P:(k0 + kw) * P]
                        pool.sem_inc(stand, 1)
                        pool.tensor_scalar(p1, p1, fac[:, i % 2, 1, s:s + 1], 1.0, ALU.mult, ALU.mult).then_inc(w1_ok, 1)

        @block.scalar
        def _(act):
            act.sem_inc(e_ok, 2)
            act.sem_inc(wt_sb, 2)
            act.wait_ge(lam_e, 1)
            nc.scalar.activation(lamd[:, 0:2], lamd[:, 2:4], ACT.Exp).then_inc(lam_e, 1)

            def expo(h, i, s):
                n = h * PER_HEAD + BASE[i] + s
                k0, kw = seg_of(i)[s]
                if s == 0:
                    wait(act, wt_tile, h * NT + i - 3)
                act.wait_ge(m_ok, n + 1)
                for c in range(2):
                    ins = nc.scalar.activation(pr[:, i % 4, c, k0 * P:(k0 + kw) * P], sps[(BASE[i] + s) % 2][:, c, 0:kw * P],
                                               ACT.Exp, bias=nmax[:, i % 2, c, s:s + 1], accum_out=zsum[:, i % 2, c, s:s + 1])
                ins.then_inc(e_ok, 1)

            def factor(h, i):
                act.wait_ge(nM_ok, h * NT + i + 1)
                for c in range(2):
                    ins = nc.scalar.activation(fac[:, i % 2, c, 0:NSEG[i]], nmax[:, i % 2, c, 0:NSEG[i]], ACT.Exp,
                                               scale=-1.0, bias=tot[:, i % 2, c:c + 1])
                ins.then_inc(ef_ok, 1)

            def copy_T(h, i, s):
                n = h * PER_HEAD + BASE[i] + s
                kw = seg_of(i)[s][1]
                act.wait_ge(tg_ps, n + 1)
                act.wait_ge(pv, n + 1)
                r = (BASE[i] + s) % 2
                nc.scalar.copy(wT[:, r, 0:kw * P], tps[r][:, 0:kw * P]).then_inc(wt_sb, 1)

            def step(h, i):
                cur = NSEG[i] if i < NT else 0
                h2, i2, old = tile_before(h, i, 2)
                for s in range(max(cur, old)):
                    if s < old:
                        copy_T(h2, i2, s)
                    if s < cur:
                        expo(h, i, s)
                if cur:
                    factor(h, i)

            each_head(act, step)

        @block.vector
        def _(dve):
            chain = Chain(dve, dve_step)
            tt, ts, stt = nc.vector.tensor_tensor, nc.vector.tensor_scalar, nc.vector.scalar_tensor_tensor
            red = nc.vector.tensor_reduce
            dve.sem_inc(o_free, 2)
            dve.wait_ge(lam_in, 64)
            chain.after(tt(lamv[:, 0:4:2, :], lamv[:, 0:4:2, :], lamv[:, 1:4:2, :], ALU.mult))
            red(lamd[:, 2:4], lamv[:, 0:4:2, :], AX.X, ALU.add).then_inc(lam_e, 1)
            chain.after(nc.vector.memset(coef[:, :], 1.0))
            chain.after(nc.vector.memset(qz[:, :, :, :], 0.0))
            dve.wait_ge(lam_e, 2)
            tt(coef[:, 1:2], lamd[:, 1:2], lamd[:, 0:1], ALU.subtract).then_inc(lam_e, 1)
            dve.wait_ge(lam_e, 3)
            chain.after(ts(coef[:, 1:2], coef[:, 1:2], -LAM_INIT, None, ALU.add))

            def maps(h, i):
                if i % 4 == 0:
                    dve.wait_ge(q_in[i // 4], 16)
                wait(dve, s_ps, h * PER_HEAD + (BASE[i - 1] if i else -NSEG[NT - 1]))
                for c in range(2):
                    r = slice(64 * c, 64 * c + 64)
                    ins = ts(qz[r, i % 2, c, :], q[r, i, bass.ds(h * P, P)], scale, None, ALU.mult)
                ins.then_inc(qz_ok, 1)

            def seg_max(h, i, s):
                n = h * PER_HEAD + BASE[i] + s
                kw = seg_of(i)[s][1]
                sp_ = sps[(BASE[i] + s) % 2]
                dve.wait_ge(s_ps, n + 1)
                if s == NSEG[i] - 1:
                    chain.after(nc.vector.memset(sp_[0:64, :, kw * P - 64:kw * P], HIDDEN))
                red(nmax[:, i % 2, :, s:s + 1], sp_[:, :, 0:kw * P], AX.X, ALU.max, negate=True).then_inc(m_ok, 1)

            def row_max(h, i):
                dve.wait_ge(m_ok, h * PER_HEAD + BASE[i] + NSEG[i])
                red(tot[:, i % 2, 0:2], nmax[:, i % 2, :, 0:NSEG[i]], AX.X, ALU.min).then_inc(nM_ok, 1)

            def factors(h, i):
                n, b = NSEG[i], i % 2
                dve.wait_ge(ef_ok, h * NT + i + 1)
                dve.wait_ge(e_ok, h * PER_HEAD + BASE[i] + n + 2)
                chain.after(tt(zsum[:, b, :, 0:n], zsum[:, b, :, 0:n], fac[:, b, :, 0:n], ALU.mult))
                chain.after(red(tot[:, b, 2:4], zsum[:, b, :, 0:n], AX.X, ALU.add))
                chain.after(nc.vector.reciprocal(tot[:, b, 4:6], tot[:, b, 2:4]))
                chain.after(tt(tot[:, b, 2:4], tot[:, b, 4:6], coef[:, :], ALU.mult))
                for c in range(2):
                    ins = ts(fac[:, b, c, 0:n], fac[:, b, c, 0:n], tot[:, b, 2 + c:3 + c], None, ALU.mult)
                ins.then_inc(fac_ok, 1)

            def weigh(h, i, s):
                b, r = i % 2, i % 4
                k0, kw = seg_of(i)[s]
                c = slice(k0 * P, (k0 + kw) * P)
                dve.wait_ge(w1_ok, h * PER_HEAD + BASE[i] + s + 1)
                stt(out=pr[:, r, 0, c], in0=pr[:, r, 0, c], scalar=fac[:, b, 0, s:s + 1], in1=pr[:, r, 1, c],
                    op0=ALU.mult, op1=ALU.add).then_inc(w_ok, 1)

            def out_row(h, i):
                dve.wait_ge(pv, h * PER_HEAD + BASE[i] + NSEG[i] + 2)
                dve.wait_ge(o_free, h * NT + i + 1)
                nc.vector.tensor_copy(o[:, i % 2, :], ops[i % 2][:, 0:P]).then_inc(o_ok, 1)

            steps = 4 * NT + NT
            def step(h, i):
                cur = NSEG[i] if i < NT else 0
                h1, i1, mid = tile_before(h, i, 1)
                h3, i3, done = tile_before(h, i, 3)
                if i == 0:
                    maps(h, 0)
                if i + 1 < NT:
                    maps(h, i + 1)
                if mid:
                    factors(h1, i1)
                if cur:
                    seg_max(h, i, 0)
                for s in range(max(cur - 1, mid)):
                    if s < mid:
                        weigh(h1, i1, s)
                    if s + 1 < cur:
                        seg_max(h, i, s + 1)
                if cur:
                    row_max(h, i)
                if done:
                    out_row(h3, i3)

            each_head(dve, step, chain, steps)
            out_row(HEADS - 1, NT - 1)

        @block.tensor
        def _(pe):
            pe.sem_inc(pv, 2)

            def scores(h, i, s):
                n = h * PER_HEAD + BASE[i] + s
                k0, kw = seg_of(i)[s]
                if s == 0:
                    pe.wait_ge(qz_ok, h * NT + i + 1)
                    if i % 4 == 0:
                        pe.wait_ge(k_in[i // 4], 16)
                pe.wait_ge(e_ok, n + 1)
                for c in range(2):
                    mm = pe.matmul(sps[(BASE[i] + s) % 2][:, c, 0:kw * P], qz[:, i % 2, c, :],
                                   k[:, k0:k0 + kw, bass.ds(h * P, P)], start=True, stop=True)
                mm.then_inc(s_ps, 1)

            def turn(h, i, s):
                n = h * PER_HEAD + BASE[i] + s
                k0, kw = seg_of(i)[s]
                pe.wait_ge(w_ok, n + 1)
                pe.wait_ge(wt_sb, n + 1)
                for b in range(kw):
                    mm = pe.transpose(tps[(BASE[i] + s) % 2][:, b * P:(b + 1) * P],
                                      pr[:, i % 4, 0, (k0 + b) * P:(k0 + b + 1) * P], ident[:, :])
                mm.then_inc(tg_ps, 1)
                if s == NSEG[i] - 1:
                    pe.wait_ge(tg_ps, n + 1)
                    pe.sem_inc(wt_tile, 1)

            def weighted(h, i, s):
                n = h * PER_HEAD + BASE[i] + s
                k0, kw = seg_of(i)[s]
                if s == 0:
                    if i % 4 == 0:
                        pe.wait_ge(v_in[i // 4], 16)
                    wait(pe, o_ok, h * NT + i - 1)
                pe.wait_ge(wt_sb, n + 3)
                for b in range(kw):
                    mm = pe.matmul(ops[i % 2][:, 0:P], wT[:, (BASE[i] + s) % 2, b * P:(b + 1) * P],
                                   v[:, k0 + b, bass.ds(h * P, P)], start=(s == 0 and b == 0),
                                   stop=(s == NSEG[i] - 1 and b == kw - 1))
                mm.then_inc(pv, 1)

            def step(h, i):
                cur = NSEG[i] if i < NT else 0
                h2, i2, old = tile_before(h, i, 2)
                for s in range(max(cur, old)):
                    if s < old:
                        turn(h2, i2, s)
                    if s < cur:
                        scores(h, i, s)
                    if 0 < s < old:
                        weighted(h2, i2, s - 1)
                if old:
                    weighted(h2, i2, old - 1)

            each_head(pe, step)


def attend_sample(nc, dr, consts):
    ident = consts["ident"]
    scale = 64 ** -0.5
    WIN = P + DEC
    with ExitStack() as ctx:
        sb = lambda n, s, d=F32: ctx.enter_context(nc.sbuf_tensor(n, s, d))
        ps = lambda n, s, d=F32: ctx.enter_context(nc.psum_tensor(n, s, d))
        sem = stage_semaphores(nc, ctx)
        q, kn, vn = sb("smp_q", [P, HW]), sb("smp_k", [P, HW]), sb("smp_v", [P, HW])
        kc, vc = sb("cache_k_sb", [P, DEC_B, HW]), sb("cache_v_sb", [P, DEC_B, HW])
        kcT = sb("cache_k_T", [P, 2, DEC_B, P])
        qw = sb("q_windows", [P, 2, DEC_B * WIN])
        qz = sb("smp_q_by_map", [P, 2, P])
        hide = sb("hide_others", [P, 2 * P])
        s_sb = sb("smp_scores", [P, 2, 2 * P])
        nM, zs, rz = sb("smp_neg_max", [P, 2]), sb("smp_sum", [P, 2]), sb("smp_factor", [P, 2])
        ww = sb("weight_windows", [P, DEC_B * WIN])
        wn = sb("new_weights_T", [P, P])
        coef = sb("smp_coef", [P, 2])
        lamv = sb("smp_lam_rows", [P, 4, 64])
        lamd = sb("smp_lam_dots", [P, 4])
        orow = sb("smp_o", [P, HW])
        kps = ps("cache_k_T_psum", [P, 2, HW])
        sps = ps("smp_score_psum", [P, 2, HW])
        tps = ps("smp_weights_T_psum", [P, HW])
        ops = ps("smp_out_psum", [P, HW])
        lam_in, new_in, kc_in, vc_in = sem("smp_lam_loaded"), sem("smp_new_loaded"), sem("cache_k_loaded"), sem("cache_v_loaded")
        step, lam_e, hide_ok = sem("p3_dve_step"), sem("smp_lam_exp"), sem("hide_ready")
        pool_step = sem("p3_pool_step")
        qz_ok, kT_ps, kT_ok, s_ps = sem("smp_q_ready"), sem("cache_k_T_in_psum"), sem("cache_k_T_ready"), sem("smp_scores_in_psum")
        m_ok, e_ok, w_ok, t_ps, t_ok = sem("smp_max_ready"), sem("smp_exp_ready"), sem("smp_weights_ready"), sem("smp_T_in_psum"), sem("smp_T_ready")
        o_ps, o_ok, o_out = sem("smp_o_in_psum"), sem("smp_o_ready"), sem("smp_o_stored")
        block = ctx.enter_context(nc.Block())

        @block.sync
        def _(sp):
            for n, name in enumerate(("lam_q1", "lam_k1", "lam_q2", "lam_k2")):
                sp.dma_start(lamv[:, n, :], dr[name].to_broadcast([P, 64])).then_inc(lam_in, 16)
            sp.dma_start(q[:, :], dr["z"][QA][NT]).then_inc(new_in, 16)
            sp.dma_start(kn[:, :], dr["z"][KT][NT]).then_inc(new_in, 16)
            sp.dma_start(vn[:, :], dr["v_sample"].rearrange("l b t h d -> (l b t) (h d)")).then_inc(new_in, 16)
            sp.dma_start(kc[:, :, :], dr["cache_k"].rearrange("l b t h d -> t (l b) (h d)")).then_inc(kc_in, 16)
            sp.dma_start(vc[:, :, :], dr["cache_v"].rearrange("l b t h d -> t (l b) (h d)")).then_inc(vc_in, 16)
            sp.wait_ge(o_ok, HEADS)
            sp.dma_start(dr["att"][NT], orow[:, :]).then_inc(o_out, 16)
            sp.wait_ge(o_out, 16)

        @block.gpsimd
        def _(pool):
            chain = Chain(pool, pool_step)
            chain.after(pool.memset(hide[:, :], 0.0))
            own = hide[:, P:2 * P].rearrange("p (b r) -> p b r", r=DEC)
            chain.after(pool.affine_select(out=own, in_=own, compare_op=ALU.is_ge, fill=HIDDEN, base=0,
                                           pattern=[[-DEC, DEC_B], [0, DEC]], channel_multiplier=1))
            pool.affine_select(out=own, in_=own, compare_op=ALU.is_ge, fill=HIDDEN, base=DEC - 1,
                               pattern=[[DEC, DEC_B], [0, DEC]], channel_multiplier=-1).then_inc(hide_ok, 1)

        @block.scalar
        def _(act):
            act.wait_ge(lam_e, 1)
            nc.scalar.activation(lamd[:, 0:2], lamd[:, 2:4], ACT.Exp).then_inc(lam_e, 1)
            for h in range(HEADS):
                act.wait_ge(kT_ps, h + 1)
                nc.scalar.copy(kcT[:, h % 2, :, :].rearrange("p b t -> p (b t)"),
                               kps[:, :, :].rearrange("p a n -> p (a n)")).then_inc(kT_ok, 1)
                act.wait_ge(m_ok, h + 1)
                for c in range(2):
                    ins = nc.scalar.activation(s_sb[:, c, :], s_sb[:, c, :], ACT.Exp, bias=nM[:, c:c + 1], accum_out=zs[:, c:c + 1])
                ins.then_inc(e_ok, 1)

        @block.vector
        def _(dve):
            chain = Chain(dve, step)
            tt, ts, stt = nc.vector.tensor_tensor, nc.vector.tensor_scalar, nc.vector.scalar_tensor_tensor
            red = nc.vector.tensor_reduce
            dve.wait_ge(lam_in, 64)
            chain.after(tt(lamv[:, 0:4:2, :], lamv[:, 0:4:2, :], lamv[:, 1:4:2, :], ALU.mult))
            red(lamd[:, 2:4], lamv[:, 0:4:2, :], AX.X, ALU.add).then_inc(lam_e, 1)
            nc.vector.memset(coef[:, :], 1.0)
            nc.vector.memset(ww[:, :], 0.0)
            nc.vector.memset(qz[:, :, :], 0.0)
            chain.after(nc.vector.memset(qw[:, :, :], 0.0))
            dve.wait_ge(lam_e, 2)
            tt(coef[:, 1:2], lamd[:, 1:2], lamd[:, 0:1], ALU.subtract).then_inc(lam_e, 1)
            dve.wait_ge(lam_e, 3)
            chain.after(ts(coef[:, 1:2], coef[:, 1:2], -LAM_INIT, None, ALU.add))
            dve.wait_ge(new_in, 48)
            dve.wait_ge(hide_ok, 1)
            for h in range(HEADS):
                hc = slice(h * P, (h + 1) * P)
                wait(dve, s_ps, h)
                for c in range(2):
                    r = slice(64 * c, 64 * c + 64)
                    ts(qz[r, c, :], q[r, hc], scale, None, ALU.mult)
                    own = qw[r, c, :].rearrange("p (b r) -> p b r", r=WIN)[:, :, 0:DEC]
                    ins = ts(own, q[r, hc].rearrange("p (b r) -> p b r", r=DEC), scale, None, ALU.mult)
                ins.then_inc(qz_ok, 1)
                dve.wait_ge(s_ps, h + 1)
                for c in range(2):
                    ins = tt(s_sb[:, c, :], sps[:, c, 0:2 * P], hide[:, :], ALU.add)
                chain.after(ins)
                red(nM[:, :], s_sb[:, :, :], AX.X, ALU.max, negate=True).then_inc(m_ok, 1)
                dve.wait_ge(e_ok, h + 1)
                chain.after(nc.vector.reciprocal(rz[:, :], zs[:, :]))
                chain.after(tt(rz[:, :], rz[:, :], coef[:, :], ALU.mult))
                chain.after(ts(s_sb[:, 1, :], s_sb[:, 1, :], rz[:, 1:2], None, ALU.mult))
                stt(out=s_sb[:, 0, :], in0=s_sb[:, 0, :], scalar=rz[:, 0:1], in1=s_sb[:, 1, :], op0=ALU.mult,
                    op1=ALU.add).then_inc(w_ok, 1)
                dve.wait_ge(t_ps, h + 1)
                nc.vector.tensor_copy(ww[:, :].rearrange("p (b r) -> p b r", r=WIN)[:, :, 0:DEC],
                                      tps[:, 0:P].rearrange("p (b r) -> p b r", r=DEC))
                nc.vector.tensor_copy(wn[:, :], tps[:, P:2 * P]).then_inc(t_ok, 1)
                dve.wait_ge(o_ps, h + 1)
                nc.vector.tensor_copy(orow[:, hc], ops[:, hc]).then_inc(o_ok, 1)

        @block.tensor
        def _(pe):
            pe.wait_ge(kc_in, 16)
            for h in range(HEADS):
                hc = slice(h * P, (h + 1) * P)
                wait(pe, kT_ok, h)
                for b in range(DEC_B):
                    mm = pe.transpose(kps[:, b // 4, (b % 4) * P:(b % 4 + 1) * P], kc[:, b, hc], ident[:, :])
                mm.then_inc(kT_ps, 1)
                pe.wait_ge(kT_ok, h + 1)
                pe.wait_ge(qz_ok, h + 1)
                pe.wait_ge(new_in, 48)
                wait(pe, m_ok, h)
                for c in range(2):
                    for b in range(DEC_B):
                        pe.matmul(sps[:, c, 0:P], qw[:, c, b * P:(b + 1) * P], kcT[:, h % 2, b, :],
                                  start=(b == 0), stop=(b == DEC_B - 1))
                    mm = pe.matmul(sps[:, c, P:2 * P], qz[:, c, :], kn[:, hc], start=True, stop=True)
                mm.then_inc(s_ps, 1)
                pe.wait_ge(w_ok, h + 1)
                for b in range(2):
                    mm = pe.transpose(tps[:, b * P:(b + 1) * P], s_sb[:, 0, b * P:(b + 1) * P], ident[:, :])
                mm.then_inc(t_ps, 1)
                pe.wait_ge(t_ok, h + 1)
                pe.wait_ge(vc_in, 16)
                for b in range(DEC_B):
                    pe.matmul(ops[:, hc], ww[:, b * P:(b + 1) * P], vc[:, b, hc], start=(b == 0), stop=False)
                mm = pe.matmul(ops[:, hc], wn[:, :], vn[:, hc], start=False, stop=True)
                mm.then_inc(o_ps, 1)


def mix_and_route(nc, dr, consts, keep):
    ident = consts["ident"]
    y, gates, work, trips = keep["y"], keep["gates"], keep["work"], keep["trips"]
    slot_all, tok_all = keep["slot_all"], keep["tok_all"]
    with ExitStack() as ctx:
        sb = lambda n, s, d=F32: ctx.enter_context(nc.sbuf_tensor(n, s, d))
        ps = lambda n, s, d=F32: ctx.enter_context(nc.psum_tensor(n, s, d))
        sem = stage_semaphores(nc, ctx)
        wo = sb("w_out_sb", [P, DC, D])
        wr = sb("w_router_sb", [P, DC, LOGITS])
        n2 = sb("norm2_row", [P, D])
        sub = sb("subln_row", [P, P])
        m = sb("mix", [P, 2, D])
        x = sb("x_res", [P, 2, D])
        mT = sb("mix_T", [P, 2, DC, P])
        h = sb("h2", [P, 2, D])
        hT = sb("h2_T", [P, DC, P])
        junk = sb("square_out4", [P, D], BF16)
        ast = sb("att_stats", [P, 2, 12])
        st = sb("norm2_stats", [P, 4])
        zero = sb("zero_rows", [PAD_ROWS, D])
        glog = sb("group_logits", [P, 8])
        elog = sb("expert_logits", [P, N_EXP])
        elm = sb("masked_logits", [P, N_EXP])
        gtop, etop = sb("group_top", [P, 8]), sb("expert_top", [P, 8])
        gidx, eidx = sb("group_index", [P, 8], U32), sb("expert_index", [P, 8], U32)
        sel = sb("selected", [P, 4])
        rt = sb("route_tmp", [P, 8])
        oh = sb("one_hot", [P, 2, 2, N_EXP])
        both = sb("both_hot", [P, 2, N_EXP])
        place = sb("place", [P, N_EXP])
        hit = sb("hit", [P, 2, N_EXP])
        pos = sb("position", [P, 2])
        posi = sb("position_index", [P, 2, 2], U32)
        cnt = sb("expert_count", [P, N_EXP])
        slot = sb("slot_number", [P, TILES, 2], U32)
        init = sb("table_init", [109, 5, P], U32)
        e_of = sb("expert_row", [P, N_EXP])
        g_of = sb("group_row", [P, N_EXP])
        q_of = sb("queue_start_row", [P, N_EXP])
        tri = sb("earlier_tokens", [P, P])
        ones = sb("ones", [P, P])
        full = sb("entry_there", [P, N_EXP, TILES])
        rank = sb("entry_rank", [P, N_EXP * TILES])
        en_of = sb("entry_number", [P, N_EXP * TILES])
        ee_of = sb("entry_expert", [P, N_EXP, TILES])
        th_of = sb("entry_start", [P, TILES])
        one_row = sb("one_row", [P, N_EXP * TILES])
        me = sb("list_place", [P, 1])
        lst = sb("block_list", [P, 4])
        blk_at = sb("block_queue_row", [P, 1], U32)
        blk_rows = sb("block_queue_rows", [P, P], U32)
        blk = sb("block_queue_floats", [P, P])

        mps = ps("mix_T_psum", [P, 2, HW])
        yps = ps("y_psum", [P, 2, HW])
        hps = ps("h2_T_psum", [P, 2, HW])
        lps = ps("logit_psum", [P, HW])
        rps = ps("rank_psum", [P, 2, N_EXP])

        wo_in, rows_in = sem("w_out_loaded"), sem("stage4_rows_loaded")
        m_in = [sem(f"mix_loaded{u}") for u in range(2)]
        x_in = [sem(f"residual_loaded{u}") for u in range(2)]
        act_step, dve_step, pool_step = sem("p4_act_step"), sem("p4_dve_step"), sem("p4_pool_step")
        iota_ok, tab_out = sem("route_consts_ready"), sem("table_initialised")
        ar_ok, mix_ok, mT_ps, mT_act, mT_dve = sem("att_rstd"), sem("mix_ready"), sem("mix_T_in_psum"), sem("mix_T_half0"), sem("mix_T_half1")
        y_ps, y_ok, r_ok, h_ok, h_free, h_out = sem("y_in_psum"), sem("y_ready"), sem("norm2_rstd"), sem("h2_ready"), sem("h2_free"), sem("h2_stored")
        hT_ps, hT_act, hT_dve, lg_ps = sem("h2_T_in_psum"), sem("h2_T_half0"), sem("h2_T_half1"), sem("logits_in_psum")
        gm_ok, ge_ok, ev_ok, ee_ok = sem("group_max"), sem("group_exp"), sem("expert_top2"), sem("gate_exp")
        both_ok, rk_ps, pos_ok, sc_free = sem("one_hots_ready"), sem("ranks_in_psum"), sem("positions_ready"), sem("positions_free")
        sc_out = sem("table_scattered")
        stand, pool_stand = sem("dve_stand"), sem("pool_stand")
        blk_in, blk_ok, blk_ps = sem("block_rows_loaded"), sem("block_rows_as_floats"), sem("block_rows_in_psum")
        lst_ok, lst_ps, zero_ok = sem("list_ready"), sem("list_in_psum"), sem("zero_rows_ready")
        block = ctx.enter_context(nc.Block())
        xp = dr["x_prompt"].rearrange("b (t p) d -> (b t) p d", p=P)
        h2 = dr["h2"][0:TILES * P].rearrange("(t p) d -> t p d", p=P)
        STEPS = TILES + 2

        def steps(eng, step, chain=None, per_step=0, last=NT):
            step(0, 0)
            step(1, 1)
            with eng.Fori(1, last // 2) as i:
                if chain:
                    chain.loop(i - 1, 2 * per_step)
                for u in range(2):
                    step(i * 2 + u, u)
            if chain:
                chain.end_loop(last // 2 - 1)
            for t in range(last, STEPS):
                step(t, t % 2)

        def there(t):
            return not isinstance(t, int) or 0 <= t < TILES

        @block.sync
        def _(sp):
            sp.sem_inc(h_free, 2)

            def load_mix(t, u):
                wait(sp, mT_ps, t - 1)
                sp.dma_start(m[:, u, 0:HW], row(dr["att"], t)).then_inc(m_in[u], 16)
                sp.dma_start(m[:, u, HW:D], row(dr["rec"], t)).then_inc(m_in[u], 16)

            def load_x(t, u):
                wait(sp, y_ok, 2 * t - 2)
                src = dr["x_sample"].rearrange("b t d -> (b t) d") if isinstance(t, int) and t == NT else row(xp, t)
                sp.dma_start(x[:, u, :], src).then_inc(x_in[u], 16)

            def step(t, u):
                if isinstance(t, int) and t == 0:
                    load_mix(0, 0)
                    load_mix(1, 1)
                    sp.dma_start(sub[:, :], dr["subln_w"].to_broadcast([P, P])).then_inc(rows_in, 16)
                    sp.dma_start(wo[:, :, :], dr["w_out"].rearrange("l (c p) n -> p (l c) n", p=P)).then_inc(wo_in, 16)
                    sp.dma_start(n2[:, :], dr["norm2_w"].to_broadcast([P, D])).then_inc(rows_in, 16)
                    sp.dma_start(wr[:, :, 0:N_GRP], dr["w_group"].rearrange("l (c p) n -> p (l c) n", p=P)).then_inc(rows_in, 16)
                    sp.dma_start(wr[:, :, N_GRP:LOGITS], dr["w_router"].rearrange("l (c p) n -> p (l c) n", p=P)).then_inc(rows_in, 16)
                    load_x(0, 0)
                if there(t + 2):
                    load_mix(t + 2, u)
                if there(t + 1):
                    load_x(t + 1, 1 - u)
                if there(t - 1):
                    sp.wait_ge(h_ok, t)
                    sp.dma_start(row(h2, t - 1), h[:, 1 - u, :]).then_inc(h_out, 16)
                    sp.wait_ge(h_out, 16 * t)
                    sp.sem_inc(h_free, 1)

            with nc.allow_non_contiguous_dma(reason="router columns are short rows"):
                steps(sp, step, last=NT - 2)
            sp.wait_ge(zero_ok, 1)
            sp.dma_start(dr["h2"][TILES * P:TILES * P + PAD_ROWS], zero[:, :]).then_inc(h_out, 16)
            sp.wait_ge(h_out, 16 * (TILES + 1))

        @block.gpsimd
        def _(pool):
            chain = Chain(pool, pool_step)
            kw = dict(allow_small_or_imprecise_dtypes=True)
            chain.after(pool.iota(init[:, :, :], [[0, 5], [1, P]], base=2 * TILES * P, channel_multiplier=0))
            pool.dma_start(dr["table"].rearrange("(a b) r o -> a (b r o)", b=5), init[:, :, :].rearrange("a b r -> a (b r)")).then_inc(tab_out, 16)
            pool.iota(slot[:, :, :], [[2 * P, TILES], [1, 2]], base=0, channel_multiplier=2)
            pool.iota(e_of[:, :], [[1, N_EXP]], base=0, channel_multiplier=0, **kw)
            pool.iota(g_of[:, :], [[1, N_GRP], [0, N_EXP // N_GRP]], base=0, channel_multiplier=0, **kw)
            pool.iota(q_of[:, :], [[QUEUE, N_EXP]], base=0, channel_multiplier=0, **kw)
            pool.iota(en_of[:, :], [[1, N_EXP * TILES]], base=0, channel_multiplier=0, **kw)
            pool.iota(ee_of[:, :, :], [[1, N_EXP], [0, TILES]], base=0, channel_multiplier=0, **kw)
            pool.iota(th_of[:, :], [[P, TILES]], base=0, channel_multiplier=0, **kw)
            pool.iota(me[:, :], [[0, 1]], base=1, channel_multiplier=1, **kw)
            pool.memset(one_row[:, :], 1.0)
            pool.memset(cnt[:, :], 0.0)
            pool.memset(glog[:, :], 4 * HIDDEN)
            pool.memset(zero[:, :], 0.0).then_inc(zero_ok, 1)
            pool.memset(ones[:, :], 1.0)
            chain.after(pool.memset(tri[:, :], 1.0))
            pool.affine_select(out=tri[:, :], in_=tri[:, :], compare_op=ALU.is_gt, fill=0.0, base=0,
                               pattern=[[1, P]], channel_multiplier=-1).then_inc(iota_ok, 1)
            pool.sem_inc(sc_free, 2)
            pool.wait_ge(tab_out, 16)

            def step(t, u):
                if there(t - 2):
                    pool.wait_ge(pos_ok, t)
                    pool.sem_inc(pool_stand, 1)
                    for c in range(2):
                        pool.indirect_dma_start(
                            out=dr["table"].rearrange("a r o -> (a r) o"),
                            out_offset=bass.IndirectOffsetOnAxis(ap=posi[:, u, c:c + 1], axis=0),
                            in_=slot_now[:, u, c:c + 1], in_offset=None).then_inc(sc_out, 16)
                    pool.wait_ge(sc_out, 32 * (t - 1))
                    pool.sem_inc(sc_free, 1)

            slot_now = posi[:, :, :]
            slot_now = keep["slot_now"]
            steps(pool, step)
            pool.wait_ge(lst_ok, 1)
            pool.indirect_dma_start(out=blk_rows[:, :], out_offset=None, in_=dr["table"].rearrange("a r o -> a (r o)"),
                                    in_offset=bass.IndirectOffsetOnAxis(ap=blk_at[:, :], axis=0)).then_inc(blk_in, 16)

        @block.scalar
        def _(act):
            chain = Chain(act, act_step)
            eps = consts["eps"][:, 0:1]

            def att_stats(t, u):
                act.wait_ge(m_in[u], 32 * (t // 2) + 32 if isinstance(t, int) else (t - u) * 16 + 32)
                wait(act, mix_ok, t - 1)
                for hd in range(HEADS):
                    chain.after(nc.scalar.activation(junk[:, 0:P], m[:, u, hd * P:(hd + 1) * P], ACT.Square,
                                                     accum_out=ast[:, u, hd:hd + 1]))
                chain.after(nc.scalar.activation(ast[:, u, 4:8], ast[:, u, 0:4], ACT.Ln, scale=1.0 / P, bias=eps))
                nc.scalar.activation(ast[:, u, 8:12], ast[:, u, 4:8], ACT.Exp, scale=-0.5).then_inc(ar_ok, 1)

            def copy_mT(t, u):
                act.wait_ge(mT_ps, t + 1)
                nc.scalar.copy(mT[:, u, 0:4, :].rearrange("p c t -> p (c t)"), mps[:, 0, :]).then_inc(mT_act, 1)

            def step(t, u):
                if there(t - 1):
                    act.wait_ge(y_ok, 2 * t)
                    wait(act, h_ok, t - 1)
                    chain.after(nc.scalar.activation(junk[:, :], y[:, bass.ds(t - 1, 1), :].rearrange("p o d -> p (o d)"),
                                                     ACT.Square, accum_out=st[:, 0:1]))
                    chain.after(nc.scalar.activation(st[:, 1:2], st[:, 0:1], ACT.Ln, scale=1.0 / D, bias=eps))
                    nc.scalar.activation(st[:, 2:3], st[:, 1:2], ACT.Exp, scale=-0.5).then_inc(r_ok, 1)
                if there(t - 2):
                    act.wait_ge(gm_ok, t - 1)
                    nc.scalar.activation(rt[:, 4:8], glog[:, 0:4], ACT.Exp, bias=rt[:, 0:1], accum_out=rt[:, 1:2]).then_inc(ge_ok, 1)
                    act.wait_ge(ev_ok, t - 1)
                    nc.scalar.activation(rt[:, 3:4], rt[:, 2:3], ACT.Exp).then_inc(ee_ok, 1)
                if there(t - 1):
                    act.wait_ge(hT_ps, t)
                    nc.scalar.copy(hT[:, 0:4, :].rearrange("p c t -> p (c t)"), hps[:, 0, :]).then_inc(hT_act, 1)
                if there(t + 1):
                    copy_mT(t + 1, 1 - u)
                if there(t + 2):
                    att_stats(t + 2, u)

            act.wait_ge(consts["sem"], consts["n"])
            att_stats(0, 0)
            att_stats(1, 1)
            copy_mT(0, 0)
            steps(act, step, chain, 7, last=NT - 2)

        @block.vector
        def _(dve):
            chain = Chain(dve, dve_step)
            tt, ts, stt = nc.vector.tensor_tensor, nc.vector.tensor_scalar, nc.vector.scalar_tensor_tensor
            red, cp = nc.vector.tensor_reduce, nc.vector.tensor_copy

            def mix(t, u):
                dve.wait_ge(ar_ok, t + 1)
                for hd in range(HEADS):
                    c = slice(hd * P, (hd + 1) * P)
                    ins = stt(out=m[:, u, c], in0=m[:, u, c], scalar=ast[:, u, 8 + hd:9 + hd], in1=sub[:, :], op0=ALU.mult, op1=ALU.mult)
                ins.then_inc(mix_ok, 1)

            def norm(t, u):
                dve.wait_ge(r_ok, t + 1)
                dve.wait_ge(h_free, t + 1)
                wait(dve, hT_ps, t)
                stt(out=h[:, u, :], in0=y[:, bass.ds(t, 1), :].rearrange("p o d -> p (o d)"), scalar=st[:, 2:3], in1=n2[:, :],
                    op0=ALU.mult, op1=ALU.mult).then_inc(h_ok, 1)

            def residual(t, u, half):
                c = slice(half * HW, (half + 1) * HW)
                dve.wait_ge(x_in[u], 16 * (t // 2) + 16 if isinstance(t, int) else (t - u) * 8 + 16)
                dve.wait_ge(y_ps, 2 * t + half + 1)
                tt(y[:, bass.ds(t, 1), c].rearrange("p o n -> p (o n)"), yps[:, half, :], x[:, u, c], ALU.add).then_inc(y_ok, 1)

            def copy_mT(t, u):
                dve.wait_ge(mT_ps, t + 1)
                cp(mT[:, u, 4:8, :].rearrange("p c t -> p (c t)"), mps[:, 1, :]).then_inc(mT_dve, 1)

            def route(t, u):
                dve.wait_ge(lg_ps, t + 1)
                cp(glog[:, 0:N_GRP], lps[:, 0:N_GRP])
                chain.after(cp(elog[:, :], lps[:, N_GRP:LOGITS]))
                dve.sem_inc(stand, 1)
                chain.after(nc.vector.max(gtop[:, :], glog[:, :]))
                ts(rt[:, 0:1], gtop[:, 0:1], -1.0, None, ALU.mult).then_inc(gm_ok, 1)
                chain.after(nc.vector.max_index(gidx[:, :], gtop[:, :], glog[:, :]))
                chain.after(cp(sel[:, 0:1], gidx[:, 0:1]))
                chain.after(ts(place[:, :], g_of[:, :], sel[:, 0:1], None, ALU.is_equal))
                tt(elog[:, :], elog[:, :], place[:, :], ALU.mult)
                chain.after(ts(elm[:, :], place[:, :], -1.0, -HIDDEN, ALU.add, ALU.mult))
                chain.after(tt(elm[:, :], elog[:, :], elm[:, :], ALU.add))
                dve.sem_inc(stand, 1)
                chain.after(nc.vector.max(etop[:, :], elm[:, :]))
                tt(rt[:, 2:3], etop[:, 1:2], etop[:, 0:1], ALU.subtract).then_inc(ev_ok, 1)
                chain.after(nc.vector.max_index(eidx[:, :], etop[:, :], elm[:, :]))
                chain.after(cp(sel[:, 2:4], eidx[:, 0:2]))
                for c in range(2):
                    ins = ts(oh[:, u, c, :], e_of[:, :], sel[:, 2 + c:3 + c], None, ALU.is_equal)
                chain.after(ins)
                tt(both[:, u, :], oh[:, u, 0, :], oh[:, u, 1, :], ALU.add).then_inc(both_ok, 1)

            def gate(t):
                dve.wait_ge(ge_ok, t + 1)
                dve.wait_ge(ee_ok, t + 1)
                chain.after(ts(sel[:, 0:1], rt[:, 3:4], 1.0, rt[:, 1:2], ALU.add, ALU.mult))
                g = gates[:, bass.ds(t, 1), :].rearrange("p o c -> p (o c)")
                chain.after(nc.vector.reciprocal(g[:, 0:1], sel[:, 0:1]))
                chain.after(tt(g[:, 1:2], g[:, 0:1], rt[:, 3:4], ALU.mult))

            def positions(t, u):
                dve.wait_ge(rk_ps, t + 1)
                dve.wait_ge(sc_free, t + 1)
                chain.after(tt(place[:, :], rps[:, 0, :], cnt[:, :], ALU.add))
                chain.after(tt(place[:, :], place[:, :], q_of[:, :], ALU.add))
                chain.after(tt(cnt[:, :], rps[:, 1, :], cnt[:, :], ALU.add))
                for c in range(2):
                    ins = tt(hit[:, c, :], oh[:, u, c, :], place[:, :], ALU.mult)
                chain.after(ins)
                chain.after(red(pos[:, :], hit[:, :, :], AX.X, ALU.add))
                cp(posi[:, u, :], pos[:, :])
                cp(slot_now[:, u, :], slot[:, bass.ds(t, 1), :].rearrange("p o c -> p (o c)")).then_inc(pos_ok, 1)

            slot_now = keep["slot_now"]

            def step(t, u):
                if there(t - 1):
                    residual(t - 1, 1 - u, 1)
                if there(t + 1):
                    mix(t + 1, 1 - u)
                if there(t - 2):
                    route(t - 2, u)
                if there(t - 1):
                    norm(t - 1, 1 - u)
                if there(t - 2):
                    gate(t - 2)
                if there(t - 1):
                    dve.wait_ge(hT_ps, t)
                    cp(hT[:, 4:8, :].rearrange("p c t -> p (c t)"), hps[:, 1, :]).then_inc(hT_dve, 1)
                if there(t + 1):
                    copy_mT(t + 1, 1 - u)
                if there(t):
                    residual(t, u, 0)
                if there(t - 2):
                    positions(t - 2, u)

            dve.wait_ge(rows_in, 64)
            dve.wait_ge(iota_ok, 1)
            dve.sem_inc(pos_ok, 1)
            chain.after(ts(sub[:, :], sub[:, :], 1.0 - LAM_INIT, None, ALU.mult))
            mix(0, 0)
            copy_mT(0, 0)
            steps(dve, step, chain, 19)
            chain.after(tt(full[:, :, :], cnt[:, :, None].to_broadcast([P, N_EXP, TILES]),
                           th_of[:, None, :].to_broadcast([P, N_EXP, TILES]), ALU.is_gt))
            fl = full[:, :, :].rearrange("p e j -> p (e j)")
            chain.after(nc.vector.tensor_tensor_scan(rank[:, :], one_row[:, :], fl, 0.0, ALU.mult, ALU.add))
            chain.after(cp(lst[:, 2:3], rank[:, N_EXP * TILES - 1:N_EXP * TILES]))
            chain.after(tt(rank[:, :], rank[:, :], fl, ALU.mult))
            chain.after(ts(rank[:, :], rank[:, :], me[:, 0:1], None, ALU.is_equal))
            chain.after(tt(one_row[:, :], rank[:, :], en_of[:, :], ALU.mult))
            chain.after(red(lst[:, 0:1], one_row[:, :], AX.X, ALU.add))
            chain.after(tt(one_row[:, :], rank[:, :], ee_of[:, :, :].rearrange("p e j -> p (e j)"), ALU.mult))
            chain.after(red(lst[:, 1:2], one_row[:, :], AX.X, ALU.add))
            chain.after(ts(lst[:, 3:4], me[:, :], lst[:, 2:3], float(N_EXP * TILES), ALU.is_gt, ALU.mult))
            chain.after(tt(lst[:, 0:1], lst[:, 0:1], lst[:, 3:4], ALU.add))
            chain.after(ts(lst[:, 2:3], lst[:, 2:3], 0.5, -0.25, ALU.mult, ALU.add))
            cp(blk_at[:, :], lst[:, 0:1]).then_inc(lst_ok, 1)
            dve.wait_ge(lst_ps, 1)
            cp(work[:, :], lps[0:1, 0:P])
            chain.after(cp(trips[:, :], lps[0:1, P:P + 1]))
            dve.wait_ge(blk_in, 16)
            cp(blk[:, :], blk_rows[:, :]).then_inc(blk_ok, 1)
            dve.wait_ge(blk_ps, 1)
            chain.after(cp(slot_all[:, :], lps[:, 2 * P:3 * P]))
            ts(tok_all[:, :], slot_all[:, :], 0.5, -0.25, ALU.mult, ALU.add)

        @block.tensor
        def _(pe):
            def turn_mix(t, u):
                pe.wait_ge(mix_ok, t + 1)
                wait(pe, mT_act, t)
                wait(pe, mT_dve, t)
                for c in range(DC):
                    mm = pe.transpose(mps[:, c // 4, (c % 4) * P:(c % 4 + 1) * P], m[:, u, c * P:(c + 1) * P], ident[:, :])
                mm.then_inc(mT_ps, 1)

            def project_out(t, u, half):
                pe.wait_ge(mT_act, t + 1)
                pe.wait_ge(mT_dve, t + 1)
                wait(pe, y_ok, 2 * t - 1 + half)
                if isinstance(t, int) and t == 0:
                    pe.wait_ge(wo_in, 16)
                for c in range(DC):
                    mm = pe.matmul(yps[:, half, :], mT[:, u, c, :], wo[:, c, half * HW:(half + 1) * HW],
                                   start=(c == 0), stop=(c == DC - 1))
                mm.then_inc(y_ps, 1)

            def turn_h(t, u):
                pe.wait_ge(h_ok, t + 1)
                wait(pe, hT_act, t)
                wait(pe, hT_dve, t)
                for c in range(DC):
                    mm = pe.transpose(hps[:, c // 4, (c % 4) * P:(c % 4 + 1) * P], h[:, u, c * P:(c + 1) * P], ident[:, :])
                mm.then_inc(hT_ps, 1)

            def logits(t, u):
                pe.wait_ge(hT_act, t + 1)
                pe.wait_ge(hT_dve, t + 1)
                wait(pe, both_ok, t)
                for c in range(DC):
                    mm = pe.matmul(lps[:, 0:LOGITS], hT[:, c, :], wr[:, c, :], start=(c == 0), stop=(c == DC - 1))
                mm.then_inc(lg_ps, 1)

            def ranks(t, u):
                pe.wait_ge(both_ok, t + 1)
                pe.wait_ge(pos_ok, t + 1)
                pe.matmul(rps[:, 0, :], tri[:, :], both[:, u, :], start=True, stop=True)
                pe.matmul(rps[:, 1, :], ones[:, :], both[:, u, :], start=True, stop=True).then_inc(rk_ps, 1)

            def step(t, u):
                if there(t):
                    project_out(t, u, 0)
                if there(t - 1):
                    turn_h(t - 1, 1 - u)
                if there(t + 1):
                    turn_mix(t + 1, 1 - u)
                if there(t - 2):
                    ranks(t - 2, u)
                if there(t):
                    project_out(t, u, 1)
                if there(t - 1):
                    logits(t - 1, 1 - u)

            pe.wait_ge(rows_in, 64)
            pe.wait_ge(iota_ok, 1)
            turn_mix(0, 0)
            steps(pe, step)
            pe.wait_ge(lst_ok, 1)
            for c in range(2):
                mm = pe.matmul(lps[0:1, c * P:(c + 1) * P], lst[:, c + 1:c + 2], ident[:, :], start=True, stop=True)
            mm.then_inc(lst_ps, 1)
            pe.wait_ge(blk_ok, 1)
            pe.transpose(lps[:, 2 * P:3 * P], blk[:, :], ident[:, :]).then_inc(blk_ps, 1)


def experts(nc, dr, consts, keep):
    ident = consts["ident"]
    work, trips, slot_all, tok_all = keep["work"], keep["trips"], keep["slot_all"], keep["tok_all"]
    FC = D_EXP // P
    with ExitStack() as ctx:
        sb = lambda n, s, d=F32: ctx.enter_context(nc.sbuf_tensor(n, s, d))
        ps = lambda n, s, d=F32: ctx.enter_context(nc.psum_tensor(n, s, d))
        sem = stage_semaphores(nc, ctx)
        wg, wu = sb("w_gate_sb", [P, 2, DC, D_EXP]), sb("w_up_sb", [P, 2, DC, D_EXP])
        wd = sb("w_down_sb", [P, 2, FC, D])
        slots = sb("block_slots", [P, 2], U32)
        toks = sb("block_tokens", [P, 2], U32)
        xg = sb("block_rows", [P, 2, D])
        xT = sb("block_rows_T", [P, 2, DC, P])
        sg = sb("silu_gate", [P, D_EXP])
        a = sb("hidden", [P, D_EXP])
        aT = sb("hidden_T", [P, 2, FC, P])
        out = sb("block_out", [P, 2, D])
        xps = ps("block_rows_T_psum", [P, 2, HW])
        gps, ups = ps("gate_psum", [P, D_EXP]), ps("up_psum", [P, D_EXP])
        aps = ps("hidden_T_psum", [P, HW])
        dps = ps("down_psum", [P, 2, HW])
        g_in, u_in, d_in = ([sem(f"w_{n}_loaded{u}") for u in range(2)] for n in ("gate", "up", "down"))
        slot_ok, x_in, o_out = sem("slots_ready"), [sem(f"rows_gathered{u}") for u in range(2)], sem("rows_scattered")
        tok_ok, x_ps, x_act, x_dve = sem("tokens_ready"), sem("rows_T_in_psum"), sem("rows_T_half0"), sem("rows_T_half1")
        g_ps, u_ps, eg_ok, a_ok = sem("gate_in_psum"), sem("up_in_psum"), sem("gate_exp_ready"), sem("hidden_ready")
        a_ps, aT_ok, d_ps, d_act, d_dve = (sem("hidden_T_in_psum"), sem("hidden_T_ready"), sem("down_in_psum"),
                                           sem("out_half0"), sem("out_half1"))
        step_ = sem("p5_dve_step")
        stand = sem("p5_pool_stand")
        block = ctx.enter_context(nc.Block())
        MAXT = (N_BLOCKS - 1) // 2

        def load(eng, src, lo, hi):
            return eng.value_load(src, min_val=lo, max_val=hi)

        @block.sync
        def _(sp):
            n = load(sp, trips[0:1, 0:1], 1, MAXT)
            wgv = dr["w_e_gate"].rearrange("l e (c p) f -> (l e) p c f", p=P)
            wuv = dr["w_e_up"].rearrange("l e (c p) f -> (l e) p c f", p=P)
            wdv = dr["w_e_down"].rearrange("l e (c p) d -> (l e) p c d", p=P)

            def gate_up(b, u):
                e = load(sp, work[0:1, bass.ds(b, 1)], 0, N_EXP - 1)
                wait(sp, u_ps, b - 1)
                for v, w, arrived in ((wgv, wg, g_in), (wuv, wu, u_in)):
                    sp.dma_start(w[:, u, :, :], v[bass.ds(e, 1)].rearrange("o p c n -> (o p) c n")).then_inc(arrived[u], 16)

            def down(b, u):
                e = load(sp, work[0:1, bass.ds(b, 1)], 0, N_EXP - 1)
                wait(sp, d_ps, b)
                sp.dma_start(wd[:, u, :, :], wdv[bass.ds(e, 1)].rearrange("o p c n -> (o p) c n")).then_inc(d_in[u], 16)

            gate_up(0, 0)
            down(0, 0)
            gate_up(1, 1)
            down(1, 1)
            gate_up(2, 0)
            with sp.Fori(1, n) as i:
                down(i * 2, 0)
                gate_up(i * 2 + 1, 1)
                down(i * 2 + 1, 1)
                gate_up(i * 2 + 2, 0)
            down(n * 2, 0)

        @block.gpsimd
        def _(pool):
            n = load(pool, trips[0:1, 0:1], 1, MAXT)
            col = lambda ap, b: ap[:, bass.ds(b, 1)]

            def gather(b, u):
                wait(pool, x_ps, b - 1)
                pool.tensor_copy(toks[:, u:u + 1], col(tok_all, b)).then_inc(tok_ok, 1)
                pool.wait_ge(tok_ok, b + 1)
                pool.sem_inc(stand, 1)
                pool.indirect_dma_start(out=xg[:, u, :], out_offset=None, in_=dr["h2"],
                                        in_offset=bass.IndirectOffsetOnAxis(ap=toks[:, u:u + 1], axis=0)).then_inc(x_in[u], 16)

            def scatter(b, u):
                wait(pool, o_out, 16 * b)
                pool.tensor_copy(slots[:, u:u + 1], col(slot_all, b)).then_inc(slot_ok, 1)
                pool.wait_ge(slot_ok, b + 1)
                pool.wait_ge(d_act, b + 1)
                pool.wait_ge(d_dve, b + 1)
                pool.sem_inc(stand, 1)
                pool.indirect_dma_start(out=dr["moe"], out_offset=bass.IndirectOffsetOnAxis(ap=slots[:, u:u + 1], axis=0),
                                        in_=out[:, u, :], in_offset=None).then_inc(o_out, 16)

            gather(0, 0)
            gather(1, 1)
            gather(2, 0)
            scatter(0, 0)
            gather(3, 1)
            scatter(1, 1)
            with pool.Fori(1, n) as i:
                gather(i * 2 + 2, 0)
                scatter(i * 2, 0)
                gather(i * 2 + 3, 1)
                scatter(i * 2 + 1, 1)
            scatter(n * 2, 0)
            pool.wait_ge(x_in[1], n * 16 + 16)
            pool.wait_ge(o_out, n * 32 + 16)

        @block.scalar
        def _(act):
            n = load(act, trips[0:1, 0:1], 1, MAXT)

            def copy_x(b, u):
                act.wait_ge(x_ps, b + 1)
                nc.scalar.copy(xT[:, u, 0:4, :].rearrange("p c t -> p (c t)"), xps[:, 0, :]).then_inc(x_act, 1)

            def gate(b):
                act.wait_ge(g_ps, b + 1)
                wait(act, a_ok, b)
                nc.scalar.activation(sg[:, :], gps[:, :], ACT.Exp, scale=-1.0).then_inc(eg_ok, 1)

            def copy_a(b, u):
                act.wait_ge(a_ps, b + 1)
                nc.scalar.copy(aT[:, u, :, :].rearrange("p c t -> p (c t)"), aps[:, :]).then_inc(aT_ok, 1)

            def copy_out(b, u):
                act.wait_ge(d_ps, b + 2)
                wait(act, o_out, 16 * b)
                nc.scalar.copy(out[:, u, 0:HW], dps[:, 0, :]).then_inc(d_act, 1)

            def blk(b, u):
                gate(b)
                copy_out(b - 1, 1 - u)
                copy_x(b + 1, 1 - u)
                copy_a(b, u)

            copy_x(0, 0)
            gate(0)
            copy_x(1, 1)
            copy_a(0, 0)
            blk(1, 1)
            blk(2, 0)
            with act.Fori(1, n) as i:
                blk(i * 2 + 1, 1)
                blk(i * 2 + 2, 0)
            copy_out(n * 2, 0)

        @block.vector
        def _(dve):
            chain = Chain(dve, step_)
            tt, ts, cp = nc.vector.tensor_tensor, nc.vector.tensor_scalar, nc.vector.tensor_copy
            n = load(dve, trips[0:1, 0:1], 1, MAXT)

            def copy_x(b, u):
                dve.wait_ge(x_ps, b + 1)
                cp(xT[:, u, 4:8, :].rearrange("p c t -> p (c t)"), xps[:, 1, :]).then_inc(x_dve, 1)

            def hidden(b):
                dve.wait_ge(eg_ok, b + 1)
                chain.after(ts(sg[:, :], sg[:, :], 1.0, None, ALU.add))
                chain.after(nc.vector.reciprocal(sg[:, :], sg[:, :]))
                chain.after(tt(sg[:, :], gps[:, :], sg[:, :], ALU.mult))
                dve.wait_ge(u_ps, b + 1)
                wait(dve, a_ps, b)
                tt(a[:, :], ups[:, :], sg[:, :], ALU.mult).then_inc(a_ok, 1)

            def copy_out(b, u):
                dve.wait_ge(d_ps, b + 2)
                wait(dve, o_out, 16 * b)
                cp(out[:, u, HW:D], dps[:, 1, :]).then_inc(d_dve, 1)

            def blk(b, u):
                hidden(b)
                copy_out(b - 1, 1 - u)
                copy_x(b + 1, 1 - u)

            copy_x(0, 0)
            hidden(0)
            copy_x(1, 1)
            blk(1, 1)
            blk(2, 0)
            with dve.Fori(1, n) as i:
                chain.loop(i - 1, 6)
                blk(i * 2 + 1, 1)
                blk(i * 2 + 2, 0)
            copy_out(n * 2, 0)

        @block.tensor
        def _(pe):
            n = load(pe, trips[0:1, 0:1], 1, MAXT)

            def turn_x(b, u):
                half = b // 2 if isinstance(b, int) else None
                pe.wait_ge(x_in[u], 16 * half + 16 if half is not None else (b - u) * 8 + 16)
                wait(pe, x_act, b)
                wait(pe, x_dve, b)
                for c in range(DC):
                    mm = pe.transpose(xps[:, c // 4, (c % 4) * P:(c % 4 + 1) * P], xg[:, u, c * P:(c + 1) * P], ident[:, :])
                mm.then_inc(x_ps, 1)

            def in_count(b, u):
                return 16 * (b // 2) + 16 if isinstance(b, int) else (b - u) * 8 + 16

            def gate_up(b, u):
                pe.wait_ge(x_act, b + 1)
                pe.wait_ge(x_dve, b + 1)
                wait(pe, a_ok, b)
                pe.wait_ge(g_in[u], in_count(b, u))
                for c in range(DC):
                    mm = pe.matmul(gps[:, :], xT[:, u, c, :], wg[:, u, c, :], start=(c == 0), stop=(c == DC - 1))
                mm.then_inc(g_ps, 1)
                pe.wait_ge(u_in[u], in_count(b, u))
                for c in range(DC):
                    mm = pe.matmul(ups[:, :], xT[:, u, c, :], wu[:, u, c, :], start=(c == 0), stop=(c == DC - 1))
                mm.then_inc(u_ps, 1)

            def turn_a(b, u):
                pe.wait_ge(a_ok, b + 1)
                wait(pe, aT_ok, b)
                for c in range(FC):
                    mm = pe.transpose(aps[:, c * P:(c + 1) * P], a[:, c * P:(c + 1) * P], ident[:, :])
                mm.then_inc(a_ps, 1)

            def down(b, u):
                pe.wait_ge(aT_ok, b + 1)
                pe.wait_ge(d_in[u], in_count(b, u))
                wait(pe, d_act, b)
                wait(pe, d_dve, b)
                for half in range(2):
                    for c in range(FC):
                        mm = pe.matmul(dps[:, half, :], aT[:, u, c, :], wd[:, u, c, half * HW:(half + 1) * HW],
                                       start=(c == 0), stop=(c == FC - 1))
                mm.then_inc(d_ps, 1)

            def blk(b, u):
                gate_up(b, u)
                down(b - 1, 1 - u)
                turn_x(b + 1, 1 - u)
                turn_a(b, u)

            pe.sem_inc(d_ps, 1)
            turn_x(0, 0)
            gate_up(0, 0)
            turn_x(1, 1)
            turn_a(0, 0)
            blk(1, 1)
            blk(2, 0)
            with pe.Fori(1, n) as i:
                blk(i * 2 + 1, 1)
                blk(i * 2 + 2, 0)
            down(n * 2, 0)


def finish(nc, dr, consts, keep):
    y, gates = keep["y"], keep["gates"]
    with ExitStack() as ctx:
        sb = lambda n, s, d=F32: ctx.enter_context(nc.sbuf_tensor(n, s, d))
        sem = stage_semaphores(nc, ctx)
        e = sb("expert_rows", [P, 4, 2, D])
        fw = sb("final_row", [P, D])
        o = sb("y_out", [P, 2, D])
        junk = sb("square_out6", [P, D], BF16)
        st = sb("final_stats", [P, TILES, 4])
        fw_in, e_in = sem("final_row_loaded"), [sem(f"expert_rows_loaded{s}") for s in range(4)]
        y_ok, r_ok, o_ok, o_out = sem("moe_added"), sem("final_rstd"), sem("out_ready"), [sem(f"out_stored{u}") for u in range(2)]
        act_step, dve_step = sem("p6_act_step"), sem("p6_dve_step")
        block = ctx.enter_context(nc.Block())
        moe = dr["moe"][0:2 * TILES * P].rearrange("(t p c) d -> t p (c d)", p=P, c=2)
        yp = dr["y_prompt"].rearrange("b (t p) d -> (b t) p d", p=P)

        @block.sync
        def _(sp):
            def load(t):
                wait(sp, y_ok, t - 3)
                sp.dma_start(e[:, t % 4, :, :].rearrange("p c d -> p (c d)"), moe[t]).then_inc(e_in[t % 4], 16)

            sp.dma_start(fw[:, :], dr["final_w"].to_broadcast([P, D])).then_inc(fw_in, 16)
            for t in range(3):
                load(t)
            for t in range(TILES):
                if t + 3 < TILES:
                    load(t + 3)
                sp.wait_ge(o_ok, t + 1)
                dst = yp[t] if t < NT else dr["y_sample"].rearrange("b t d -> (b t) d")
                sp.dma_start(dst, o[:, t % 2, :]).then_inc(o_out[t % 2], 16)
            sp.wait_ge(o_out[0], 16 * (NT // 2 + 1))
            sp.wait_ge(o_out[1], 16 * (NT // 2))

        @block.scalar
        def _(act):
            chain = Chain(act, act_step)
            for t in range(TILES):
                act.wait_ge(y_ok, t + 1)
                chain.after(nc.scalar.activation(junk[:, :], y[:, t, :], ACT.Square, accum_out=st[:, t, 0:1]))
                chain.after(nc.scalar.activation(st[:, t, 1:2], st[:, t, 0:1], ACT.Ln, scale=1.0 / D, bias=consts["eps"][:, 0:1]))
                nc.scalar.activation(st[:, t, 2:3], st[:, t, 1:2], ACT.Exp, scale=-0.5).then_inc(r_ok, 1)

        @block.vector
        def _(dve):
            chain = Chain(dve, dve_step)
            stt = nc.vector.scalar_tensor_tensor
            dve.wait_ge(fw_in, 16)

            def add(t):
                dve.wait_ge(e_in[t % 4], 16 * (t // 4) + 16)
                chain.after(stt(out=y[:, t, :], in0=e[:, t % 4, 0, :], scalar=gates[:, t, 0:1], in1=y[:, t, :], op0=ALU.mult, op1=ALU.add))
                stt(out=y[:, t, :], in0=e[:, t % 4, 1, :], scalar=gates[:, t, 1:2], in1=y[:, t, :], op0=ALU.mult, op1=ALU.add).then_inc(y_ok, 1)

            add(0)
            for t in range(TILES):
                if t + 1 < TILES:
                    add(t + 1)
                dve.wait_ge(r_ok, t + 1)
                wait(dve, o_out[t % 2], 16 * (t // 2))
                stt(out=o[:, t % 2, :], in0=y[:, t, :], scalar=st[:, t, 2:3], in1=fw[:, :], op0=ALU.mult, op1=ALU.mult).then_inc(o_ok, 1)


def make_consts(nc, ctx):
    sb = lambda n, s, d=F32: ctx.enter_context(nc.sbuf_tensor(n, s, d))
    sem = lambda n: ctx.enter_context(nc.semaphore(n))
    c = {"ident": sb("ident", [P, P]), "eps": sb("eps_col", [P, 1])}
    c["sem"] = sem("consts_ready")
    c["zeroed"] = sem("consts_zeroed")
    with nc.Block() as block:
        @block.gpsimd
        def _(g):
            g.memset(c["ident"][:, :], 0.0).then_inc(c["zeroed"], 1)
            g.memset(c["eps"][:, :], EPS).then_inc(c["sem"], 1)
            g.wait_ge(c["zeroed"], 1)
            g.affine_select(out=c["ident"][:, :], in_=c["ident"][:, :], compare_op=ALU.not_equal, fill=1.0,
                            base=0, pattern=[[-1, P]], channel_multiplier=1).then_inc(c["sem"], 1)
    c["n"] = 2
    return c


def build(nc, dr):
    dr["z"] = {j: nc.dram_tensor(f"scratch_z{j}", [TILES, P, HW], F32, kind="Internal").ap() for j in (QA, KT)}
    dr["rec"] = nc.dram_tensor("scratch_rec", [TILES, P, HW], F32, kind="Internal").ap()
    dr["att"] = nc.dram_tensor("scratch_att", [TILES, P, HW], F32, kind="Internal").ap()
    dr["table"] = nc.dram_tensor("scratch_table", [N_EXP * TILES + 1, P, 1], U32, kind="Internal").ap()
    dr["h2"] = nc.dram_tensor("scratch_h2", [TILES * P + PAD_ROWS, D], F32, kind="Internal").ap()
    dr["moe"] = nc.dram_tensor("scratch_moe", [2 * (TILES * P + PAD_ROWS), D], F32, kind="Internal").ap()
    with ExitStack() as ctx:
        consts = make_consts(nc, ctx)
        project(nc, dr, consts)
        attend(nc, dr, consts)
        attend_sample(nc, dr, consts)
        sb = lambda n, s, d=F32: ctx.enter_context(nc.sbuf_tensor(n, s, d))
        keep = {"y": sb("y_rows", [P, TILES, D]), "gates": sb("gates", [P, TILES, 2]), "work": sb("work_list", [1, P], I32),
                "slot_all": sb("block_slots_all", [P, P], U32), "tok_all": sb("block_tokens_all", [P, P], U32),
                "trips": sb("loop_trips", [1, 1], I32), "slot_now": sb("slot_now", [P, 2, 2], U32)}
        mix_and_route(nc, dr, consts, keep)
        experts(nc, dr, consts, keep)
        finish(nc, dr, consts, keep)


_INS = ['x_prompt', 'x_sample', 'cache_k', 'cache_v', 'state_rec', 'w_in', 'lam_q1', 'lam_k1', 'lam_q2', 'lam_k2',
        'subln_w', 'lb_param', 'gnorm_w', 'w_out', 'norm1_w', 'norm2_w', 'w_group', 'w_router', 'w_e_gate', 'w_e_up',
        'w_e_down', 'final_w']
_OUTS = [('y_prompt', (1, 2048, 1024)), ('y_sample', (8, 16, 1024)), ('k_prompt', (1, 1, 2048, 4, 128)),
         ('v_prompt', (1, 1, 2048, 4, 128)), ('state_prompt', (1, 1, 4, 128, 128)), ('k_sample', (1, 8, 16, 4, 128)),
         ('v_sample', (1, 8, 16, 4, 128)), ('state_sample', (1, 8, 4, 128, 128))]


def kernel(**inputs):
    import numpy as _np
    import concourse.bacc as _bacc
    from concourse import mybir as _mybir
    from concourse.bass_utils import run_bass_kernel_spmd as _run

    nc = _bacc.Bacc("TRN2", target_bir_lowering=False, num_devices=1)
    arrays, dr = {}, {}
    for name in _INS:
        a = _np.ascontiguousarray(inputs[name])
        if a.ndim == 1:
            a = a.reshape(1, -1)
        arrays[f"in_{name}"] = a
        dr[name] = nc.dram_tensor(f"in_{name}", a.shape, _mybir.dt.from_np(a.dtype), kind="ExternalInput").ap()
    for name, shape in _OUTS:
        dr[name] = nc.dram_tensor(f"out_{name}", shape, _mybir.dt.float32, kind="ExternalOutput").ap()
    build(nc, dr)
    r = _run(nc, [arrays], core_ids=[0])
    return tuple(r.results[0][f"out_{name}"] for name, _ in _OUTS)
```

```python
from contextlib import ExitStack

import concourse.bass as bass
from concourse import mybir

P = 128
D = 1024
DC = D // P
SEQ = 2048
NT = SEQ // P
TILES = NT + 1
HEADS = 4
HW = 512
EPS = 1e-6
N_GRP = 4
N_EXP = 32
LOGITS = N_GRP + N_EXP
D_EXP = 512
QUEUE = TILES * P
PAD_ROWS = P // 2
N_BLOCKS = 2 * TILES + N_EXP - 1
LAM_INIT = 0.8 - 0.6
HIDDEN = -1e30
DEC_B = 8
DEC = 16
F32 = mybir.dt.float32
I32 = mybir.dt.int32
U32 = mybir.dt.uint32
U8 = mybir.dt.uint8
BF16 = mybir.dt.bfloat16
ALU = mybir.AluOpType
ACT = mybir.ActivationFunctionType
AX = mybir.AxisListType
QA, KA, VA, KT, FR, QR, IR, GR = range(8)
W_COL = {QA: 0, KA: 1, VA: 2, QR: 3, FR: 4, IR: 5, GR: 6}
CHANNEL_MAJOR = (QA, QR, FR)


class Chain:

    def __init__(self, eng, sem):
        self.eng, self.sem, self.base, self.n = eng, sem, 0, 0

    def loop(self, i, per_iter):
        self.start, self.n = self.base + self.n, 0
        self.base = i * per_iter + self.start
        self.per_iter = per_iter

    def end_loop(self, trips):
        assert self.n == self.per_iter, (self.sem, self.n, self.per_iter)
        self.base, self.n = self.start + trips * self.per_iter, 0

    def after(self, ins):
        ins.then_inc(self.sem, 1)
        self.n += 1
        self.eng.wait_ge(self.sem, self.base + self.n)


def stage_semaphores(nc, ctx):
    held = []

    def give_back():
        nc.clear_and_free_semaphores(held)
        nc.all_engine_barrier()

    def sem(name):
        held.append(nc.alloc_semaphore(name))
        return held[-1]

    ctx.callback(give_back)
    return sem


def row(ap, t):
    return ap[bass.ds(t, 1)].rearrange("o p d -> (o p) d")


def wait(eng, sem, value):
    if not isinstance(value, int) or value > 0:
        eng.wait_ge(sem, value)


def levels(t):
    top = P // 2 if not (isinstance(t, int) and t == NT) else DEC // 2
    halves = []
    while top >= 1:
        halves.append(top)
        top //= 2
    return list(enumerate([0] + halves))


def heads(ap):
    return ap.rearrange("p (h t) -> p h t", h=HEADS)


def project(nc, dr, consts):
    ident = consts["ident"]
    with ExitStack() as ctx:
        sb = lambda n, s, d=F32: ctx.enter_context(nc.sbuf_tensor(n, s, d))
        ps = lambda n, s, d=F32: ctx.enter_context(nc.psum_tensor(n, s, d))
        sem = stage_semaphores(nc, ctx)
        w = sb("w_in_sb", [P, DC, 7 * HW])
        n1 = sb("norm1_row", [P, D])
        x = sb("x_tile", [P, D])
        h = sb("h_tile", [P, D])
        junk = sb("square_out", [P, D], BF16)
        st = sb("rms_stats", [P, 4])
        hT = sb("hT", [P, 2, DC, P])
        z = sb("z_ring", [P, 4, HW])
        F = sb("forget", [P, HW])
        qraw = sb("q_raw", [P, HW])
        eq = sb("exp_q", [P, HW])
        dl = sb("decay_to_end", [P, HW])
        bcum = sb("log_decay", [P, 2, HW])
        q = sb("q_silu", [P, 2, HW])
        k = sb("k_gate", [P, 2, HW])
        qe = sb("q_decayed", [P, 2, HW])
        kd = sb("k_decayed", [P, HW])
        kdT = sb("k_decayed_T", [P, HW])
        ir = sb("ir", [P, 2, HW])
        gr = sb("gr", [P, 2, HW])
        gate = sb("gate", [P, HW])
        gnrow = sb("gnorm_row", [P, P])
        diff = sb("level_decay", [P, 2, HW])
        X = sb("level_operand", [P, 2, HW])
        A = sb("scores_T", [P, HW])
        S = sb("state", [P, HW])
        o_row = sb("rec_out", [P, HW])
        mask = sb("level_mask", [P, 8, P], U8)
        reset = sb("reset", [P, HW])
        lb = sb("lb", [P, HEADS])
        oml = sb("one_minus_lb", [P, HEADS])
        lbp = sb("lb_param_sb", [P, 2, HEADS])
        eL = sb("decay_of_tile", [P, 2, HEADS * DEC_B])
        ssr = sb("rec_stats", [P, 12])
        rowmask = sb("stream_mask", [P, DEC_B])
        S0 = w[:, :, 0:HW]
        qez = w[:, :, HW:2 * HW]
        kdz = w[:, :, 2 * HW:3 * HW]
        Sout = w[:, :, 3 * HW:4 * HW]

        hps = ps("hT_psum", [P, 2, HW])
        zps = [ps(f"z_psum{s}", [P, HW]) for s in range(2)]
        lps = [ps(f"level_psum{s}", [P, HW]) for s in range(2)]
        ops = ps("rec_out_psum", [P, HW])
        mps = ps("state_psum", [P, HW])

        w_in = [sem(f"w_loaded{g}") for g in range(7)]
        n1_in, row_in = sem("norm1_row_loaded"), sem("rows_loaded")
        x_in = sem("x_loaded")
        act_step, dve_step, pool_step = sem("p1_act_step"), sem("p1_dve_step"), sem("p1_pool_step")
        rstd_ok, h_ok, hT_ps = sem("rstd_ready"), sem("h_ready"), sem("hT_transposed")
        hT_act, hT_dve = sem("hT_half0_ready"), sem("hT_half1_ready")
        z_ps, z_act, z_dve = sem("z_in_psum"), sem("z_even_copied"), sem("z_odd_copied")
        z_out = [sem(f"z_stored{s}") for s in range(4)]
        f_ok, lf_ok, b_ok, eq_ok, qk_ok = sem("f_ready"), sem("logf_ready"), sem("b_ready"), sem("expq_ready"), sem("qk_ready")
        eb_ok, dl_ok, ed_ok, qek_ok = sem("expb_ready"), sem("enddiff_ready"), sem("enddecay_ready"), sem("decayed_ready")
        diff_ok, E_ok, X_ok = sem("level_diff_ready"), sem("level_exp_ready"), sem("level_operand_ready")
        lv_ps, cp_ok = sem("level_in_psum"), sem("level_merged")
        kdt_ps, kdt_ok, st_ps, s_ok = sem("kdT_in_psum"), sem("kdT_ready"), sem("state_in_psum"), sem("state_ready")
        o_ps, r_ok, eg_ok, orow_ok, orow_out = sem("o_in_psum"), sem("rec_rstd_ready"), sem("expg_ready"), sem("rec_out_ready"), sem("rec_out_stored")
        lb_e, masks_ok, sp_out = sem("lb_exp"), sem("masks_ready"), sem("state_prompt_stored")
        S0_in, qz_ok, kz_ok, so_ps, so_ok, ss_out = (sem("state_rec_loaded"), sem("sample_q_zeroed"), sem("sample_k_ready"),
                                                    sem("sample_state_in_psum"), sem("sample_state_ready"), sem("state_sample_stored"))
        qzf_ok = sem("sample_q_ready")
        merge_turn = sem("merge_turn")
        block = ctx.enter_context(nc.Block())

        xp = dr["x_prompt"].rearrange("b (t p) d -> (b t) p d", p=P)
        xs = dr["x_sample"].rearrange("b t d -> (b t) d")
        kp = dr["k_prompt"].rearrange("l b (t p) h d -> (l b t) p (h d)", p=P)
        vp = dr["v_prompt"].rearrange("l b (t p) h d -> (l b t) p (h d)", p=P)
        ksm = dr["k_sample"].rearrange("l b t h d -> (l b t) (h d)")
        vsm = dr["v_sample"].rearrange("l b t h d -> (l b t) (h d)")
        TRIPS = NT // 2 - 1

        def is_last(t):
            return isinstance(t, int) and t == NT

        @block.sync
        def _(sp):
            wv = dr["w_in"].rearrange("l (c p) n -> p (l c) n", p=P)

            def load_x(t):
                wait(sp, h_ok, t)
                sp.dma_start(x[:, :], xs if is_last(t) else row(xp, t)).then_inc(x_in, 16)

            load_x(0)
            sp.dma_start(n1[:, :], dr["norm1_w"].to_broadcast([P, D])).then_inc(n1_in, 16)
            sp.dma_start(gnrow[:, :], dr["gnorm_w"].to_broadcast([P, P])).then_inc(row_in, 16)
            with nc.allow_non_contiguous_dma(reason="1024 floats, once"):
                for i in range(2):
                    sp.dma_start(lbp[:, i, :], dr["lb_param"][i].rearrange("(h p) -> p h", p=P)).then_inc(row_in, 16)
            for j in (QA, KA, VA, FR, QR, IR, GR):
                g = W_COL[j]
                sp.dma_start(w[:, :, g * HW:(g + 1) * HW], wv[:, :, g * HW:(g + 1) * HW]).then_inc(w_in[g], 16)
                if j == VA:
                    load_x(1)

            def store(t, j):
                sp.wait_ge(z_dve if j % 2 else z_act, 4 * t + j // 2 + 2)
                if j == KA:
                    dst = ksm if is_last(t) else row(kp, t)
                elif j == VA:
                    dst = vsm if is_last(t) else row(vp, t)
                else:
                    dst = row(dr["z"][j], t)
                sp.dma_start(dst, z[:, j, :]).then_inc(z_out[j], 16)

            def store_rec(t):
                sp.wait_ge(orow_ok, t + 1)
                sp.dma_start(row(dr["rec"], t), o_row[:, :]).then_inc(orow_out, 16)

            def tile(t, rec=True):
                if not is_last(t) and not (isinstance(t, int) and t == 0):
                    load_x(t + 1)
                for j in (QA, KA, VA, KT):
                    store(t, j)
                if rec:
                    store_rec(t - 1)

            tile(0, False)
            tile(1)
            with sp.Fori(1, NT // 2 - 1) as i:
                for u in range(2):
                    tile(i * 2 + u)
            for t in (NT - 2, NT - 1, NT):
                tile(t)
            sp.wait_ge(s_ok, NT + 1)
            sp.dma_start(dr["state_prompt"][0, 0].rearrange("h k v -> k h v"), heads(S[:, :])).then_inc(sp_out, 16)
            sp.wait_ge(z_ps, 8 * TILES)
            for b in range(DEC_B):
                sp.dma_start(heads(S0[:, b, :]), dr["state_rec"][0, b].rearrange("h k v -> k h v")).then_inc(S0_in, 16)
            store_rec(NT)
            for b in range(DEC_B):
                sp.wait_ge(so_ok, b + 1)
                sp.dma_start(dr["state_sample"][0, b].rearrange("h k v -> k h v"), heads(Sout[:, b, :])).then_inc(ss_out, 16)
            for s in range(4):
                sp.wait_ge(z_out[s], 16 * TILES)
            sp.wait_ge(orow_out, 16 * TILES)
            sp.wait_ge(sp_out, 16)
            sp.wait_ge(ss_out, 16 * DEC_B)

        @block.gpsimd
        def _(pool):
            chain = Chain(pool, pool_step)
            pool.memset(mask[:, :, :], 0.0)
            chain.after(pool.memset(rowmask[:, :], 1.0))
            mf = diff[:, :, :].rearrange("p a n -> p (a n)").rearrange("p (l t) -> p l t", t=P)
            chain.after(pool.memset(mf, 0.0))
            for l, m in levels(0)[1:]:
                v = mf[:, l, :].rearrange("p (g s m) -> p g s m", s=2, m=m)[:, :, 1, :]
                chain.after(pool.memset(v, 1.0))
                chain.after(pool.affine_select(out=v, in_=v, compare_op=ALU.is_ge, fill=0.0, base=0,
                                               pattern=[[-2 * m, P // (2 * m)], [0, m]], channel_multiplier=1))
                chain.after(pool.affine_select(out=v, in_=v, compare_op=ALU.is_ge, fill=0.0, base=m - 1,
                                               pattern=[[2 * m, P // (2 * m)], [0, m]], channel_multiplier=-1))
            chain.after(pool.tensor_copy(mask[:, 1:8, :], mf[:, 1:8, :]))
            chain.after(pool.tensor_copy(mask[:, 0, :], ident[:, :]))
            chain.after(pool.affine_select(out=rowmask[:, :], in_=rowmask[:, :], compare_op=ALU.is_ge, fill=0.0, base=0,
                                           pattern=[[-DEC, DEC_B]], channel_multiplier=1))
            pool.affine_select(out=rowmask[:, :], in_=rowmask[:, :], compare_op=ALU.is_ge, fill=0.0, base=DEC - 1,
                               pattern=[[DEC, DEC_B]], channel_multiplier=-1).then_inc(masks_ok, 1)

            def diffs(t, u):
                pool.wait_ge(b_ok, t + 1)
                n = DEC if is_last(t) else P
                bg = bcum[:, u, :].rearrange("p (g n) -> p g n", n=n)
                end = bg[:, :, n - 1:n].to_broadcast([P, HW // n, n])
                pool.tensor_tensor(dl[:, :].rearrange("p (g n) -> p g n", n=n), end, bg, ALU.subtract).then_inc(dl_ok, 1)
                for pos, m in levels(t)[1:]:
                    s = (u + pos - 1) % 2
                    wait(pool, X_ok, 7 * t + pos - 2)
                    bv = bcum[:, u, :].rearrange("p (g s m) -> p g s m", s=2, m=m)
                    dv = diff[:, s, :].rearrange("p (g s m) -> p g s m", s=2, m=m)
                    split = bv[:, :, 0, m - 1:m].to_broadcast([P, HW // (2 * m), m])
                    pool.tensor_tensor(dv[:, :, 0, :], split, bv[:, :, 0, :], ALU.subtract)
                    pool.tensor_tensor(dv[:, :, 1, :], bv[:, :, 1, :], split, ALU.subtract).then_inc(diff_ok, 1)

            diffs(0, 0)
            diffs(1, 1)
            with pool.Fori(1, NT // 2) as i:
                for u in range(2):
                    diffs(i * 2 + u, u)
            diffs(NT, 0)
            pool.wait_ge(z_ps, 8 * TILES)
            pool.memset(qez, 0.0).then_inc(qz_ok, 1)

        @block.scalar
        def _(act):
            chain = Chain(act, act_step)
            act.sem_inc(z_act, 1)
            act.wait_ge(consts["sem"], consts["n"])

            def stats(t):
                act.wait_ge(x_in, 16 * t + 16)
                wait(act, h_ok, t)
                chain.after(nc.scalar.activation(junk[:, :], x[:, :], ACT.Square, accum_out=st[:, 0:1]))
                chain.after(nc.scalar.activation(st[:, 1:2], st[:, 0:1], ACT.Ln, scale=1.0 / D, bias=consts["eps"][:, 0:1]))
                nc.scalar.activation(st[:, 2:3], st[:, 1:2], ACT.Exp, scale=-0.5).then_inc(rstd_ok, 1)

            def hT_copy(t, u):
                act.wait_ge(hT_ps, t + 1)
                nc.scalar.copy(hT[:, u, 0:4, :].rearrange("p c t -> p (c t)"), hps[:, 0, :]).then_inc(hT_act, 1)

            def evac(t, u, j):
                act.wait_ge(z_ps, 8 * t + j + 1)
                if j == FR:
                    wait(act, b_ok, t)
                    nc.scalar.activation(F[:, :], zps[0][:, :], ACT.Exp, scale=-1.0).then_inc(z_act, 1)
                elif j == IR:
                    nc.scalar.copy(ir[:, u, :], zps[0][:, :]).then_inc(z_act, 1)
                else:
                    wait(act, z_out[j], 16 * t)
                    nc.scalar.copy(z[:, j, :], zps[0][:, :]).then_inc(z_act, 1)

            def expo(t, u, pos):
                s = (u + pos - 1) % 2
                act.wait_ge(diff_ok, 7 * t + pos)
                nc.scalar.activation(diff[:, s, :], diff[:, s, :], ACT.Exp).then_inc(E_ok, 1)

            def logf(t):
                act.wait_ge(f_ok, t + 1)
                nc.scalar.activation(F[:, :], F[:, :], ACT.Ln).then_inc(lf_ok, 1)

            def expq(t):
                act.wait_ge(z_dve, 4 * t + 4)
                nc.scalar.activation(eq[:, :], qraw[:, :], ACT.Exp, scale=-1.0).then_inc(eq_ok, 1)

            def expb(t, u):
                act.wait_ge(b_ok, t + 1)
                nc.scalar.activation(eq[:, :], bcum[:, u, :], ACT.Exp).then_inc(eb_ok, 1)
                act.wait_ge(dl_ok, t + 1)
                nc.scalar.activation(dl[:, :], dl[:, :], ACT.Exp).then_inc(ed_ok, 1)

            def expg(t, u):
                act.wait_ge(z_dve, 4 * t + 5)
                wait(act, orow_ok, t)
                nc.scalar.activation(gate[:, :], gr[:, u, :], ACT.Exp, scale=-1.0).then_inc(eg_ok, 1)

            def kdT_copy(t):
                act.wait_ge(kdt_ps, t + 1)
                nc.scalar.copy(kdT[:, :], mps[:, :]).then_inc(kdt_ok, 1)

            def rec_stats(t):
                act.wait_ge(o_ps, t + 1)
                for hd in range(HEADS):
                    ins = nc.scalar.activation(junk[:, 0:P], ops[:, hd * P:(hd + 1) * P], ACT.Square, accum_out=ssr[:, hd:hd + 1])
                    chain.after(ins)
                chain.after(nc.scalar.activation(ssr[:, 4:8], ssr[:, 0:4], ACT.Ln, scale=1.0 / P, bias=consts["eps"][:, 0:1]))
                nc.scalar.activation(ssr[:, 8:12], ssr[:, 4:8], ACT.Exp, scale=-0.5).then_inc(r_ok, 1)

            def tile(t, u, rec=True):
                g, v = t - 1, 1 - u
                evac(t, u, QA)
                if rec:
                    expo(g, v, 1)
                if not is_last(t):
                    stats(t + 1)
                if rec:
                    expo(g, v, 2)
                evac(t, u, VA)
                if rec:
                    expo(g, v, 3)
                    expo(g, v, 4)
                evac(t, u, FR)
                if not is_last(t):
                    hT_copy(t + 1, 1 - u)
                if rec:
                    expo(g, v, 5)
                logf(t)
                expq(t)
                if rec:
                    expo(g, v, 6)
                    kdT_copy(g)
                evac(t, u, IR)
                if rec:
                    expo(g, v, 7)
                expb(t, u)
                if rec:
                    rec_stats(g)
                expg(t, u)

            stats(0)
            hT_copy(0, 0)
            act.wait_ge(lb_e, 1)
            nc.scalar.activation(oml[:, :], oml[:, :], ACT.Exp).then_inc(lb_e, 1)
            tile(0, 0, False)
            tile(1, 1)
            with act.Fori(1, NT // 2) as i:
                chain.loop(i - 1, 14)
                for u in range(2):
                    tile(i * 2 + u, u)
            chain.end_loop(TRIPS)
            tile(NT, 0)
            for pos, m in levels(NT)[1:]:
                expo(NT, 0, pos)
            kdT_copy(NT)
            rec_stats(NT)

        @block.vector
        def _(dve):
            chain = Chain(dve, dve_step)
            dve.sem_inc(z_dve, 1)
            tt, ts, stt = nc.vector.tensor_tensor, nc.vector.tensor_scalar, nc.vector.scalar_tensor_tensor
            def make_h(t):
                dve.wait_ge(rstd_ok, t + 1)
                wait(dve, hT_ps, t)
                stt(out=h[:, :], in0=x[:, :], scalar=st[:, 2:3], in1=n1[:, :], op0=ALU.mult, op1=ALU.mult).then_inc(h_ok, 1)

            def hT_copy(t, u):
                dve.wait_ge(hT_ps, t + 1)
                nc.vector.tensor_copy(hT[:, u, 4:8, :].rearrange("p c t -> p (c t)"), hps[:, 1, :]).then_inc(hT_dve, 1)

            def evac(t, u, j):
                dve.wait_ge(z_ps, 8 * t + j + 1)
                if j in (KA, KT):
                    wait(dve, z_out[j], 16 * t)
                dst = {KA: z[:, KA, :], KT: z[:, KT, :], QR: qraw[:, :], GR: gr[:, u, :]}[j]
                nc.vector.tensor_copy(dst, zps[1][:, :]).then_inc(z_dve, 1)

            def forget(t, u):
                dve.wait_ge(z_act, 4 * t + 4)
                chain.after(ts(F[:, :], F[:, :], 1.0, None, ALU.add))
                chain.after(nc.vector.reciprocal(F[:, :], F[:, :]))
                for hd in range(HEADS):
                    f = F[:, hd * P:(hd + 1) * P]
                    ins = ts(f, f, oml[:, hd:hd + 1], lb[:, hd:hd + 1], ALU.mult, ALU.add)
                chain.after(ins)
                ts(k[:, u, :], F[:, :], -1.0, 1.0, ALU.mult, ALU.add).then_inc(f_ok, 1)

            def silu_q(t, u):
                dve.wait_ge(eq_ok, t + 1)
                chain.after(ts(eq[:, :], eq[:, :], 1.0, None, ALU.add))
                chain.after(nc.vector.reciprocal(eq[:, :], eq[:, :]))
                tt(q[:, u, :], qraw[:, :], eq[:, :], ALU.mult).then_inc(qk_ok, 1)

            def scan(t, u):
                dve.wait_ge(lf_ok, t + 1)
                if is_last(t):
                    chain.after(nc.vector.memset(reset[:, :].rearrange("p (g n) -> p g n", n=DEC)[:, :, 0:1], 0.0))
                nc.vector.tensor_tensor_scan(bcum[:, u, :], reset[:, :], F[:, :], 0.0, ALU.mult, ALU.add).then_inc(b_ok, 1)

            def decayed(t, u):
                n = DEC if is_last(t) else P
                dve.wait_ge(eb_ok, t + 1)
                tt(qe[:, u, :], q[:, u, :], eq[:, :], ALU.mult)
                nc.vector.tensor_copy(eL[:, u, 0:HW // n], eq[:, :].rearrange("p (g n) -> p g n", n=n)[:, :, n - 1])
                dve.wait_ge(ed_ok, t + 1)
                wait(dve, kdt_ps, t)
                tt(kd[:, :], k[:, u, :], dl[:, :], ALU.mult).then_inc(qek_ok, 1)

            def operand(t, u, pos, m):
                s = (u + pos - 1) % 2
                dve.wait_ge(E_ok, 7 * t + pos)
                wait(dve, lv_ps, 8 * t + (pos - 1 if pos >= 3 else 0))
                if pos == 1:
                    dve.wait_ge(qk_ok, t + 1)
                v = lambda a: a.rearrange("p (g s m) -> p g s m", s=2, m=m)
                tt(v(X[:, s, :])[:, :, 0, :], v(k[:, u, :])[:, :, 0, :], v(diff[:, s, :])[:, :, 0, :], ALU.mult)
                tt(v(X[:, s, :])[:, :, 1, :], v(q[:, u, :])[:, :, 1, :], v(diff[:, s, :])[:, :, 1, :], ALU.mult).then_inc(X_ok, 1)

            def merge(t, pos, m):
                dve.wait_ge(lv_ps, 8 * t + pos + 1)
                if is_last(t) and pos:
                    dve.wait_ge(cp_ok, 8 * t + pos)
                dve.sem_inc(merge_turn, 1)
                l = 0 if m == 0 else 7 - (m.bit_length() - 1)
                if pos == 0 and is_last(t):
                    chain.after(nc.vector.memset(A[:, :], 0.0))
                if isinstance(t, int) and t == 0 and pos == 0:
                    dve.wait_ge(masks_ok, 1)
                mk = mask[:, l:l + 1, :].to_broadcast([P, HEADS, P])
                ins = nc.vector.copy_predicated(heads(A[:, :]), mk, heads(lps[pos % 2][:, :]))
                ins.then_inc(cp_ok, 1)

            def rec_gate(t, u):
                dve.wait_ge(eg_ok, t + 1)
                chain.after(ts(gate[:, :], gate[:, :], 1.0, None, ALU.add))
                chain.after(nc.vector.reciprocal(gate[:, :], gate[:, :]))
                chain.after(tt(gate[:, :], gate[:, :], gr[:, u, :], ALU.mult))
                chain.after(tt(heads(gate[:, :]), heads(gate[:, :]), gnrow[:, None, :].to_broadcast([P, HEADS, P]), ALU.mult))

            def rec_row(t):
                dve.wait_ge(r_ok, t + 1)
                wait(dve, orow_out, 16 * t)
                for hd in range(HEADS):
                    c = slice(hd * P, (hd + 1) * P)
                    ins = stt(out=o_row[:, c], in0=ops[:, c], scalar=ssr[:, 8 + hd:9 + hd], in1=gate[:, c], op0=ALU.mult, op1=ALU.mult)
                ins.then_inc(orow_ok, 1)

            def state(t, u):
                dve.wait_ge(st_ps, t + 1)
                for hd in range(HEADS):
                    c = slice(hd * P, (hd + 1) * P)
                    ins = stt(out=S[:, c], in0=S[:, c], scalar=eL[:, u, hd:hd + 1], in1=mps[:, c], op0=ALU.mult, op1=ALU.add)
                ins.then_inc(s_ok, 1)

            def tile(t, u, rec=True):
                g, v = t - 1, 1 - u
                lv = levels(0)
                if rec:
                    merge(g, 0, 0)
                    operand(g, v, *lv[1])
                evac(t, u, KA)
                if not is_last(t):
                    make_h(t + 1)
                if rec:
                    merge(g, *lv[1])
                    operand(g, v, *lv[2])
                    rec_gate(g, v)
                    merge(g, *lv[2])
                    operand(g, v, *lv[3])
                evac(t, u, KT)
                if rec:
                    merge(g, *lv[3])
                    operand(g, v, *lv[4])
                forget(t, u)
                if not is_last(t):
                    hT_copy(t + 1, 1 - u)
                if rec:
                    merge(g, *lv[4])
                    operand(g, v, *lv[5])
                evac(t, u, QR)
                if rec:
                    merge(g, *lv[5])
                    operand(g, v, *lv[6])
                silu_q(t, u)
                scan(t, u)
                if rec:
                    merge(g, *lv[6])
                    operand(g, v, *lv[7])
                    merge(g, *lv[7])
                decayed(t, u)
                evac(t, u, GR)
                if rec:
                    rec_row(g)
                    state(g, v)

            dve.wait_ge(n1_in, 16)
            make_h(0)
            hT_copy(0, 0)
            dve.wait_ge(row_in, 48)
            chain.after(nc.vector.memset(reset[:, :], 1.0))
            nc.vector.memset(heads(reset[:, :])[:, :, 0:1], 0.0)
            nc.vector.memset(A[:, :], 0.0)
            chain.after(nc.vector.memset(S[:, :], 0.0))
            tt(oml[:, :], lbp[:, 1, :], lbp[:, 0, :], ALU.subtract).then_inc(lb_e, 1)
            dve.wait_ge(lb_e, 2)
            chain.after(ts(oml[:, :], oml[:, :], 1.0, None, ALU.add))
            chain.after(nc.vector.reciprocal(lb[:, :], oml[:, :]))
            chain.after(ts(oml[:, :], lb[:, :], -1.0, 1.0, ALU.mult, ALU.add))
            dve.sem_inc(s_ok, 1)
            tile(0, 0, False)
            tile(1, 1)
            with dve.Fori(1, NT // 2) as i:
                chain.loop(i - 1, 18)
                for u in range(2):
                    tile(i * 2 + u, u)
            chain.end_loop(TRIPS)
            tile(NT, 0)
            lv = levels(NT)
            for pos, m in lv[1:]:
                operand(NT, 0, pos, m)
                merge(NT, *lv[pos - 1])
            merge(NT, *lv[-1])
            dve.wait_ge(qz_ok, 1)
            dve.wait_ge(qek_ok, TILES)
            for b in range(DEC_B):
                c = slice(b * DEC, (b + 1) * DEC)
                ins = nc.vector.tensor_copy(heads(qez[:, b, :])[:, :, c], heads(qe[:, 0, :])[:, :, c])
            ins.then_inc(qzf_ok, 1)
            dve.wait_ge(kdt_ok, TILES)
            for b in range(DEC_B):
                ins = ts(kdz[:, b, :], kdT[:, :], rowmask[:, b:b + 1], None, ALU.mult)
            ins.then_inc(kz_ok, 1)
            rec_gate(NT, 0)
            dve.wait_ge(S0_in, 16 * DEC_B)
            for b in range(DEC_B):
                if b == 3:
                    rec_row(NT)
                dve.wait_ge(so_ps, b + 1)
                for hd in range(HEADS):
                    c = slice(hd * P, (hd + 1) * P)
                    g = hd * DEC_B + b
                    ins = stt(out=Sout[:, b, c], in0=S0[:, b, c], scalar=eL[:, 0, g:g + 1], in1=lps[b % 2][:, c],
                              op0=ALU.mult, op1=ALU.add)
                ins.then_inc(so_ok, 1)

        @block.tensor
        def _(pe):
            def turn(t):
                pe.wait_ge(h_ok, t + 1)
                wait(pe, hT_act, t)
                wait(pe, hT_dve, t)
                for c in range(DC):
                    mm = pe.transpose(hps[:, c // 4, (c % 4) * P:(c % 4 + 1) * P], h[:, c * P:(c + 1) * P], ident[:, :])
                mm.then_inc(hT_ps, 1)

            def group(t, u, j, middle=None):
                pe.wait_ge(z_dve if j % 2 else z_act, 4 * t + j // 2 + 1)
                out = zps[j % 2]
                if j == KT:
                    pe.wait_ge(z_dve, 4 * t + KA // 2 + 2)
                    for hd in range(HEADS):
                        mm = pe.transpose(out[:, hd * P:(hd + 1) * P], z[:, KA, hd * P:(hd + 1) * P], ident[:, :])
                    mm.then_inc(z_ps, 1)
                    return
                g = W_COL[j]
                if isinstance(t, int) and t == 0:
                    pe.wait_ge(w_in[g], 16)
                if j in CHANNEL_MAJOR:
                    for hd in range(HEADS):
                        for c in range(DC):
                            col = g * HW + hd * P
                            mm = pe.matmul(out[:, hd * P:(hd + 1) * P], w[:, c, col:col + P], hT[:, u, c, :],
                                           start=(c == 0), stop=(c == DC - 1))
                else:
                    for c in range(DC):
                        if middle and c == DC // 2:
                            middle()
                        mm = pe.matmul(out[:, :], hT[:, u, c, :], w[:, c, g * HW:(g + 1) * HW],
                                       start=(c == 0), stop=(c == DC - 1))
                mm.then_inc(z_ps, 1)

            def level(t, u, pos):
                wait(pe, cp_ok, 8 * t + pos - 1)
                if pos == 0:
                    pe.wait_ge(qk_ok, t + 1)
                    left, right = k[:, u, :], q[:, u, :]
                else:
                    pe.wait_ge(X_ok, 7 * t + pos)
                    left = right = X[:, (u + pos - 1) % 2, :]
                for hd in range(HEADS):
                    c = slice(hd * P, (hd + 1) * P)
                    mm = pe.matmul(lps[pos % 2][:, c], left[:, c], right[:, c], start=True, stop=True)
                mm.then_inc(lv_ps, 1)

            def turn_kd(t):
                pe.wait_ge(qek_ok, t + 1)
                pe.wait_ge(s_ok, t + 1)
                for hd in range(HEADS):
                    c = slice(hd * P, (hd + 1) * P)
                    mm = pe.transpose(mps[:, c], kd[:, c], ident[:, :])
                mm.then_inc(kdt_ps, 1)

            def rec_out(t, u):
                pe.wait_ge(cp_ok, 8 * t + 8 if not is_last(t) else 8 * NT + len(levels(NT)))
                wait(pe, orow_ok, t)
                pe.wait_ge(s_ok, t + 1)
                for hd in range(HEADS):
                    c = slice(hd * P, (hd + 1) * P)
                    pe.matmul(ops[:, c], A[:, c], ir[:, u, c], start=True, stop=False)
                    if is_last(t):
                        for b in range(DEC_B):
                            mm = pe.matmul(ops[:, c], qez[:, b, c], S0[:, b, c], start=False, stop=(b == DEC_B - 1))
                    else:
                        mm = pe.matmul(ops[:, c], qe[:, u, c], S[:, c], start=False, stop=True)
                mm.then_inc(o_ps, 1)

            def new_state(t, u):
                pe.wait_ge(kdt_ok, t + 1)
                for hd in range(HEADS):
                    c = slice(hd * P, (hd + 1) * P)
                    mm = pe.matmul(mps[:, c], kdT[:, c], ir[:, u, c], start=True, stop=True)
                mm.then_inc(st_ps, 1)

            def tile(t, u, rec=True):
                pe.wait_ge(hT_act, t + 1)
                pe.wait_ge(hT_dve, t + 1)
                g, v = t - 1, 1 - u
                for j in range(8):
                    if j == GR and rec:
                        group(t, u, j, lambda: level(g, v, j))
                        rec_out(g, v)
                        new_state(g, v)
                        continue
                    group(t, u, j)
                    if j == KT and not is_last(t):
                        turn(t + 1)
                    if rec:
                        level(g, v, j)
                        if j == FR:
                            turn_kd(g)

            pe.wait_ge(consts["sem"], consts["n"])
            turn(0)
            tile(0, 0, False)
            tile(1, 1)
            with pe.Fori(1, NT // 2) as i:
                for u in range(2):
                    tile(i * 2 + u, u)
            tile(NT, 0)
            for pos, m in levels(NT):
                level(NT, 0, pos)
            turn_kd(NT)
            pe.wait_ge(S0_in, 16 * DEC_B)
            pe.wait_ge(qzf_ok, 1)
            pe.wait_ge(z_act, 4 * TILES + 1)
            rec_out(NT, 0)
            pe.wait_ge(kz_ok, 1)
            for b in range(DEC_B):
                wait(pe, so_ok, b - 1)
                for hd in range(HEADS):
                    c = slice(hd * P, (hd + 1) * P)
                    mm = pe.matmul(lps[b % 2][:, c], kdz[:, b, c], ir[:, 0, c], start=True, stop=True)
                mm.then_inc(so_ps, 1)


def seg_of(i):
    return [(4 * s, min(4, i + 1 - 4 * s)) for s in range(i // 4 + 1)]


def attend(nc, dr, consts):
    ident = consts["ident"]
    scale = 64 ** -0.5
    NSEG = [len(seg_of(i)) for i in range(NT)]
    BASE = [sum(NSEG[:i]) for i in range(NT)]
    PER_HEAD = sum(NSEG)
    GROUPS = [0, 2, 6, NT]

    def tile_before(h, i, back):
        i -= back
        if i >= 0:
            return h, i, NSEG[i] if i < NT else 0
        return h - 1, i + NT, 0 if isinstance(h, int) and h == 0 else NSEG[i + NT]

    def each_head(eng, step, chain=None, per_head=0):
        for i in range(NT):
            step(0, i)
        with eng.Fori(1, HEADS) as h:
            if chain:
                chain.loop(h - 1, per_head)
            for i in range(NT):
                step(h, i)
        if chain:
            chain.end_loop(HEADS - 1)
        for i in range(NT, NT + 3):
            step(HEADS - 1, i)

    def wait_loaded(eng, groups, rest, h, i):
        if isinstance(h, int) and h == 0:
            if i in GROUPS:
                eng.wait_ge(groups[GROUPS.index(i)], 16)
        elif i == 0:
            eng.wait_ge(rest, 16)

    with ExitStack() as ctx:
        sb = lambda n, s, d=F32: ctx.enter_context(nc.sbuf_tensor(n, s, d))
        ps = lambda n, s, d=F32: ctx.enter_context(nc.psum_tensor(n, s, d))
        sem = stage_semaphores(nc, ctx)
        q = sb("att_q", [P, NT, HW])
        k = sb("att_k", [P, NT, HW])
        v = sb("att_v", [P, NT, HW])
        qz = sb("q_by_map", [P, 2, 2, P])
        pr = sb("probs", [P, 4, 2, SEQ])
        wT = sb("weights_T", [P, 2, HW])
        o = sb("att_o", [P, 2, P])
        nmax = sb("neg_max", [P, 2, 2, 4])
        zsum = sb("seg_sum", [P, 2, 2, 4])
        fac = sb("seg_factor", [P, 2, 2, 4])
        tot = sb("row_stats", [P, 2, 6])
        coef = sb("map_coef", [P, 2])
        lamv = sb("lam_rows", [P, 4, 64])
        lamd = sb("lam_dots", [P, 4])
        sps = [ps(f"score_psum{s}", [P, 2, HW]) for s in range(2)]
        tps = [ps(f"weights_T_psum{s}", [P, HW]) for s in range(2)]
        ops = [ps(f"att_out_psum{s}", [P, HW]) for s in range(2)]

        q_in, k_in, v_in = ([sem(f"att_{n}_loaded{g}") for g in range(len(GROUPS) - 1)] for n in "qkv")
        q_rest, k_rest, v_rest = (sem(f"att_{n}_other_heads_loaded") for n in "qkv")
        lam_in, lam_e = sem("lam_loaded"), sem("lam_exp")
        dve_step = sem("p2_dve_step")
        qz_ok, s_ps, m_ok, e_ok = sem("q_maps_ready"), sem("scores_in_psum"), sem("seg_max_ready"), sem("seg_exp_ready")
        nM_ok, ef_ok, w_ok = sem("row_max_ready"), sem("seg_factor_exp"), sem("weights_ready")
        tg_ps, wt_sb, pv, wt_tile = sem("weights_T_in_psum"), sem("weights_T_copied"), sem("pv_done"), sem("probs_used")
        o_ok, o_free = sem("att_o_ready"), sem("att_o_free")
        att_out = [sem(f"att_stored{s}") for s in range(2)]
        fac_ok, w1_ok, stand = sem("factors_ready"), sem("second_map_weighed"), sem("p2_pool_stand")
        block = ctx.enter_context(nc.Block())
        vp = dr["v_prompt"].rearrange("l b (t p) h d -> (l b t) p (h d)", p=P)

        @block.sync
        def _(sp):
            for n, name in enumerate(("lam_q1", "lam_k1", "lam_q2", "lam_k2")):
                sp.dma_start(lamv[:, n, :], dr[name].to_broadcast([P, 64])).then_inc(lam_in, 16)
            tensors = ((q, dr["z"][QA], (q_in, q_rest)), (k, dr["z"][KT], (k_in, k_rest)), (v, vp, (v_in, v_rest)))
            for g in range(len(GROUPS) - 1):
                c = slice(GROUPS[g], GROUPS[g + 1])
                for buf, src, arrived in tensors:
                    sp.dma_start(buf[:, c, 0:P], src[c].rearrange("t p d -> p t d")[:, :, 0:P]).then_inc(arrived[0][g], 16)
            for buf, src, arrived in tensors:
                sp.dma_start(buf[:, :, P:HW], src[0:NT].rearrange("t p d -> p t d")[:, :, P:HW]).then_inc(arrived[1], 16)
            att = dr["att"]
            with sp.Fori(0, HEADS) as h:
                for i in range(NT):
                    sp.wait_ge(o_ok, h * NT + i + 1)
                    sp.dma_start(att[i][:, bass.ds(h * P, P)], o[:, i % 2, :]).then_inc(att_out[i % 2], 16)
                    sp.wait_ge(att_out[i % 2], (h * (NT // 2) + i // 2) * 16 + 16)
                    sp.sem_inc(o_free, 1)

        @block.gpsimd
        def _(pool):
            with pool.Fori(0, HEADS) as h:
                for i in range(NT):
                    pool.wait_ge(fac_ok, h * NT + i + 1)
                    for s in range(NSEG[i]):
                        k0, kw = seg_of(i)[s]
                        p1 = pr[:, i % 4, 1, k0 * P:(k0 + kw) * P]
                        pool.sem_inc(stand, 1)
                        pool.tensor_scalar(p1, p1, fac[:, i % 2, 1, s:s + 1], 1.0, ALU.mult, ALU.mult).then_inc(w1_ok, 1)

        @block.scalar
        def _(act):
            act.sem_inc(e_ok, 2)
            act.sem_inc(wt_sb, 2)
            act.wait_ge(lam_e, 1)
            nc.scalar.activation(lamd[:, 0:2], lamd[:, 2:4], ACT.Exp).then_inc(lam_e, 1)

            def expo(h, i, s):
                n = h * PER_HEAD + BASE[i] + s
                k0, kw = seg_of(i)[s]
                if s == 0:
                    wait(act, wt_tile, h * NT + i - 3)
                act.wait_ge(m_ok, n + 1)
                for c in range(2):
                    ins = nc.scalar.activation(pr[:, i % 4, c, k0 * P:(k0 + kw) * P], sps[(BASE[i] + s) % 2][:, c, 0:kw * P],
                                               ACT.Exp, bias=nmax[:, i % 2, c, s:s + 1], accum_out=zsum[:, i % 2, c, s:s + 1])
                ins.then_inc(e_ok, 1)

            def factor(h, i):
                act.wait_ge(nM_ok, h * NT + i + 1)
                for c in range(2):
                    ins = nc.scalar.activation(fac[:, i % 2, c, 0:NSEG[i]], nmax[:, i % 2, c, 0:NSEG[i]], ACT.Exp,
                                               scale=-1.0, bias=tot[:, i % 2, c:c + 1])
                ins.then_inc(ef_ok, 1)

            def copy_T(h, i, s):
                n = h * PER_HEAD + BASE[i] + s
                kw = seg_of(i)[s][1]
                act.wait_ge(tg_ps, n + 1)
                act.wait_ge(pv, n + 1)
                r = (BASE[i] + s) % 2
                nc.scalar.copy(wT[:, r, 0:kw * P], tps[r][:, 0:kw * P]).then_inc(wt_sb, 1)

            def step(h, i):
                cur = NSEG[i] if i < NT else 0
                h3, i3, old = tile_before(h, i, 3)
                for s in range(max(cur + 1, old)):
                    if s < old:
                        copy_T(h3, i3, s)
                    if 1 <= s <= cur:
                        expo(h, i, s - 1)
                if cur:
                    factor(h, i)

            each_head(act, step)

        @block.vector
        def _(dve):
            chain = Chain(dve, dve_step)
            tt, ts, stt = nc.vector.tensor_tensor, nc.vector.tensor_scalar, nc.vector.scalar_tensor_tensor
            red = nc.vector.tensor_reduce
            dve.sem_inc(o_free, 2)
            dve.wait_ge(lam_in, 64)
            chain.after(tt(lamv[:, 0:4:2, :], lamv[:, 0:4:2, :], lamv[:, 1:4:2, :], ALU.mult))
            red(lamd[:, 2:4], lamv[:, 0:4:2, :], AX.X, ALU.add).then_inc(lam_e, 1)
            chain.after(nc.vector.memset(coef[:, :], 1.0))
            chain.after(nc.vector.memset(qz[:, :, :, :], 0.0))
            dve.wait_ge(lam_e, 2)
            tt(coef[:, 1:2], lamd[:, 1:2], lamd[:, 0:1], ALU.subtract).then_inc(lam_e, 1)
            dve.wait_ge(lam_e, 3)
            chain.after(ts(coef[:, 1:2], coef[:, 1:2], -LAM_INIT, None, ALU.add))

            def maps(h, i):
                wait_loaded(dve, q_in, q_rest, h, i)
                wait(dve, s_ps, h * PER_HEAD + (BASE[i - 1] if i else -NSEG[NT - 1]))
                for c in range(2):
                    r = slice(64 * c, 64 * c + 64)
                    ins = ts(qz[r, i % 2, c, :], q[r, i, bass.ds(h * P, P)], scale, None, ALU.mult)
                ins.then_inc(qz_ok, 1)

            def seg_max(h, i, s):
                n = h * PER_HEAD + BASE[i] + s
                kw = seg_of(i)[s][1]
                sp_ = sps[(BASE[i] + s) % 2]
                dve.wait_ge(s_ps, n + 1)
                if s == NSEG[i] - 1:
                    chain.after(nc.vector.memset(sp_[0:64, :, kw * P - 64:kw * P], HIDDEN))
                red(nmax[:, i % 2, :, s:s + 1], sp_[:, :, 0:kw * P], AX.X, ALU.max, negate=True).then_inc(m_ok, 1)

            def row_max(h, i):
                dve.wait_ge(m_ok, h * PER_HEAD + BASE[i] + NSEG[i])
                red(tot[:, i % 2, 0:2], nmax[:, i % 2, :, 0:NSEG[i]], AX.X, ALU.min).then_inc(nM_ok, 1)

            def factors(h, i):
                n, b = NSEG[i], i % 2
                dve.wait_ge(ef_ok, h * NT + i + 1)
                dve.wait_ge(e_ok, h * PER_HEAD + BASE[i] + n + 2)
                chain.after(tt(zsum[:, b, :, 0:n], zsum[:, b, :, 0:n], fac[:, b, :, 0:n], ALU.mult))
                chain.after(red(tot[:, b, 2:4], zsum[:, b, :, 0:n], AX.X, ALU.add))
                chain.after(nc.vector.reciprocal(tot[:, b, 4:6], tot[:, b, 2:4]))
                chain.after(tt(tot[:, b, 2:4], tot[:, b, 4:6], coef[:, :], ALU.mult))
                for c in range(2):
                    ins = ts(fac[:, b, c, 0:n], fac[:, b, c, 0:n], tot[:, b, 2 + c:3 + c], None, ALU.mult)
                ins.then_inc(fac_ok, 1)

            def weigh(h, i, s):
                b, r = i % 2, i % 4
                k0, kw = seg_of(i)[s]
                c = slice(k0 * P, (k0 + kw) * P)
                dve.wait_ge(w1_ok, h * PER_HEAD + BASE[i] + s + 1)
                stt(out=pr[:, r, 0, c], in0=pr[:, r, 0, c], scalar=fac[:, b, 0, s:s + 1], in1=pr[:, r, 1, c],
                    op0=ALU.mult, op1=ALU.add).then_inc(w_ok, 1)

            def out_row(h, i):
                dve.wait_ge(pv, h * PER_HEAD + BASE[i] + NSEG[i] + 2)
                dve.wait_ge(o_free, h * NT + i + 1)
                nc.vector.tensor_copy(o[:, i % 2, :], ops[i % 2][:, 0:P]).then_inc(o_ok, 1)

            steps = 4 * NT + NT
            def step(h, i):
                cur = NSEG[i] if i < NT else 0
                h1, i1, mid = tile_before(h, i, 1)
                h4, i4, done = tile_before(h, i, 4)
                if i == 0:
                    maps(h, 0)
                if i + 1 < NT:
                    maps(h, i + 1)
                if mid:
                    factors(h1, i1)
                if cur:
                    seg_max(h, i, 0)
                for s in range(max(cur - 1, mid)):
                    if s + 1 < cur:
                        seg_max(h, i, s + 1)
                    if s < mid:
                        weigh(h1, i1, s)
                if cur:
                    row_max(h, i)
                if done:
                    out_row(h4, i4)

            each_head(dve, step, chain, steps)
            out_row(HEADS - 1, NT - 1)

        @block.tensor
        def _(pe):
            pe.sem_inc(pv, 2)

            def scores(h, i, s):
                n = h * PER_HEAD + BASE[i] + s
                k0, kw = seg_of(i)[s]
                if s == 0:
                    pe.wait_ge(qz_ok, h * NT + i + 1)
                    wait_loaded(pe, k_in, k_rest, h, i)
                pe.wait_ge(e_ok, n + 1)
                for c in range(2):
                    mm = pe.matmul(sps[(BASE[i] + s) % 2][:, c, 0:kw * P], qz[:, i % 2, c, :],
                                   k[:, k0:k0 + kw, bass.ds(h * P, P)], start=True, stop=True)
                mm.then_inc(s_ps, 1)

            def turn(h, i, s):
                n = h * PER_HEAD + BASE[i] + s
                k0, kw = seg_of(i)[s]
                pe.wait_ge(w_ok, n + 1)
                pe.wait_ge(wt_sb, n + 1)
                for b in range(kw):
                    mm = pe.transpose(tps[(BASE[i] + s) % 2][:, b * P:(b + 1) * P],
                                      pr[:, i % 4, 0, (k0 + b) * P:(k0 + b + 1) * P], ident[:, :])
                mm.then_inc(tg_ps, 1)
                if s == NSEG[i] - 1:
                    pe.wait_ge(tg_ps, n + 1)
                    pe.sem_inc(wt_tile, 1)

            def weighted(h, i, s):
                n = h * PER_HEAD + BASE[i] + s
                k0, kw = seg_of(i)[s]
                if s == 0:
                    wait_loaded(pe, v_in, v_rest, h, i)
                    wait(pe, o_ok, h * NT + i - 1)
                pe.wait_ge(wt_sb, n + 3)
                for b in range(kw):
                    mm = pe.matmul(ops[i % 2][:, 0:P], wT[:, (BASE[i] + s) % 2, b * P:(b + 1) * P],
                                   v[:, k0 + b, bass.ds(h * P, P)], start=(s == 0 and b == 0),
                                   stop=(s == NSEG[i] - 1 and b == kw - 1))
                mm.then_inc(pv, 1)

            def step(h, i):
                cur = NSEG[i] if i < NT else 0
                h3, i3, old = tile_before(h, i, 3)
                for s in range(max(cur, old)):
                    if s < old:
                        turn(h3, i3, s)
                    if s < cur:
                        scores(h, i, s)
                    if 0 < s < old:
                        weighted(h3, i3, s - 1)
                if old:
                    weighted(h3, i3, old - 1)

            each_head(pe, step)


def attend_sample(nc, dr, consts, pre):
    ident = consts["ident"]
    scale = 64 ** -0.5
    WIN = P + DEC
    with ExitStack() as ctx:
        sb = lambda n, s, d=F32: ctx.enter_context(nc.sbuf_tensor(n, s, d))
        ps = lambda n, s, d=F32: ctx.enter_context(nc.psum_tensor(n, s, d))
        sem = stage_semaphores(nc, ctx)
        q, kn, vn = sb("smp_q", [P, HW]), sb("smp_k", [P, HW]), sb("smp_v", [P, HW])
        kc, vc = sb("cache_k_sb", [P, DEC_B, HW]), sb("cache_v_sb", [P, DEC_B, HW])
        kcT = sb("cache_k_T", [P, 2, DEC_B, P])
        qw = sb("q_windows", [P, 2, 2, DEC_B * WIN])
        qz = sb("smp_q_by_map", [P, 2, 2, P])
        hide = sb("hide_others", [P, 2 * P])
        s_sb = sb("smp_scores", [P, 2, 2, 2 * P])
        nM, zs, rz = sb("smp_neg_max", [P, 2, 2]), sb("smp_sum", [P, 2, 2]), sb("smp_factor", [P, 2, 2])
        ww = sb("weight_windows", [P, DEC_B * WIN])
        wn = sb("new_weights_T", [P, P])
        coef = sb("smp_coef", [P, 2])
        lamv = sb("smp_lam_rows", [P, 4, 64])
        lamd = sb("smp_lam_dots", [P, 4])
        orow = sb("smp_o", [P, HW])
        kps = ps("cache_k_T_psum", [P, 2, HW])
        sps = [ps(f"smp_score_psum{u}", [P, 2, HW]) for u in range(2)]
        tps = ps("smp_weights_T_psum", [P, HW])
        ops = ps("smp_out_psum", [P, HW])
        lam_in, new_in, pre_in = sem("smp_lam_loaded"), sem("smp_new_loaded"), sem("stage4_weights_loaded")
        kc_in = [sem(f"cache_k_loaded{h}") for h in range(HEADS)]
        vc_in = [sem(f"cache_v_loaded{h}") for h in range(HEADS)]
        step, lam_e, hide_ok = sem("p3_dve_step"), sem("smp_lam_exp"), sem("hide_ready")
        pool_step = sem("p3_pool_step")
        qz_ok, kT_ps, kT_ok, s_ps = sem("smp_q_ready"), sem("cache_k_T_in_psum"), sem("cache_k_T_ready"), sem("smp_scores_in_psum")
        m_ok, e_ok, w_ok, t_ps, t_ok = sem("smp_max_ready"), sem("smp_exp_ready"), sem("smp_weights_ready"), sem("smp_T_in_psum"), sem("smp_T_ready")
        o_ps, o_ok, o_out = sem("smp_o_in_psum"), sem("smp_o_ready"), sem("smp_o_stored")
        block = ctx.enter_context(nc.Block())

        @block.sync
        def _(sp):
            for n, name in enumerate(("lam_q1", "lam_k1", "lam_q2", "lam_k2")):
                sp.dma_start(lamv[:, n, :], dr[name].to_broadcast([P, 64])).then_inc(lam_in, 16)
            sp.dma_start(q[:, :], dr["z"][QA][NT]).then_inc(new_in, 16)
            sp.dma_start(kn[:, :], dr["z"][KT][NT]).then_inc(new_in, 16)
            sp.dma_start(vn[:, :], dr["v_sample"].rearrange("l b t h d -> (l b t) (h d)")).then_inc(new_in, 16)
            for h in range(HEADS):
                c = slice(h * P, (h + 1) * P)
                sp.dma_start(kc[:, :, c], dr["cache_k"].rearrange("l b t h d -> t (l b) (h d)")[:, :, c]).then_inc(kc_in[h], 16)
                sp.dma_start(vc[:, :, c], dr["cache_v"].rearrange("l b t h d -> t (l b) (h d)")[:, :, c]).then_inc(vc_in[h], 16)
            sp.dma_start(pre["sub"][:, :], dr["subln_w"].to_broadcast([P, P])).then_inc(pre_in, 16)
            sp.dma_start(pre["wo"][:, :, :], dr["w_out"].rearrange("l (c p) n -> p (l c) n", p=P)).then_inc(pre_in, 16)
            sp.dma_start(pre["n2"][:, :], dr["norm2_w"].to_broadcast([P, D])).then_inc(pre_in, 16)
            with nc.allow_non_contiguous_dma(reason="router columns are short rows"):
                sp.dma_start(pre["wr"][:, :, 0:N_GRP], dr["w_group"].rearrange("l (c p) n -> p (l c) n", p=P)).then_inc(pre_in, 16)
                sp.dma_start(pre["wr"][:, :, N_GRP:LOGITS], dr["w_router"].rearrange("l (c p) n -> p (l c) n", p=P)).then_inc(pre_in, 16)
            sp.wait_ge(o_ok, HEADS)
            sp.dma_start(dr["att"][NT], orow[:, :]).then_inc(o_out, 16)
            sp.wait_ge(pre_in, 16 * 5)
            sp.wait_ge(o_out, 16)

        @block.gpsimd
        def _(pool):
            chain = Chain(pool, pool_step)
            pool.memset(ww[:, :], 0.0)
            chain.after(pool.memset(hide[:, :], 0.0))
            own = hide[:, P:2 * P].rearrange("p (b r) -> p b r", r=DEC)
            chain.after(pool.affine_select(out=own, in_=own, compare_op=ALU.is_ge, fill=HIDDEN, base=0,
                                           pattern=[[-DEC, DEC_B], [0, DEC]], channel_multiplier=1))
            pool.affine_select(out=own, in_=own, compare_op=ALU.is_ge, fill=HIDDEN, base=DEC - 1,
                               pattern=[[DEC, DEC_B], [0, DEC]], channel_multiplier=-1).then_inc(hide_ok, 1)

        @block.scalar
        def _(act):
            act.wait_ge(lam_e, 1)
            nc.scalar.activation(lamd[:, 0:2], lamd[:, 2:4], ACT.Exp).then_inc(lam_e, 1)

            def copy_kT(h):
                act.wait_ge(kT_ps, h + 1)
                nc.scalar.copy(kcT[:, h % 2, :, :].rearrange("p b t -> p (b t)"),
                               kps[:, :, :].rearrange("p a n -> p (a n)")).then_inc(kT_ok, 1)

            copy_kT(0)
            copy_kT(1)
            for h in range(HEADS):
                u = h % 2
                act.wait_ge(m_ok, h + 1)
                for c in range(2):
                    ins = nc.scalar.activation(s_sb[:, u, c, :], s_sb[:, u, c, :], ACT.Exp, bias=nM[:, u, c:c + 1],
                                               accum_out=zs[:, u, c:c + 1])
                ins.then_inc(e_ok, 1)
                if h + 2 < HEADS:
                    copy_kT(h + 2)

        @block.vector
        def _(dve):
            chain = Chain(dve, step)
            tt, ts, stt = nc.vector.tensor_tensor, nc.vector.tensor_scalar, nc.vector.scalar_tensor_tensor
            red = nc.vector.tensor_reduce
            nc.vector.memset(coef[:, :], 1.0)
            nc.vector.memset(qz[:, :, :, :], 0.0)
            chain.after(nc.vector.memset(qw[:, :, :, :], 0.0))
            dve.wait_ge(lam_in, 64)
            chain.after(tt(lamv[:, 0:4:2, :], lamv[:, 0:4:2, :], lamv[:, 1:4:2, :], ALU.mult))
            red(lamd[:, 2:4], lamv[:, 0:4:2, :], AX.X, ALU.add).then_inc(lam_e, 1)
            dve.wait_ge(lam_e, 2)
            tt(coef[:, 1:2], lamd[:, 1:2], lamd[:, 0:1], ALU.subtract).then_inc(lam_e, 1)
            dve.wait_ge(lam_e, 3)
            chain.after(ts(coef[:, 1:2], coef[:, 1:2], -LAM_INIT, None, ALU.add))
            dve.wait_ge(new_in, 48)
            dve.wait_ge(hide_ok, 1)

            def queries(h):
                hc, u = slice(h * P, (h + 1) * P), h % 2
                wait(dve, s_ps, h - 1)
                for c in range(2):
                    r = slice(64 * c, 64 * c + 64)
                    ts(qz[r, u, c, :], q[r, hc], scale, None, ALU.mult)
                    own = qw[r, u, c, :].rearrange("p (b r) -> p b r", r=WIN)[:, :, 0:DEC]
                    ins = ts(own, q[r, hc].rearrange("p (b r) -> p b r", r=DEC), scale, None, ALU.mult)
                ins.then_inc(qz_ok, 1)

            def out_row(h):
                hc = slice(h * P, (h + 1) * P)
                dve.wait_ge(o_ps, h + 1)
                nc.vector.tensor_copy(orow[:, hc], ops[:, hc]).then_inc(o_ok, 1)

            queries(0)
            queries(1)
            for h in range(HEADS):
                u = h % 2
                dve.wait_ge(s_ps, h + 1)
                for c in range(2):
                    ins = tt(s_sb[:, u, c, :], sps[u][:, c, 0:2 * P], hide[:, :], ALU.add)
                chain.after(ins)
                red(nM[:, u, :], s_sb[:, u, :, :], AX.X, ALU.max, negate=True).then_inc(m_ok, 1)
                dve.wait_ge(e_ok, h + 1)
                chain.after(nc.vector.reciprocal(rz[:, u, :], zs[:, u, :]))
                chain.after(tt(rz[:, u, :], rz[:, u, :], coef[:, :], ALU.mult))
                chain.after(ts(s_sb[:, u, 1, :], s_sb[:, u, 1, :], rz[:, u, 1:2], None, ALU.mult))
                stt(out=s_sb[:, u, 0, :], in0=s_sb[:, u, 0, :], scalar=rz[:, u, 0:1], in1=s_sb[:, u, 1, :], op0=ALU.mult,
                    op1=ALU.add).then_inc(w_ok, 1)
                if h + 2 < HEADS:
                    queries(h + 2)
                if h >= 1:
                    out_row(h - 1)
                dve.wait_ge(t_ps, h + 1)
                nc.vector.tensor_copy(ww[:, :].rearrange("p (b r) -> p b r", r=WIN)[:, :, 0:DEC],
                                      tps[:, 0:P].rearrange("p (b r) -> p b r", r=DEC))
                nc.vector.tensor_copy(wn[:, :], tps[:, P:2 * P]).then_inc(t_ok, 1)
            out_row(HEADS - 1)

        @block.tensor
        def _(pe):
            def keys(h):
                hc = slice(h * P, (h + 1) * P)
                pe.wait_ge(kc_in[h], 16)
                wait(pe, kT_ok, h)
                for b in range(DEC_B):
                    mm = pe.transpose(kps[:, b // 4, (b % 4) * P:(b % 4 + 1) * P], kc[:, b, hc], ident[:, :])
                mm.then_inc(kT_ps, 1)

            def scores(h):
                hc, u = slice(h * P, (h + 1) * P), h % 2
                pe.wait_ge(kT_ok, h + 1)
                pe.wait_ge(qz_ok, h + 1)
                pe.wait_ge(new_in, 48)
                wait(pe, m_ok, h - 1)
                for c in range(2):
                    for b in range(DEC_B):
                        pe.matmul(sps[u][:, c, 0:P], qw[:, u, c, b * P:(b + 1) * P], kcT[:, u, b, :],
                                  start=(b == 0), stop=(b == DEC_B - 1))
                    mm = pe.matmul(sps[u][:, c, P:2 * P], qz[:, u, c, :], kn[:, hc], start=True, stop=True)
                mm.then_inc(s_ps, 1)

            def turn(h):
                pe.wait_ge(w_ok, h + 1)
                wait(pe, t_ok, h)
                for b in range(2):
                    mm = pe.transpose(tps[:, b * P:(b + 1) * P], s_sb[:, h % 2, 0, b * P:(b + 1) * P], ident[:, :])
                mm.then_inc(t_ps, 1)

            def weighted(h):
                hc = slice(h * P, (h + 1) * P)
                pe.wait_ge(t_ok, h + 1)
                pe.wait_ge(vc_in[h], 16)
                for b in range(DEC_B):
                    pe.matmul(ops[:, hc], ww[:, b * P:(b + 1) * P], vc[:, b, hc], start=(b == 0), stop=False)
                mm = pe.matmul(ops[:, hc], wn[:, :], vn[:, hc], start=False, stop=True)
                mm.then_inc(o_ps, 1)

            keys(0)
            scores(0)
            keys(1)
            for h in range(HEADS):
                if h + 1 < HEADS:
                    scores(h + 1)
                if h + 2 < HEADS:
                    keys(h + 2)
                turn(h)
                weighted(h)


def mix_and_route(nc, dr, consts, keep, pre):
    ident = consts["ident"]
    y, gates, trips, last_run = keep["y"], keep["gates"], keep["trips"], keep["last_run"]
    slot_all, tok_all = keep["slot_all"], keep["tok_all"]
    with ExitStack() as ctx:
        sb = lambda n, s, d=F32: ctx.enter_context(nc.sbuf_tensor(n, s, d))
        ps = lambda n, s, d=F32: ctx.enter_context(nc.psum_tensor(n, s, d))
        sem = stage_semaphores(nc, ctx)
        wo, wr, n2, sub = pre["wo"], pre["wr"], pre["n2"], pre["sub"]
        m = sb("mix", [P, 2, D])
        x = sb("x_res", [P, 2, D])
        mT = sb("mix_T", [P, 2, DC, P])
        h = sb("h2", [P, 2, D])
        hT = sb("h2_T", [P, DC, P])
        junk = sb("square_out4", [P, D], BF16)
        ast = sb("att_stats", [P, 2, 12])
        st = sb("norm2_stats", [P, 4])
        zero = sb("zero_rows", [PAD_ROWS, D])
        glog = sb("group_logits", [P, 8])
        elog = sb("expert_logits", [P, N_EXP])
        elm = sb("masked_logits", [P, N_EXP])
        gtop, etop = sb("group_top", [P, 8]), sb("expert_top", [P, 8])
        gidx, eidx = sb("group_index", [P, 8], U32), sb("expert_index", [P, 8], U32)
        sel = sb("selected", [P, 4])
        rt = sb("route_tmp", [P, 8])
        oh = sb("one_hot", [P, 2, 2, N_EXP])
        both = sb("both_hot", [P, 2, N_EXP])
        place = sb("place", [P, N_EXP])
        hit = sb("hit", [P, 2, N_EXP])
        pos = sb("position", [P, 2])
        posi = sb("position_index", [P, 2, 2], U32)
        slot_now = sb("slot_now", [P, 2, 2], U32)
        cnt = sb("expert_count", [P, N_EXP])
        slot = sb("slot_number", [P, TILES, 2], U32)
        init = sb("table_init", [109, 5, P], U32)
        e_of = sb("expert_row", [P, N_EXP])
        g_of = sb("group_row", [P, N_EXP])
        q_of = sb("queue_start_row", [P, N_EXP])
        tri = sb("earlier_tokens", [P, P])
        ones = sb("ones", [P, P])
        full = sb("entry_there", [P, N_EXP, TILES])
        rank = sb("entry_rank", [P, N_EXP * TILES])
        en_of = sb("entry_number", [P, N_EXP * TILES])
        ee_of = sb("entry_expert", [P, N_EXP, TILES])
        th_of = sb("entry_start", [P, TILES])
        one_row = sb("one_row", [P, N_EXP * TILES])
        me = sb("list_place", [P, 1])
        lst = sb("block_list", [P, 4])
        run_rank = sb("run_rank", [P, N_EXP])
        run_hit = sb("run_hit", [P, N_EXP])
        run_row = sb("run_row", [P, N_EXP])
        lists = sb("run_lists", [P, 4])
        half = sb("half_run", [P, 1], I32)
        blk_at = sb("block_queue_row", [P, 1], U32)
        blk_rows = sb("block_queue_rows", [P, P], U32)
        blk = sb("block_queue_floats", [P, P])

        mps = ps("mix_T_psum", [P, 2, HW])
        yps = ps("y_psum", [P, 2, HW])
        hps = ps("h2_T_psum", [P, 2, HW])
        lps = ps("logit_psum", [P, HW])
        rps = ps("rank_psum", [P, 2, N_EXP])

        m_in = [sem(f"mix_loaded{u}") for u in range(2)]
        x_in = [sem(f"residual_loaded{u}") for u in range(2)]
        act_step, dve_step, pool_step = sem("p4_act_step"), sem("p4_dve_step"), sem("p4_pool_step")
        iota_ok, tab_out = sem("route_consts_ready"), sem("table_initialised")
        ar_ok, mix_ok, mT_ps, mT_act, mT_dve = sem("att_rstd"), sem("mix_ready"), sem("mix_T_in_psum"), sem("mix_T_half0"), sem("mix_T_half1")
        y_ps, y_ok, r_ok, h_ok, h_free, h_out = sem("y_in_psum"), sem("y_ready"), sem("norm2_rstd"), sem("h2_ready"), sem("h2_free"), sem("h2_stored")
        hT_ps, hT_act, hT_dve, lg_ps = sem("h2_T_in_psum"), sem("h2_T_half0"), sem("h2_T_half1"), sem("logits_in_psum")
        gm_ok, ge_ok, ev_ok, ee_ok = sem("group_max"), sem("group_exp"), sem("expert_top2"), sem("gate_exp")
        both_ok, rk_ps, pos_ok, sc_free = sem("one_hots_ready"), sem("ranks_in_psum"), sem("positions_ready"), sem("positions_free")
        sc_out = sem("table_scattered")
        stand, pool_stand = sem("dve_stand"), sem("pool_stand")
        blk_in, blk_ok, blk_ps = sem("block_rows_loaded"), sem("block_rows_as_floats"), sem("block_rows_in_psum")
        lst_ok, lst_ps, zero_ok = sem("list_ready"), sem("list_in_psum"), sem("zero_rows_ready")
        block = ctx.enter_context(nc.Block())
        xp = dr["x_prompt"].rearrange("b (t p) d -> (b t) p d", p=P)
        h2 = dr["h2"][0:TILES * P].rearrange("(t p) d -> t p d", p=P)
        STEPS = TILES + 2

        def steps(eng, step, chain=None, per_step=0, last=NT):
            step(0, 0)
            step(1, 1)
            with eng.Fori(1, last // 2) as i:
                if chain:
                    chain.loop(i - 1, 2 * per_step)
                for u in range(2):
                    step(i * 2 + u, u)
            if chain:
                chain.end_loop(last // 2 - 1)
            for t in range(last, STEPS):
                step(t, t % 2)

        def there(t):
            return not isinstance(t, int) or 0 <= t < TILES

        @block.sync
        def _(sp):
            sp.sem_inc(h_free, 2)

            def load_mix(t, u):
                wait(sp, mT_ps, t - 1)
                sp.dma_start(m[:, u, 0:HW], row(dr["att"], t)).then_inc(m_in[u], 16)
                sp.dma_start(m[:, u, HW:D], row(dr["rec"], t)).then_inc(m_in[u], 16)

            def load_x(t, u):
                wait(sp, y_ok, 2 * t - 2)
                src = dr["x_sample"].rearrange("b t d -> (b t) d") if isinstance(t, int) and t == NT else row(xp, t)
                sp.dma_start(x[:, u, :], src).then_inc(x_in[u], 16)

            def step(t, u):
                if isinstance(t, int) and t == 0:
                    load_mix(0, 0)
                    load_mix(1, 1)
                    load_x(0, 0)
                if there(t + 2):
                    load_mix(t + 2, u)
                if there(t + 1):
                    load_x(t + 1, 1 - u)
                if there(t - 1):
                    sp.wait_ge(h_ok, t)
                    sp.dma_start(row(h2, t - 1), h[:, 1 - u, :]).then_inc(h_out, 16)
                    sp.wait_ge(h_out, 16 * t)
                    sp.sem_inc(h_free, 1)

            steps(sp, step, last=NT - 2)
            sp.wait_ge(zero_ok, 1)
            sp.dma_start(dr["h2"][TILES * P:TILES * P + PAD_ROWS], zero[:, :]).then_inc(h_out, 16)
            sp.wait_ge(h_out, 16 * (TILES + 1))

        @block.gpsimd
        def _(pool):
            chain = Chain(pool, pool_step)
            kw = dict(allow_small_or_imprecise_dtypes=True)
            chain.after(pool.iota(init[:, :, :], [[0, 5], [1, P]], base=2 * TILES * P, channel_multiplier=0))
            pool.dma_start(dr["table"].rearrange("(a b) r o -> a (b r o)", b=5), init[:, :, :].rearrange("a b r -> a (b r)")).then_inc(tab_out, 16)
            pool.iota(slot[:, :, :], [[2 * P, TILES], [1, 2]], base=0, channel_multiplier=2)
            pool.iota(e_of[:, :], [[1, N_EXP]], base=0, channel_multiplier=0, **kw)
            pool.iota(g_of[:, :], [[1, N_GRP], [0, N_EXP // N_GRP]], base=0, channel_multiplier=0, **kw)
            pool.iota(q_of[:, :], [[QUEUE, N_EXP]], base=0, channel_multiplier=0, **kw)
            pool.iota(en_of[:, :], [[1, N_EXP * TILES]], base=0, channel_multiplier=0, **kw)
            pool.iota(ee_of[:, :, :], [[1, N_EXP], [0, TILES]], base=0, channel_multiplier=0, **kw)
            pool.iota(th_of[:, :], [[P, TILES]], base=0, channel_multiplier=0, **kw)
            pool.iota(me[:, :], [[0, 1]], base=1, channel_multiplier=1, **kw)
            pool.iota(keep["run_slot"][:, :], [[0, P // 2], [-1, 2]], base=1, channel_multiplier=0)
            pool.memset(one_row[:, :], 1.0)
            pool.memset(cnt[:, :], 0.0)
            pool.memset(glog[:, :], 4 * HIDDEN)
            pool.memset(zero[:, :], 0.0).then_inc(zero_ok, 1)
            pool.memset(ones[:, :], 1.0)
            chain.after(pool.memset(tri[:, :], 1.0))
            pool.affine_select(out=tri[:, :], in_=tri[:, :], compare_op=ALU.is_gt, fill=0.0, base=0,
                               pattern=[[1, P]], channel_multiplier=-1).then_inc(iota_ok, 1)
            pool.sem_inc(sc_free, 2)
            pool.wait_ge(tab_out, 16)

            def step(t, u):
                if there(t - 2):
                    pool.wait_ge(pos_ok, t)
                    pool.sem_inc(pool_stand, 1)
                    for c in range(2):
                        pool.indirect_dma_start(
                            out=dr["table"].rearrange("a r o -> (a r) o"),
                            out_offset=bass.IndirectOffsetOnAxis(ap=posi[:, u, c:c + 1], axis=0),
                            in_=slot_now[:, u, c:c + 1], in_offset=None).then_inc(sc_out, 16)
                    pool.wait_ge(sc_out, 32 * (t - 1))
                    pool.sem_inc(sc_free, 1)

            steps(pool, step)
            pool.wait_ge(lst_ok, 1)
            pool.indirect_dma_start(out=blk_rows[:, :], out_offset=None, in_=dr["table"].rearrange("a r o -> a (r o)"),
                                    in_offset=bass.IndirectOffsetOnAxis(ap=blk_at[:, :], axis=0)).then_inc(blk_in, 16)

        @block.scalar
        def _(act):
            chain = Chain(act, act_step)
            eps = consts["eps"][:, 0:1]

            def att_stats(t, u):
                act.wait_ge(m_in[u], 32 * (t // 2) + 32 if isinstance(t, int) else (t - u) * 16 + 32)
                wait(act, mix_ok, t - 1)
                for hd in range(HEADS):
                    chain.after(nc.scalar.activation(junk[:, 0:P], m[:, u, hd * P:(hd + 1) * P], ACT.Square,
                                                     accum_out=ast[:, u, hd:hd + 1]))
                chain.after(nc.scalar.activation(ast[:, u, 4:8], ast[:, u, 0:4], ACT.Ln, scale=1.0 / P, bias=eps))
                nc.scalar.activation(ast[:, u, 8:12], ast[:, u, 4:8], ACT.Exp, scale=-0.5).then_inc(ar_ok, 1)

            def copy_mT(t, u):
                act.wait_ge(mT_ps, t + 1)
                nc.scalar.copy(mT[:, u, 0:4, :].rearrange("p c t -> p (c t)"), mps[:, 0, :]).then_inc(mT_act, 1)

            def step(t, u):
                if there(t - 1):
                    act.wait_ge(y_ok, 2 * t)
                    wait(act, h_ok, t - 1)
                    chain.after(nc.scalar.activation(junk[:, :], y[:, bass.ds(t - 1, 1), :].rearrange("p o d -> p (o d)"),
                                                     ACT.Square, accum_out=st[:, 0:1]))
                    chain.after(nc.scalar.activation(st[:, 1:2], st[:, 0:1], ACT.Ln, scale=1.0 / D, bias=eps))
                    nc.scalar.activation(st[:, 2:3], st[:, 1:2], ACT.Exp, scale=-0.5).then_inc(r_ok, 1)
                if there(t - 2):
                    act.wait_ge(gm_ok, t - 1)
                    nc.scalar.activation(rt[:, 4:8], glog[:, 0:4], ACT.Exp, bias=rt[:, 0:1], accum_out=rt[:, 1:2]).then_inc(ge_ok, 1)
                    act.wait_ge(ev_ok, t - 1)
                    nc.scalar.activation(rt[:, 3:4], rt[:, 2:3], ACT.Exp).then_inc(ee_ok, 1)
                if there(t - 1):
                    act.wait_ge(hT_ps, t)
                    nc.scalar.copy(hT[:, 0:4, :].rearrange("p c t -> p (c t)"), hps[:, 0, :]).then_inc(hT_act, 1)
                if there(t + 1):
                    copy_mT(t + 1, 1 - u)
                if there(t + 2):
                    att_stats(t + 2, u)

            act.wait_ge(consts["sem"], consts["n"])
            att_stats(0, 0)
            copy_mT(0, 0)
            att_stats(1, 1)
            steps(act, step, chain, 7, last=NT - 2)

        @block.vector
        def _(dve):
            chain = Chain(dve, dve_step)
            tt, ts, stt = nc.vector.tensor_tensor, nc.vector.tensor_scalar, nc.vector.scalar_tensor_tensor
            red, cp = nc.vector.tensor_reduce, nc.vector.tensor_copy

            def mix(t, u):
                dve.wait_ge(ar_ok, t + 1)
                for hd in range(HEADS):
                    c = slice(hd * P, (hd + 1) * P)
                    ins = stt(out=m[:, u, c], in0=m[:, u, c], scalar=ast[:, u, 8 + hd:9 + hd], in1=sub[:, :], op0=ALU.mult, op1=ALU.mult)
                ins.then_inc(mix_ok, 1)

            def norm(t, u):
                dve.wait_ge(r_ok, t + 1)
                dve.wait_ge(h_free, t + 1)
                wait(dve, hT_ps, t)
                stt(out=h[:, u, :], in0=y[:, bass.ds(t, 1), :].rearrange("p o d -> p (o d)"), scalar=st[:, 2:3], in1=n2[:, :],
                    op0=ALU.mult, op1=ALU.mult).then_inc(h_ok, 1)

            def residual(t, u, half):
                c = slice(half * HW, (half + 1) * HW)
                dve.wait_ge(x_in[u], 16 * (t // 2) + 16 if isinstance(t, int) else (t - u) * 8 + 16)
                dve.wait_ge(y_ps, 2 * t + half + 1)
                tt(y[:, bass.ds(t, 1), c].rearrange("p o n -> p (o n)"), yps[:, half, :], x[:, u, c], ALU.add).then_inc(y_ok, 1)

            def copy_mT(t, u):
                dve.wait_ge(mT_ps, t + 1)
                cp(mT[:, u, 4:8, :].rearrange("p c t -> p (c t)"), mps[:, 1, :]).then_inc(mT_dve, 1)

            def route(t, u):
                dve.wait_ge(lg_ps, t + 1)
                cp(glog[:, 0:N_GRP], lps[:, 0:N_GRP])
                chain.after(cp(elog[:, :], lps[:, N_GRP:LOGITS]))
                dve.sem_inc(stand, 1)
                chain.after(nc.vector.max(gtop[:, :], glog[:, :]))
                ts(rt[:, 0:1], gtop[:, 0:1], -1.0, None, ALU.mult).then_inc(gm_ok, 1)
                chain.after(nc.vector.max_index(gidx[:, :], gtop[:, :], glog[:, :]))
                chain.after(cp(sel[:, 0:1], gidx[:, 0:1]))
                chain.after(ts(place[:, :], g_of[:, :], sel[:, 0:1], None, ALU.is_equal))
                tt(elog[:, :], elog[:, :], place[:, :], ALU.mult)
                chain.after(ts(elm[:, :], place[:, :], -1.0, -HIDDEN, ALU.add, ALU.mult))
                chain.after(tt(elm[:, :], elog[:, :], elm[:, :], ALU.add))
                dve.sem_inc(stand, 1)
                chain.after(nc.vector.max(etop[:, :], elm[:, :]))
                tt(rt[:, 2:3], etop[:, 1:2], etop[:, 0:1], ALU.subtract).then_inc(ev_ok, 1)
                chain.after(nc.vector.max_index(eidx[:, :], etop[:, :], elm[:, :]))
                chain.after(cp(sel[:, 2:4], eidx[:, 0:2]))
                for c in range(2):
                    ins = ts(oh[:, u, c, :], e_of[:, :], sel[:, 2 + c:3 + c], None, ALU.is_equal)
                chain.after(ins)
                tt(both[:, u, :], oh[:, u, 0, :], oh[:, u, 1, :], ALU.add).then_inc(both_ok, 1)

            def gate(t):
                dve.wait_ge(ge_ok, t + 1)
                dve.wait_ge(ee_ok, t + 1)
                chain.after(ts(sel[:, 0:1], rt[:, 3:4], 1.0, rt[:, 1:2], ALU.add, ALU.mult))
                g = gates[:, bass.ds(t, 1), :].rearrange("p o c -> p (o c)")
                chain.after(nc.vector.reciprocal(g[:, 0:1], sel[:, 0:1]))
                chain.after(tt(g[:, 1:2], g[:, 0:1], rt[:, 3:4], ALU.mult))

            def positions(t, u):
                dve.wait_ge(rk_ps, t + 1)
                dve.wait_ge(sc_free, t + 1)
                chain.after(tt(place[:, :], rps[:, 0, :], cnt[:, :], ALU.add))
                chain.after(tt(place[:, :], place[:, :], q_of[:, :], ALU.add))
                chain.after(tt(cnt[:, :], rps[:, 1, :], cnt[:, :], ALU.add))
                for c in range(2):
                    ins = tt(hit[:, c, :], oh[:, u, c, :], place[:, :], ALU.mult)
                chain.after(ins)
                chain.after(red(pos[:, :], hit[:, :, :], AX.X, ALU.add))
                cp(posi[:, u, :], pos[:, :])
                cp(slot_now[:, u, :], slot[:, bass.ds(t, 1), :].rearrange("p o c -> p (o c)")).then_inc(pos_ok, 1)

            def step(t, u):
                if there(t - 1):
                    residual(t - 1, 1 - u, 1)
                if there(t + 1):
                    mix(t + 1, 1 - u)
                if there(t - 2):
                    route(t - 2, u)
                if there(t - 1):
                    norm(t - 1, 1 - u)
                if there(t - 2):
                    gate(t - 2)
                if there(t - 1):
                    dve.wait_ge(hT_ps, t)
                    cp(hT[:, 4:8, :].rearrange("p c t -> p (c t)"), hps[:, 1, :]).then_inc(hT_dve, 1)
                if there(t + 1):
                    copy_mT(t + 1, 1 - u)
                if there(t):
                    residual(t, u, 0)
                if there(t - 2):
                    positions(t - 2, u)

            dve.wait_ge(iota_ok, 1)
            dve.sem_inc(pos_ok, 1)
            chain.after(ts(sub[:, :], sub[:, :], 1.0 - LAM_INIT, None, ALU.mult))
            mix(0, 0)
            copy_mT(0, 0)
            steps(dve, step, chain, 19)
            chain.after(tt(full[:, :, :], cnt[:, :, None].to_broadcast([P, N_EXP, TILES]),
                           th_of[:, None, :].to_broadcast([P, N_EXP, TILES]), ALU.is_gt))
            fl = full[:, :, :].rearrange("p e j -> p (e j)")
            chain.after(nc.vector.tensor_tensor_scan(rank[:, :], one_row[:, :], fl, 0.0, ALU.mult, ALU.add))
            chain.after(cp(lst[:, 2:3], rank[:, N_EXP * TILES - 1:N_EXP * TILES]))
            chain.after(tt(rank[:, :], rank[:, :], fl, ALU.mult))
            there0 = full[:, :, 0]
            chain.after(nc.vector.tensor_tensor_scan(run_rank[:, :], ones[:, 0:N_EXP], there0, 0.0, ALU.mult, ALU.add))
            ts(last_run[:, :], run_rank[0:1, N_EXP - 1:N_EXP], -1.0, None, ALU.add)
            chain.after(tt(run_hit[:, :], run_rank[:, :], there0, ALU.mult))
            chain.after(ts(run_hit[:, :], run_hit[:, :], me[:, 0:1], None, ALU.is_equal))
            chain.after(tt(run_row[:, :], run_hit[:, :], e_of[:, :], ALU.mult))
            chain.after(red(lists[:, 0:1], run_row[:, :], AX.X, ALU.add))
            chain.after(tt(run_row[:, :], run_hit[:, :], rank[:, :].rearrange("p (e j) -> p e j", j=TILES)[:, :, 0], ALU.mult))
            chain.after(red(lists[:, 1:2], run_row[:, :], AX.X, ALU.add))
            chain.after(ts(rank[:, :], rank[:, :], me[:, 0:1], None, ALU.is_equal))
            chain.after(tt(one_row[:, :], rank[:, :], en_of[:, :], ALU.mult))
            chain.after(red(lst[:, 0:1], one_row[:, :], AX.X, ALU.add))
            chain.after(tt(one_row[:, :], rank[:, :], ee_of[:, :, :].rearrange("p e j -> p (e j)"), ALU.mult))
            chain.after(red(lst[:, 1:2], one_row[:, :], AX.X, ALU.add))
            chain.after(ts(lst[:, 3:4], me[:, :], lst[:, 2:3], float(N_EXP * TILES), ALU.is_gt, ALU.mult))
            chain.after(tt(lst[:, 0:1], lst[:, 0:1], lst[:, 3:4], ALU.add))
            cp(blk_at[:, :], lst[:, 0:1]).then_inc(lst_ok, 1)
            chain.after(tt(lst[:, 1:2], lst[:, 1:2], lst[:, 3:4], ALU.add))
            ts(trips[:, :], lst[0:1, 2:3], 0.5, -0.25, ALU.mult, ALU.add)
            chain.after(ts(run_hit[:, :], e_of[:, :], lst[:, 1:2], None, ALU.is_le))
            chain.after(tt(run_hit[:, :], run_hit[:, :], there0, ALU.mult))
            chain.after(red(lists[:, 2:3], run_hit[:, :], AX.X, ALU.add))
            chain.after(ts(half[:, :], lists[:, 2:3], 0.5, -0.25, ALU.mult, ALU.add))
            chain.after(cp(lst[:, 3:4], half[:, :]))
            stt(out=lists[:, 3:4], in0=lst[:, 3:4], scalar=-2.0, in1=lists[:, 2:3], op0=ALU.mult, op1=ALU.add).then_inc(lst_ok, 1)
            dve.wait_ge(lst_ps, 1)
            cp(keep["run_expert"][:, :], lps[0:1, 0:P])
            cp(keep["run_before"][:, 1:P], lps[0:1, P:2 * P - 1])
            cp(keep["block_run"][:, :], lps[0:1, 2 * P:3 * P])
            cp(keep["block_slot"][:, :], lps[0:1, 3 * P:4 * P])
            dve.wait_ge(blk_in, 16)
            cp(blk[:, :], blk_rows[:, :]).then_inc(blk_ok, 1)
            dve.wait_ge(blk_ps, 1)
            chain.after(cp(slot_all[:, :], yps[:, 0, 0:P]))
            ts(tok_all[:, :], slot_all[:, :], 0.5, -0.25, ALU.mult, ALU.add)

        @block.tensor
        def _(pe):
            def turn_mix(t, u):
                pe.wait_ge(mix_ok, t + 1)
                wait(pe, mT_act, t)
                wait(pe, mT_dve, t)
                for c in range(DC):
                    mm = pe.transpose(mps[:, c // 4, (c % 4) * P:(c % 4 + 1) * P], m[:, u, c * P:(c + 1) * P], ident[:, :])
                mm.then_inc(mT_ps, 1)

            def project_out(t, u, half):
                pe.wait_ge(mT_act, t + 1)
                pe.wait_ge(mT_dve, t + 1)
                wait(pe, y_ok, 2 * t - 1 + half)
                for c in range(DC):
                    mm = pe.matmul(yps[:, half, :], mT[:, u, c, :], wo[:, c, half * HW:(half + 1) * HW],
                                   start=(c == 0), stop=(c == DC - 1))
                mm.then_inc(y_ps, 1)

            def turn_h(t, u):
                pe.wait_ge(h_ok, t + 1)
                wait(pe, hT_act, t)
                wait(pe, hT_dve, t)
                for c in range(DC):
                    mm = pe.transpose(hps[:, c // 4, (c % 4) * P:(c % 4 + 1) * P], h[:, u, c * P:(c + 1) * P], ident[:, :])
                mm.then_inc(hT_ps, 1)

            def logits(t, u):
                pe.wait_ge(hT_act, t + 1)
                pe.wait_ge(hT_dve, t + 1)
                wait(pe, both_ok, t)
                for c in range(DC):
                    mm = pe.matmul(lps[:, 0:LOGITS], hT[:, c, :], wr[:, c, :], start=(c == 0), stop=(c == DC - 1))
                mm.then_inc(lg_ps, 1)

            def ranks(t, u):
                pe.wait_ge(both_ok, t + 1)
                pe.wait_ge(pos_ok, t + 1)
                pe.matmul(rps[:, 0, :], tri[:, :], both[:, u, :], start=True, stop=True)
                pe.matmul(rps[:, 1, :], ones[:, :], both[:, u, :], start=True, stop=True).then_inc(rk_ps, 1)

            def step(t, u):
                if there(t):
                    project_out(t, u, 0)
                if there(t - 1):
                    turn_h(t - 1, 1 - u)
                if there(t + 1):
                    turn_mix(t + 1, 1 - u)
                if there(t - 2):
                    ranks(t - 2, u)
                if there(t):
                    project_out(t, u, 1)
                if there(t - 1):
                    logits(t - 1, 1 - u)

            pe.wait_ge(iota_ok, 1)
            turn_mix(0, 0)
            steps(pe, step)
            pe.wait_ge(lst_ok, 2)
            for c in range(4):
                mm = pe.matmul(lps[0:1, c * P:(c + 1) * P], lists[:, c:c + 1], ident[:, :], start=True, stop=True)
            mm.then_inc(lst_ps, 1)
            pe.wait_ge(blk_ok, 1)
            pe.transpose(yps[:, 0, 0:P], blk[:, :], ident[:, :]).then_inc(blk_ps, 1)


def experts(nc, dr, consts, keep):
    ident = consts["ident"]
    trips, slot_all, tok_all = keep["trips"], keep["slot_all"], keep["tok_all"]
    FC = D_EXP // P
    with ExitStack() as ctx:
        sb = lambda n, s, d=F32: ctx.enter_context(nc.sbuf_tensor(n, s, d))
        ps = lambda n, s, d=F32: ctx.enter_context(nc.psum_tensor(n, s, d))
        sem = stage_semaphores(nc, ctx)
        wg, wu = sb("w_gate_sb", [P, 2, DC, D_EXP]), sb("w_up_sb", [P, 2, DC, D_EXP])
        wd = sb("w_down_sb", [P, 2, FC, D])
        slots = sb("block_slots", [P, 2], U32)
        toks = sb("block_tokens", [P, 2], U32)
        xg = sb("block_rows", [P, 2, D])
        xT = sb("block_rows_T", [P, 2, DC, P])
        sg = sb("silu_gate", [P, D_EXP])
        a = sb("hidden", [P, D_EXP])
        aT = sb("hidden_T", [P, 2, FC, P])
        out = sb("block_out", [P, 2, D])
        xps = ps("block_rows_T_psum", [P, 2, HW])
        gps, ups = ps("gate_psum", [P, D_EXP]), ps("up_psum", [P, D_EXP])
        aps = ps("hidden_T_psum", [P, HW])
        dps = ps("down_psum", [P, 2, HW])
        g_in, u_in, d_in = (sem(f"w_{n}_loaded") for n in ("gate", "up", "down"))
        g_run, u_run, d_run = (sem(f"w_{n}_of_run") for n in ("gate", "up", "down"))
        slot_ok, x_in, o_out = sem("slots_ready"), [sem(f"rows_gathered{u}") for u in range(2)], sem("rows_scattered")
        tok_ok, x_ps, x_act, x_dve = sem("tokens_ready"), sem("rows_T_in_psum"), sem("rows_T_half0"), sem("rows_T_half1")
        g_ps, u_ps, eg_ok, a_ok = sem("gate_in_psum"), sem("up_in_psum"), sem("gate_exp_ready"), sem("hidden_ready")
        a_ps, aT_ok, d_ps, d_act, d_dve = (sem("hidden_T_in_psum"), sem("hidden_T_ready"), sem("down_in_psum"),
                                           sem("out_half0"), sem("out_half1"))
        step_ = sem("p5_dve_step")
        stand, sp_stand = sem("p5_pool_stand"), sem("p5_sync_stand")
        block = ctx.enter_context(nc.Block())
        MAXT = (N_BLOCKS - 1) // 2

        def load(eng, src, lo, hi):
            return eng.value_load(src, min_val=lo, max_val=hi)

        @block.sync
        def _(sp):
            n = load(sp, trips[0:1, 0:1], 1, MAXT)
            wgv = dr["w_e_gate"].rearrange("l e (c p) f -> (l e) p c f", p=P)
            wuv = dr["w_e_up"].rearrange("l e (c p) f -> (l e) p c f", p=P)
            wdv = dr["w_e_down"].rearrange("l e (c p) d -> (l e) p c d", p=P)

            def fetch(r, done, parts):
                entry = lambda name, lo, hi: load(sp, keep[name][0:1, bass.ds(r, 1)], lo, hi)
                e, slot = entry("run_expert", 0, N_EXP - 1), entry("run_slot", 0, 1)
                if not isinstance(r, int) or r > 0:
                    sp.wait_ge(done, entry("run_before", 1, N_BLOCKS))
                    sp.sem_inc(sp_stand, 1)
                for v, w, arrived in parts:
                    sp.dma_start(w[:, bass.ds(slot, 1), :, :].rearrange("p o c n -> p (o c) n"),
                                 v[bass.ds(e, 1)].rearrange("o p c n -> (o p) c n")).then_inc(arrived, 16)

            def gate_up(r):
                fetch(r, u_ps, ((wgv, wg, g_in), (wuv, wu, u_in)))

            def down(r):
                fetch(r, d_ps, ((wdv, wd, d_in),))

            def arrived(r, *pairs):
                for loaded, of_run in pairs:
                    sp.wait_ge(loaded, r * 16 + 16)
                    sp.sem_inc(of_run, 1)

            last = load(sp, keep["last_run"][0:1, 0:1], 1, N_EXP - 1)
            gate_up(0)
            down(0)
            arrived(0, (g_in, g_run), (u_in, u_run))
            gate_up(1)
            arrived(0, (d_in, d_run))
            arrived(1, (g_in, g_run), (u_in, u_run))
            with sp.Fori(2, last + 1) as r:
                gate_up(r)
                down(r - 1)
                arrived(r - 1, (d_in, d_run))
                arrived(r, (g_in, g_run), (u_in, u_run))
            down(last)
            arrived(last, (d_in, d_run))

        @block.gpsimd
        def _(pool):
            n = load(pool, trips[0:1, 0:1], 1, MAXT)
            col = lambda ap, b: ap[:, bass.ds(b, 1)]

            def gather(b, u):
                wait(pool, x_ps, b - 1)
                pool.tensor_copy(toks[:, u:u + 1], col(tok_all, b)).then_inc(tok_ok, 1)
                pool.wait_ge(tok_ok, b + 1)
                pool.sem_inc(stand, 1)
                pool.indirect_dma_start(out=xg[:, u, :], out_offset=None, in_=dr["h2"],
                                        in_offset=bass.IndirectOffsetOnAxis(ap=toks[:, u:u + 1], axis=0)).then_inc(x_in[u], 16)

            def scatter(b, u):
                wait(pool, o_out, 16 * b)
                pool.tensor_copy(slots[:, u:u + 1], col(slot_all, b)).then_inc(slot_ok, 1)
                pool.wait_ge(slot_ok, b + 1)
                pool.wait_ge(d_act, b + 1)
                pool.wait_ge(d_dve, b + 1)
                pool.sem_inc(stand, 1)
                pool.indirect_dma_start(out=dr["moe"], out_offset=bass.IndirectOffsetOnAxis(ap=slots[:, u:u + 1], axis=0),
                                        in_=out[:, u, :], in_offset=None).then_inc(o_out, 16)

            gather(0, 0)
            gather(1, 1)
            gather(2, 0)
            scatter(0, 0)
            gather(3, 1)
            scatter(1, 1)
            with pool.Fori(1, n) as i:
                gather(i * 2 + 2, 0)
                scatter(i * 2, 0)
                gather(i * 2 + 3, 1)
                scatter(i * 2 + 1, 1)
            scatter(n * 2, 0)
            pool.wait_ge(x_in[1], n * 16 + 16)
            pool.wait_ge(o_out, n * 32 + 16)

        @block.scalar
        def _(act):
            n = load(act, trips[0:1, 0:1], 1, MAXT)

            def copy_x(b, u):
                act.wait_ge(x_ps, b + 1)
                nc.scalar.copy(xT[:, u, 0:4, :].rearrange("p c t -> p (c t)"), xps[:, 0, :]).then_inc(x_act, 1)

            def gate(b):
                act.wait_ge(g_ps, b + 1)
                wait(act, a_ok, b)
                nc.scalar.activation(sg[:, :], gps[:, :], ACT.Exp, scale=-1.0).then_inc(eg_ok, 1)

            def copy_a(b, u):
                act.wait_ge(a_ps, b + 1)
                nc.scalar.copy(aT[:, u, :, :].rearrange("p c t -> p (c t)"), aps[:, :]).then_inc(aT_ok, 1)

            def copy_out(b, u):
                act.wait_ge(d_ps, b + 2)
                wait(act, o_out, 16 * b)
                nc.scalar.copy(out[:, u, 0:HW], dps[:, 0, :]).then_inc(d_act, 1)

            def blk(b, u):
                gate(b)
                copy_x(b + 1, 1 - u)
                copy_out(b - 1, 1 - u)
                copy_a(b, u)

            copy_x(0, 0)
            gate(0)
            copy_x(1, 1)
            copy_a(0, 0)
            blk(1, 1)
            blk(2, 0)
            with act.Fori(1, n) as i:
                blk(i * 2 + 1, 1)
                blk(i * 2 + 2, 0)
            copy_out(n * 2, 0)

        @block.vector
        def _(dve):
            chain = Chain(dve, step_)
            tt, ts, cp = nc.vector.tensor_tensor, nc.vector.tensor_scalar, nc.vector.tensor_copy
            n = load(dve, trips[0:1, 0:1], 1, MAXT)

            def copy_x(b, u):
                dve.wait_ge(x_ps, b + 1)
                cp(xT[:, u, 4:8, :].rearrange("p c t -> p (c t)"), xps[:, 1, :]).then_inc(x_dve, 1)

            def hidden(b):
                dve.wait_ge(eg_ok, b + 1)
                chain.after(ts(sg[:, :], sg[:, :], 1.0, None, ALU.add))
                chain.after(nc.vector.reciprocal(sg[:, :], sg[:, :]))
                chain.after(tt(sg[:, :], gps[:, :], sg[:, :], ALU.mult))
                dve.wait_ge(u_ps, b + 2)
                wait(dve, a_ps, b)
                tt(a[:, :], ups[:, :], sg[:, :], ALU.mult).then_inc(a_ok, 1)

            def copy_out(b, u):
                dve.wait_ge(d_ps, b + 2)
                wait(dve, o_out, 16 * b)
                cp(out[:, u, HW:D], dps[:, 1, :]).then_inc(d_dve, 1)

            def blk(b, u):
                hidden(b)
                copy_x(b + 1, 1 - u)
                copy_out(b - 1, 1 - u)

            copy_x(0, 0)
            hidden(0)
            copy_x(1, 1)
            blk(1, 1)
            blk(2, 0)
            with dve.Fori(1, n) as i:
                chain.loop(i - 1, 6)
                blk(i * 2 + 1, 1)
                blk(i * 2 + 2, 0)
            copy_out(n * 2, 0)

        @block.tensor
        def _(pe):
            n = load(pe, trips[0:1, 0:1], 1, MAXT)

            def turn_x(b, u):
                half = b // 2 if isinstance(b, int) else None
                pe.wait_ge(x_in[u], 16 * half + 16 if half is not None else (b - u) * 8 + 16)
                wait(pe, x_act, b)
                wait(pe, x_dve, b)
                for c in range(DC):
                    mm = pe.transpose(xps[:, c // 4, (c % 4) * P:(c % 4 + 1) * P], xg[:, u, c * P:(c + 1) * P], ident[:, :])
                mm.then_inc(x_ps, 1)

            def run_of(b):
                return (load(pe, keep["block_run"][0:1, bass.ds(b, 1)], 1, N_EXP),
                        load(pe, keep["block_slot"][0:1, bass.ds(b, 1)], 0, 1))

            def part(w, slot, c, cols=slice(None)):
                return w[:, bass.ds(slot, 1), c, cols].rearrange("p o n -> p (o n)")

            def gate_up(b, u):
                run, slot = run_of(b)
                pe.wait_ge(x_act, b + 1)
                pe.wait_ge(x_dve, b + 1)
                wait(pe, a_ok, b)
                pe.wait_ge(g_run, run)
                for c in range(DC):
                    mm = pe.matmul(gps[:, :], xT[:, u, c, :], part(wg, slot, c), start=(c == 0), stop=(c == DC - 1))
                mm.then_inc(g_ps, 1)
                pe.wait_ge(u_run, run)
                for c in range(DC):
                    mm = pe.matmul(ups[:, :], xT[:, u, c, :], part(wu, slot, c), start=(c == 0), stop=(c == DC - 1))
                mm.then_inc(u_ps, 1)

            def turn_a(b, u):
                pe.wait_ge(a_ok, b + 1)
                wait(pe, aT_ok, b)
                for c in range(FC):
                    mm = pe.transpose(aps[:, c * P:(c + 1) * P], a[:, c * P:(c + 1) * P], ident[:, :])
                mm.then_inc(a_ps, 1)

            def down(b, u, middle=None):
                run, slot = run_of(b)
                pe.wait_ge(aT_ok, b + 1)
                pe.wait_ge(d_run, run)
                wait(pe, d_act, b)
                wait(pe, d_dve, b)
                for half in range(2):
                    if half and middle:
                        middle()
                    for c in range(FC):
                        mm = pe.matmul(dps[:, half, :], aT[:, u, c, :], part(wd, slot, c, slice(half * HW, (half + 1) * HW)),
                                       start=(c == 0), stop=(c == FC - 1))
                mm.then_inc(d_ps, 1)

            def blk(b, u):
                gate_up(b, u)
                down(b - 1, 1 - u, lambda: turn_x(b + 1, 1 - u))
                turn_a(b, u)

            pe.sem_inc(u_ps, 1)
            pe.sem_inc(d_ps, 1)
            turn_x(0, 0)
            gate_up(0, 0)
            turn_x(1, 1)
            turn_a(0, 0)
            blk(1, 1)
            blk(2, 0)
            with pe.Fori(1, n) as i:
                blk(i * 2 + 1, 1)
                blk(i * 2 + 2, 0)
            down(n * 2, 0)


def finish(nc, dr, consts, keep):
    y, gates = keep["y"], keep["gates"]
    with ExitStack() as ctx:
        sb = lambda n, s, d=F32: ctx.enter_context(nc.sbuf_tensor(n, s, d))
        sem = stage_semaphores(nc, ctx)
        e = sb("expert_rows", [P, 4, 2, D])
        fw = sb("final_row", [P, D])
        o = sb("y_out", [P, 2, D])
        junk = sb("square_out6", [P, D], BF16)
        st = sb("final_stats", [P, TILES, 4])
        fw_in, e_in = sem("final_row_loaded"), [sem(f"expert_rows_loaded{s}") for s in range(4)]
        y_ok, r_ok, o_ok, o_out = sem("moe_added"), sem("final_rstd"), sem("out_ready"), [sem(f"out_stored{u}") for u in range(2)]
        act_step, dve_step = sem("p6_act_step"), sem("p6_dve_step")
        block = ctx.enter_context(nc.Block())
        moe = dr["moe"][0:2 * TILES * P].rearrange("(t p c) d -> t p (c d)", p=P, c=2)
        yp = dr["y_prompt"].rearrange("b (t p) d -> (b t) p d", p=P)

        @block.sync
        def _(sp):
            def load(t):
                wait(sp, y_ok, t - 3)
                sp.dma_start(e[:, t % 4, :, :].rearrange("p c d -> p (c d)"), moe[t]).then_inc(e_in[t % 4], 16)

            sp.dma_start(fw[:, :], dr["final_w"].to_broadcast([P, D])).then_inc(fw_in, 16)
            for t in range(3):
                load(t)
            for t in range(TILES):
                if t + 3 < TILES:
                    load(t + 3)
                sp.wait_ge(o_ok, t + 1)
                dst = yp[t] if t < NT else dr["y_sample"].rearrange("b t d -> (b t) d")
                sp.dma_start(dst, o[:, t % 2, :]).then_inc(o_out[t % 2], 16)
            sp.wait_ge(o_out[0], 16 * (NT // 2 + 1))
            sp.wait_ge(o_out[1], 16 * (NT // 2))

        @block.scalar
        def _(act):
            chain = Chain(act, act_step)
            for t in range(TILES):
                act.wait_ge(y_ok, t + 1)
                chain.after(nc.scalar.activation(junk[:, :], y[:, t, :], ACT.Square, accum_out=st[:, t, 0:1]))
                chain.after(nc.scalar.activation(st[:, t, 1:2], st[:, t, 0:1], ACT.Ln, scale=1.0 / D, bias=consts["eps"][:, 0:1]))
                nc.scalar.activation(st[:, t, 2:3], st[:, t, 1:2], ACT.Exp, scale=-0.5).then_inc(r_ok, 1)

        @block.vector
        def _(dve):
            chain = Chain(dve, dve_step)
            stt = nc.vector.scalar_tensor_tensor
            dve.wait_ge(fw_in, 16)

            def add(t):
                dve.wait_ge(e_in[t % 4], 16 * (t // 4) + 16)
                chain.after(stt(out=y[:, t, :], in0=e[:, t % 4, 0, :], scalar=gates[:, t, 0:1], in1=y[:, t, :], op0=ALU.mult, op1=ALU.add))
                stt(out=y[:, t, :], in0=e[:, t % 4, 1, :], scalar=gates[:, t, 1:2], in1=y[:, t, :], op0=ALU.mult, op1=ALU.add).then_inc(y_ok, 1)

            add(0)
            for t in range(TILES):
                if t + 1 < TILES:
                    add(t + 1)
                dve.wait_ge(r_ok, t + 1)
                wait(dve, o_out[t % 2], 16 * (t // 2))
                stt(out=o[:, t % 2, :], in0=y[:, t, :], scalar=st[:, t, 2:3], in1=fw[:, :], op0=ALU.mult, op1=ALU.mult).then_inc(o_ok, 1)


def make_consts(nc, ctx):
    sb = lambda n, s, d=F32: ctx.enter_context(nc.sbuf_tensor(n, s, d))
    sem = lambda n: ctx.enter_context(nc.semaphore(n))
    c = {"ident": sb("ident", [P, P]), "eps": sb("eps_col", [P, 1])}
    c["sem"] = sem("consts_ready")
    c["zeroed"] = sem("consts_zeroed")
    with nc.Block() as block:
        @block.gpsimd
        def _(g):
            g.memset(c["ident"][:, :], 0.0).then_inc(c["zeroed"], 1)
            g.memset(c["eps"][:, :], EPS).then_inc(c["sem"], 1)
            g.wait_ge(c["zeroed"], 1)
            g.affine_select(out=c["ident"][:, :], in_=c["ident"][:, :], compare_op=ALU.not_equal, fill=1.0,
                            base=0, pattern=[[-1, P]], channel_multiplier=1).then_inc(c["sem"], 1)
    c["n"] = 2
    return c


def build(nc, dr):
    dr["z"] = {j: nc.dram_tensor(f"scratch_z{j}", [TILES, P, HW], F32, kind="Internal").ap() for j in (QA, KT)}
    dr["rec"] = nc.dram_tensor("scratch_rec", [TILES, P, HW], F32, kind="Internal").ap()
    dr["att"] = nc.dram_tensor("scratch_att", [TILES, P, HW], F32, kind="Internal").ap()
    dr["table"] = nc.dram_tensor("scratch_table", [N_EXP * TILES + 1, P, 1], U32, kind="Internal").ap()
    dr["h2"] = nc.dram_tensor("scratch_h2", [TILES * P + PAD_ROWS, D], F32, kind="Internal").ap()
    dr["moe"] = nc.dram_tensor("scratch_moe", [2 * (TILES * P + PAD_ROWS), D], F32, kind="Internal").ap()
    with ExitStack() as ctx:
        consts = make_consts(nc, ctx)
        project(nc, dr, consts)
        attend(nc, dr, consts)
        sb = lambda n, s, d=F32: ctx.enter_context(nc.sbuf_tensor(n, s, d))
        keep = {"y": sb("y_rows", [P, TILES, D]), "gates": sb("gates", [P, TILES, 2]), "last_run": sb("last_run", [1, 1], I32),
                "slot_all": sb("block_slots_all", [P, P], U32), "tok_all": sb("block_tokens_all", [P, P], U32),
                "trips": sb("loop_trips", [1, 1], I32)}
        for name in ("run_slot", "run_expert", "run_before", "block_run", "block_slot"):
            keep[name] = sb(name, [1, P], I32)
        with ExitStack() as pre_ctx:
            psb = lambda n, s: pre_ctx.enter_context(nc.sbuf_tensor(n, s, F32))
            pre = {"wo": psb("w_out_sb", [P, DC, D]), "wr": psb("w_router_sb", [P, DC, LOGITS]),
                   "n2": psb("norm2_row", [P, D]), "sub": psb("subln_row", [P, P])}
            attend_sample(nc, dr, consts, pre)
            mix_and_route(nc, dr, consts, keep, pre)
        experts(nc, dr, consts, keep)
        finish(nc, dr, consts, keep)


_INS = ['x_prompt', 'x_sample', 'cache_k', 'cache_v', 'state_rec', 'w_in', 'lam_q1', 'lam_k1', 'lam_q2', 'lam_k2',
        'subln_w', 'lb_param', 'gnorm_w', 'w_out', 'norm1_w', 'norm2_w', 'w_group', 'w_router', 'w_e_gate', 'w_e_up',
        'w_e_down', 'final_w']
_OUTS = [('y_prompt', (1, 2048, 1024)), ('y_sample', (8, 16, 1024)), ('k_prompt', (1, 1, 2048, 4, 128)),
         ('v_prompt', (1, 1, 2048, 4, 128)), ('state_prompt', (1, 1, 4, 128, 128)), ('k_sample', (1, 8, 16, 4, 128)),
         ('v_sample', (1, 8, 16, 4, 128)), ('state_sample', (1, 8, 4, 128, 128))]


def kernel(**inputs):
    import numpy as _np
    import concourse.bacc as _bacc
    from concourse import mybir as _mybir
    from concourse.bass_utils import run_bass_kernel_spmd as _run

    nc = _bacc.Bacc("TRN2", target_bir_lowering=False, num_devices=1)
    arrays, dr = {}, {}
    for name in _INS:
        a = _np.ascontiguousarray(inputs[name])
        if a.ndim == 1:
            a = a.reshape(1, -1)
        arrays[f"in_{name}"] = a
        dr[name] = nc.dram_tensor(f"in_{name}", a.shape, _mybir.dt.from_np(a.dtype), kind="ExternalInput").ap()
    for name, shape in _OUTS:
        dr[name] = nc.dram_tensor(f"out_{name}", shape, _mybir.dt.float32, kind="ExternalOutput").ap()
    build(nc, dr)
    r = _run(nc, [arrays], core_ids=[0])
    return tuple(r.results[0][f"out_{name}"] for name, _ in _OUTS)
```
